# Optimizing a Trainium2 kernel written in Bass

```python
import math
import jax
import jax.numpy as jnp
from jax import lax
import numpy as np

D_MODEL = 1024
BATCH = 1
SEQ = 512
DEPTH = 1
DEC_BATCH = 1
DEC_SEQ = 32
PAST_LEN = 256

CHUNK = 64
S5_WIDTH = D_MODEL // 2
S5_GROUP_CH = 16
S5_GROUPS = S5_WIDTH // S5_GROUP_CH
S5_STATE = 64
SB_WIDTH = D_MODEL - S5_WIDTH
SB_HEAD_DIM = 64
SB_HEADS = SB_WIDTH // SB_HEAD_DIM
SB_BLOCK = 128
N_EXPERTS = 32
TOP_K = 4
D_FF = D_MODEL
SWIGLU_LIMIT = 7.0
SWIGLU_ALPHA = 1.702
MOE_BLOCK = 128
LN_EPS = 1e-5
DEEPNORM_ALPHA = (2 * DEPTH) ** 0.25
DEEPNORM_BETA = (8 * DEPTH) ** -0.25

kernel_name = 'hybrid_s5_stickbreak_moe_stream_step'

def layer_norm(x, g, b):
    xf = x.astype(jnp.float32)
    mu = jnp.mean(xf, axis=-1, keepdims=True)
    var = jnp.mean(jnp.square(xf - mu), axis=-1, keepdims=True)
    return ((xf - mu) * lax.rsqrt(var + LN_EPS) * g.astype(jnp.float32) + b.astype(jnp.float32)).astype(x.dtype)

def adaln_params(c, w_ada, b_ada):
    mod = jax.nn.silu(c) @ w_ada + b_ada
    return [m[:, None, :] for m in jnp.split(mod, 6, axis=-1)]

def _ssm_combine(e1, e2):
    a1r, a1i, b1r, b1i = e1
    a2r, a2i, b2r, b2i = e2
    return (a2r * a1r - a2i * a1i,
            a2r * a1i + a2i * a1r,
            a2r * b1r - a2i * b1i + b2r,
            a2r * b1i + a2i * b1r + b2i)

def s5_mixer(u, a_re, a_im, log_dt, b_re, b_im, c_re, c_im, d, w_glu, b_glu, x0_re, x0_im):
    f32 = jnp.float32
    bsz, L, _ = u.shape
    a_re, a_im = a_re.astype(f32), a_im.astype(f32)
    dt = jnp.exp(log_dt.astype(f32))[:, None]
    mag = jnp.exp(a_re * dt)
    ab_re = mag * jnp.cos(a_im * dt)
    ab_im = mag * jnp.sin(a_im * dt)
    den = a_re * a_re + a_im * a_im
    nr, ni = ab_re - 1.0, ab_im
    f_re = (nr * a_re + ni * a_im) / den
    f_im = (ni * a_re - nr * a_im) / den
    b_re, b_im = b_re.astype(f32), b_im.astype(f32)
    bb_re = f_re[..., None] * b_re - f_im[..., None] * b_im
    bb_im = f_re[..., None] * b_im + f_im[..., None] * b_re
    uf = u.astype(f32)
    ug = uf.reshape(bsz, L, S5_GROUPS, S5_GROUP_CH)
    bu_re = jnp.einsum('blgn,gpn->blgp', ug, bb_re)
    bu_im = jnp.einsum('blgn,gpn->blgp', ug, bb_im)
    shape_a = (1, L, S5_GROUPS, S5_STATE)
    cum_re, cum_im, xs_re, xs_im = lax.associative_scan(
        _ssm_combine,
        (jnp.broadcast_to(ab_re, shape_a), jnp.broadcast_to(ab_im, shape_a), bu_re, bu_im),
        axis=1)
    if x0_re is not None:
        x0r = x0_re.astype(f32)[:, None]
        x0i = x0_im.astype(f32)[:, None]
        xs_re = xs_re + cum_re * x0r - cum_im * x0i
        xs_im = xs_im + cum_re * x0i + cum_im * x0r
    y = (jnp.einsum('gnp,blgp->blgn', c_re.astype(f32), xs_re)
         - jnp.einsum('gnp,blgp->blgn', c_im.astype(f32), xs_im))
    y = y.reshape(bsz, L, S5_WIDTH) + d.astype(f32) * uf
    g = jax.nn.gelu(y)
    out = g * jax.nn.sigmoid(g @ w_glu.astype(f32) + b_glu.astype(f32))
    return out.astype(u.dtype), xs_re[:, -1].astype(u.dtype), xs_im[:, -1].astype(u.dtype)

def _stick_breaking_block(q, k, v, q_pos):
    z = jnp.einsum('bhqd,bhkd->bhqk', q.astype(jnp.float32), k.astype(jnp.float32)) * (SB_HEAD_DIM ** -0.5)
    k_pos = jnp.arange(k.shape[2])
    mask = k_pos[None, :] < q_pos[:, None]
    log_not = jnp.where(mask, jax.nn.log_sigmoid(-z), 0.0)
    after = lax.cumsum(log_not, axis=3, reverse=True) - log_not
    w = jnp.where(mask, jnp.exp(jax.nn.log_sigmoid(z) + after), 0.0)
    return jnp.einsum('bhqk,bhkd->bhqd', w, v.astype(jnp.float32)).astype(q.dtype)

def stick_breaking_prompt(q, k, v):
    L = q.shape[2]
    outs = []
    for qs in range(0, L, SB_BLOCK):
        qe = min(qs + SB_BLOCK, L)
        outs.append(_stick_breaking_block(q[:, :, qs:qe], k[:, :, :qe], v[:, :, :qe], jnp.arange(qs, qe)))
    return jnp.concatenate(outs, axis=2)

def stick_breaking_sample(q, k, v, k_past, v_past):
    past = k_past.shape[2]
    k_all = jnp.concatenate([k_past.astype(k.dtype), k], axis=2)
    v_all = jnp.concatenate([v_past.astype(v.dtype), v], axis=2)
    return _stick_breaking_block(q, k_all, v_all, past + jnp.arange(q.shape[2]))

def moe_ffn(h, w_router, b_router, w_gate_up, b_gate_up, w_down, b_down):
    T, D = h.shape
    logits = (h @ w_router + b_router).astype(jnp.float32)
    top_val, top_idx = lax.top_k(logits, TOP_K)
    gates = jax.nn.softmax(top_val, axis=-1).astype(h.dtype)
    n_assign = T * TOP_K
    e_flat = top_idx.reshape(-1)
    tok_flat = jnp.repeat(jnp.arange(T, dtype=jnp.int32), TOP_K)
    g_flat = gates.reshape(-1)
    order = jnp.argsort(e_flat)
    e_sorted = e_flat[order]
    counts = jnp.bincount(e_flat, length=N_EXPERTS)
    padded = (counts + MOE_BLOCK - 1) // MOE_BLOCK * MOE_BLOCK
    start = jnp.cumsum(counts) - counts
    pend = jnp.cumsum(padded)
    pstart = pend - padded
    dest = pstart[e_sorted] + (jnp.arange(n_assign) - start[e_sorted])
    n_blocks = (n_assign + N_EXPERTS * (MOE_BLOCK - 1) + MOE_BLOCK - 1) // MOE_BLOCK
    n_rows = n_blocks * MOE_BLOCK
    row_tok = jnp.full((n_rows,), T, jnp.int32).at[dest].set(tok_flat[order])
    row_gate = jnp.zeros((n_rows,), h.dtype).at[dest].set(g_flat[order])
    block_expert = jnp.minimum(
        jnp.searchsorted(pend, jnp.arange(n_blocks) * MOE_BLOCK, side='right'), N_EXPERTS - 1)
    h_pad = jnp.concatenate([h, jnp.zeros((1, D), h.dtype)], axis=0)

    def run_block(args):
        tok, e = args
        gu = h_pad[tok] @ w_gate_up[e] + b_gate_up[e]
        gate = jnp.minimum(gu[:, :D_FF], SWIGLU_LIMIT)
        up = jnp.clip(gu[:, D_FF:], -SWIGLU_LIMIT, SWIGLU_LIMIT)
        act = (up + 1.0) * gate * jax.nn.sigmoid(SWIGLU_ALPHA * gate)
        return act @ w_down[e] + b_down[e]

    out_rows = lax.map(run_block, (row_tok.reshape(n_blocks, MOE_BLOCK), block_expert))
    out_rows = out_rows.reshape(n_rows, D) * row_gate[:, None]
    return jnp.zeros((T + 1, D), h.dtype).at[row_tok].add(out_rows)[:T]

def setup_inputs(seed: int = 0) -> dict:
    key = jax.random.key(seed)
    ks = jax.random.split(key, 40)
    f32 = jnp.float32

    def nrm(k, shape, s):
        return jax.random.normal(k, shape, f32) * s

    n_idx = jnp.arange(S5_STATE, dtype=f32)
    return {
        'x_prompt': nrm(ks[0], (BATCH, SEQ, D_MODEL), 1.0),
        'x_sample': nrm(ks[1], (DEC_BATCH, DEC_SEQ, D_MODEL), 1.0),
        'cache_k': nrm(ks[2], (DEPTH, DEC_BATCH, SB_HEADS, PAST_LEN, SB_HEAD_DIM), 1.0),
        'cache_v': nrm(ks[3], (DEPTH, DEC_BATCH, SB_HEADS, PAST_LEN, SB_HEAD_DIM), 1.0),
        'state_s5_re': nrm(ks[4], (DEPTH, DEC_BATCH, S5_GROUPS, S5_STATE), 0.1),
        'state_s5_im': nrm(ks[5], (DEPTH, DEC_BATCH, S5_GROUPS, S5_STATE), 0.1),
        'c_prompt': nrm(ks[6], (BATCH, D_MODEL), 1.0),
        'c_sample': nrm(ks[7], (DEC_BATCH, D_MODEL), 1.0),
        'ln_in_g': 1.0 + nrm(ks[8], (D_MODEL,), 0.02),
        'ln_in_b': nrm(ks[9], (D_MODEL,), 0.02),
        'w_ada': nrm(ks[10], (DEPTH, D_MODEL, 6 * D_MODEL), 0.1 * D_MODEL ** -0.5),
        'b_ada': nrm(ks[11], (DEPTH, 6 * D_MODEL), 0.02),
        'w_in': nrm(ks[12], (DEPTH, D_MODEL, S5_WIDTH + 3 * SB_WIDTH), D_MODEL ** -0.5),
        's5_a_re': -0.5 + nrm(ks[13], (DEPTH, S5_GROUPS, S5_STATE), 0.01),
        's5_a_im': jnp.broadcast_to(math.pi * n_idx, (DEPTH, S5_GROUPS, S5_STATE)).astype(f32),
        's5_log_dt': jax.random.uniform(ks[14], (DEPTH, S5_GROUPS), f32, math.log(1e-3), math.log(1e-1)),
        's5_b_re': nrm(ks[15], (DEPTH, S5_GROUPS, S5_STATE, S5_GROUP_CH), (2 * S5_GROUP_CH) ** -0.5),
        's5_b_im': nrm(ks[16], (DEPTH, S5_GROUPS, S5_STATE, S5_GROUP_CH), (2 * S5_GROUP_CH) ** -0.5),
        's5_c_re': nrm(ks[17], (DEPTH, S5_GROUPS, S5_GROUP_CH, S5_STATE), S5_STATE ** -0.5),
        's5_c_im': nrm(ks[18], (DEPTH, S5_GROUPS, S5_GROUP_CH, S5_STATE), S5_STATE ** -0.5),
        's5_d': nrm(ks[19], (DEPTH, S5_WIDTH), 1.0),
        's5_w_glu': nrm(ks[20], (DEPTH, S5_WIDTH, S5_WIDTH), S5_WIDTH ** -0.5),
        's5_b_glu': nrm(ks[21], (DEPTH, S5_WIDTH), 0.02),
        'w_out': nrm(ks[22], (DEPTH, D_MODEL, D_MODEL), DEEPNORM_BETA * D_MODEL ** -0.5),
        'ln1_g': 1.0 + nrm(ks[23], (DEPTH, D_MODEL), 0.02),
        'ln1_b': nrm(ks[24], (DEPTH, D_MODEL), 0.02),
        'w_router': nrm(ks[25], (DEPTH, D_MODEL, N_EXPERTS), D_MODEL ** -0.5),
        'b_router': nrm(ks[26], (DEPTH, N_EXPERTS), 0.01),
        'w_gate_up': nrm(ks[27], (DEPTH, N_EXPERTS, D_MODEL, 2 * D_FF), D_MODEL ** -0.5),
        'b_gate_up': nrm(ks[28], (DEPTH, N_EXPERTS, 2 * D_FF), 0.02),
        'w_down': nrm(ks[29], (DEPTH, N_EXPERTS, D_FF, D_MODEL), DEEPNORM_BETA * D_FF ** -0.5),
        'b_down': nrm(ks[30], (DEPTH, N_EXPERTS, D_MODEL), 0.02),
        'ln2_g': 1.0 + nrm(ks[31], (DEPTH, D_MODEL), 0.02),
        'ln2_b': nrm(ks[32], (DEPTH, D_MODEL), 0.02),
    }

def reference(x_prompt, x_sample, cache_k, cache_v, state_s5_re, state_s5_im, c_prompt, c_sample,
              ln_in_g, ln_in_b, w_ada, b_ada, w_in, s5_a_re, s5_a_im, s5_log_dt, s5_b_re, s5_b_im,
              s5_c_re, s5_c_im, s5_d, s5_w_glu, s5_b_glu, w_out, ln1_g, ln1_b, w_router, b_router,
              w_gate_up, b_gate_up, w_down, b_down, ln2_g, ln2_b):
    assert x_sample.shape[1] <= CHUNK

    def run_layer(l, x, c, k_past, v_past, s0_re, s0_im):
        bsz, L, _ = x.shape
        sh1, sc1, g1, sh2, sc2, g2 = adaln_params(c, w_ada[l], b_ada[l])
        h = x * (1.0 + sc1) + sh1
        proj = h @ w_in[l]
        u = proj[..., :S5_WIDTH]
        qkv = proj[..., S5_WIDTH:].reshape(bsz, L, 3, SB_HEADS, SB_HEAD_DIM)
        q, k, v = [qkv[:, :, i].transpose(0, 2, 1, 3) for i in range(3)]
        s5_out, s_re, s_im = s5_mixer(u, s5_a_re[l], s5_a_im[l], s5_log_dt[l], s5_b_re[l], s5_b_im[l],
                                      s5_c_re[l], s5_c_im[l], s5_d[l], s5_w_glu[l], s5_b_glu[l],
                                      s0_re, s0_im)
        if k_past is None:
            attn = stick_breaking_prompt(q, k, v)
        else:
            attn = stick_breaking_sample(q, k, v, k_past, v_past)
        attn = attn.transpose(0, 2, 1, 3).reshape(bsz, L, SB_WIDTH)
        mix = jnp.concatenate([s5_out, attn], axis=-1) @ w_out[l]
        x = layer_norm(DEEPNORM_ALPHA * x + (1.0 + g1) * mix, ln1_g[l], ln1_b[l])
        h2 = x * (1.0 + sc2) + sh2
        ff = moe_ffn(h2.reshape(bsz * L, D_MODEL), w_router[l], b_router[l], w_gate_up[l], b_gate_up[l],
                     w_down[l], b_down[l]).reshape(bsz, L, D_MODEL)
        x = layer_norm(DEEPNORM_ALPHA * x + (1.0 + g2) * ff, ln2_g[l], ln2_b[l])
        return x, k, v, s_re, s_im

    xp = layer_norm(x_prompt, ln_in_g, ln_in_b)
    xs = layer_norm(x_sample, ln_in_g, ln_in_b)
    kp, vp, srp, sip = [], [], [], []
    ksm, vsm, srs, sis = [], [], [], []
    for l in range(DEPTH):
        xp, k, v, s_re, s_im = run_layer(l, xp, c_prompt, None, None, None, None)
        kp.append(k); vp.append(v); srp.append(s_re); sip.append(s_im)
        xs, k, v, s_re, s_im = run_layer(l, xs, c_sample, cache_k[l], cache_v[l], state_s5_re[l], state_s5_im[l])
        ksm.append(k); vsm.append(v); srs.append(s_re); sis.append(s_im)
    return (xp, xs, jnp.stack(kp), jnp.stack(vp), jnp.stack(srp), jnp.stack(sip),
            jnp.stack(ksm), jnp.stack(vsm), jnp.stack(srs), jnp.stack(sis))


_drawn_inputs = setup_inputs


def setup_inputs(seed=0):
    import zlib

    import numpy as np

    out = dict(_drawn_inputs(seed))
    spreads = {}
    factors = {'cache_k': 2.755,
     's5_a_re': 52.918,
     's5_c_re': 2.901,
     's5_b_glu': 20.771,
     'b_router': 4.003,
     'b_gate_up': 8.0,
     'b_down': 6.37,
     'ln2_g': 24.183,
     'ln2_b': 22.935,
     's5_c_im': 5.635}
    for name, (base, spread) in spreads.items():
        noise = np.random.default_rng([zlib.crc32(name.encode()), seed]).standard_normal(out[name].shape)
        drawn = base * np.exp(spread * noise) if base else spread * noise
        out[name] = jnp.asarray(drawn.astype(out[name].dtype))
    for name, factor in factors.items():
        out[name] = (out[name] * factor).astype(out[name].dtype)
    return out
```

```python
import math
from contextlib import ExitStack

import concourse.bass as bass
from concourse import mybir

F32 = mybir.dt.float32
BF16 = mybir.dt.bfloat16
I32 = mybir.dt.int32
U32 = mybir.dt.uint32
ALU = mybir.AluOpType
ACT = mybir.ActivationFunctionType
AX = mybir.AxisListType

P = 128
D = 1024
KT = D // P
LP, LS, PAST = 512, 32, 256
T = LP + LS
HALF = T // 2
NT = LP // P + 1
ROWS = [P] * (NT - 1) + [LS]
H, DH = 8, 64
G, NC, NS = 32, 16, 64
CH = 8
CP, CS = LP // CH, LS // CH
C = CP + CS
POS = CP + 1 + CS + 1
S5W = G * NC
E, TOPK = 32, 4
FF = D
EPS = 1e-5
DN_ALPHA = 2 ** 0.25
LIMIT, SW_ALPHA = 7.0, 1.702
CW = 256
RING = 12
PRE_RING = 4
N_ADA, N_IN, N_OUT = 6 * D // CW, 2 * D // CW, D // CW
PRE = N_ADA + N_IN + N_OUT
OVF = 16
NB = E + OVF
assert PRE % PRE_RING == 0 and N_OUT == PRE_RING


def chained(eng, sem):
    n = [0]

    def link(ins):
        n[0] += 1
        ins.then_inc(sem, 1)
        eng.wait_ge(sem, n[0])
    return link


def build(nc, A, O):
    top = ExitStack()
    with top:
        stage_sems = []

        def sem(name, lasting=False):
            s = nc.alloc_semaphore(name=name)
            if not lasting:
                stage_sems.append(s)
            return s

        def end_stage():
            nc.clear_and_free_semaphores(stage_sems)
            stage_sems.clear()
            nc.all_engine_barrier()

        def keep(name, shape, dt=F32):
            return top.enter_context(nc.sbuf_tensor(name, shape, dt))

        def scratch(name, shape, dt=F32):
            return nc.dram_tensor(name, shape, dt, kind="Internal").ap()

        PS = top.enter_context(nc.psum_tensor("PS", [P, 8, 512], F32))
        ring = keep("ring", [P, RING, 2048])
        ring_full = [sem(f"ring_full{s}", True) for s in range(RING)]
        ident = keep("ident", [P, P])
        x_tok = keep("x_tok", [P, NT, D])
        one_p = keep("one_p", [P, 2])
        posblk = keep("posblk", [P, NT, NB])
        gates = keep("gates", [P, NT, TOPK])
        gate_of = keep("gate_of", [P, NT, E])
        yrow = keep("yrow", [P, NT, TOPK], U32)
        ovf = keep("ovf", [P, 1 + OVF], I32)
        sel96 = keep("sel96", [3 * E, NB])
        bias3 = keep("bias3", [3 * E, 2 * FF], BF16)
        mod_rows = scratch("mod_rows", (2, 6 * D))
        h2_dram = scratch("h2_dram", (T, D))
        y_dram = scratch("y_dram", (NB * P, D))

        def spare(offset, parts, *dims):
            size = math.prod(dims)
            assert offset + size <= (RING - PRE_RING) * 2048
            v = ring[0:parts, PRE_RING:RING, :].rearrange("p s c -> p (s c)")[:, offset:offset + size]
            names = "abcde"[:len(dims)]
            if len(dims) == 1:
                return v
            return v.rearrange(f"p ({' '.join(names)}) -> p {' '.join(names)}", **dict(zip(names, dims)))

        def wide(n):
            return ring[:, n % PRE_RING, :].rearrange("p (k c) -> p k c", k=KT)

        def dense_source(n):
            for w, first, count in ((A["w_ada"], 0, N_ADA), (A["w_in"], N_ADA, N_IN), (A["w_out"], N_ADA + N_IN, N_OUT)):
                if n < first + count:
                    c = n - first
                    return w[0, :, c * CW:(c + 1) * CW].rearrange("(k p) c -> p k c", p=P)

        def stream_dense(sp, first, last, wait_used):
            for n in range(first, last):
                if n >= PRE_RING:
                    wait_used(n - PRE_RING)
                sp.dma_start(wide(n), dense_source(n)).then_inc(ring_full[n % PRE_RING], 16)

        def wait_dense(pe, n):
            pe.wait_ge(ring_full[n % PRE_RING], 16 * (n // PRE_RING + 1))

        mid = ExitStack()
        pj = ExitStack()
        with mid:
            def hold(name, shape, dt=F32):
                return mid.enter_context(nc.sbuf_tensor(name, shape, dt))
            mod = hold("mod", [P, 2, 6 * KT])
            TB = hold("TB", [P, G, P])
            CA = hold("CA", [P, G, CH + 1, NC])
            Dg = hold("Dg", [P, G, P])
            Jm = hold("Jm", [P, P])
            phase = hold("phase", [P, 3, G])
            env = dict(locals())
            stage_tables(nc, A, env)
            env["projT"] = hold("projT", [P, 2 * KT, T])
            end_stage()
            stage_project(nc, A, env)
            end_stage()
            stage_s5(nc, A, O, env)
            end_stage()
            stage_attention(nc, A, O, env)
            end_stage()
            stage_mix(nc, A, env)
            end_stage()
        stage_moe(nc, A, env)
        end_stage()
        stage_output(nc, A, O, env)


def stage_tables(nc, A, env):
    PS, ident, x_tok, one_p, mod = (env[k] for k in ("PS", "ident", "x_tok", "one_p", "mod"))
    TB, CA, Dg, Jm, phase = (env[k] for k in ("TB", "CA", "Dg", "Jm", "phase"))
    mod_rows, sem = env["mod_rows"], env["sem"]
    ada_used = sem("ada_used")
    spare = env["spare"]
    stream_dense, wait_dense, wide = env["stream_dense"], env["wait_dense"], env["wide"]
    st = ExitStack()
    with st:
        def sb(name, shape, dt=F32):
            return st.enter_context(nc.sbuf_tensor(name, shape, dt))
        c16 = sb("c16", [2 * KT, P])
        cT = sb("cT", [P, 2 * KT])
        bada = sb("bada", [6 * KT, P])
        modT = sb("modT", [2 * 6 * KT, P])
        ln_row = spare(12000, P, 2, D)
        stats = sb("stats", [P, NT, 2, 6])
        mv = sb("mv", [P, NT, 2])
        std = sb("std", [P, NT])
        q = sb("q", [G, 24, NS])
        qi = sb("qi", [G, NS], I32)
        ldt = sb("ldt", [G, 1])
        dt_ = sb("dt_", [G, 1])
        M = spare(8192, G, 23, 2, NS)
        s5c = spare(14048, P, 23, G)
        V = sb("V", [P, G, NC])
        JV = sb("JV", [P, G, NC])
        tmp = sb("tmp", [P, G, NC])
        tmp2 = sb("tmp2", [P, G, NC])
        cs = sb("cs", [P, 4, 2, 2, NS])
        V2 = sb("V2", [P, 2, G, NC])
        JB = sb("JB", [P, G, NC])
        TBs = spare(0, P, G, CH, NC)
        Kt = spare(4096, NC, G, P)
        d16 = sb("d16", [NC, G])
        dd = sb("dd", [NC, G, NC])
        bcol = sb("bcol", [P, 6 * KT])

        ld_x, ld_c, ld_b, ld_ln, ld_q, ld_v, ld_cs, ld_d = (sem(n) for n in ("ld_x", "ld_c", "ld_b", "ld_ln", "ld_q", "ld_v", "ld_cs", "ld_d"))
        s_pool, s_const, s_one = sem("t_pool"), sem("t_const"), sem("t_one")
        c_silu, c_turned, c_ready = sem("c_silu"), sem("c_turned"), sem("c_ready")
        mod_done, bada_turned, mod_sum, modT_turned, modT_ready, mod_sent = (sem(n) for n in ("mod_done", "bada_turned", "mod_sum", "modT_turned", "modT_ready", "mod_sent"))
        var_ready, std_ready = sem("var_ready"), sem("std_ready")
        t_dve, t_act = sem("t_dve"), sem("t_act")
        dt_ready, ang_ready, trig_ready = sem("dt_ready"), sem("ang_ready"), sem("trig_ready")
        m_ready, m_turned, m_copied = sem("m_ready"), sem("m_turned"), sem("m_copied")
        cs_ready, cs_turned, cs_copied = sem("cs_ready"), sem("cs_turned"), sem("cs_copied")
        bb_ready, jb_done, tbs_ready, tb_turned, tb_copied = (sem(n) for n in ("bb_ready", "jb_done", "tbs_ready", "tb_turned", "tb_copied"))
        ca_ready, k_done, k_copied, kt_ready, dg_zero, dg_done = (sem(n) for n in ("ca_ready", "k_done", "k_copied", "kt_ready", "dg_zero", "dg_done"))

        block = st.enter_context(nc.Block())

        @block.sync
        def _(sp):
            stream_dense(sp, 0, N_ADA + PRE_RING, lambda n: sp.wait_ge(ada_used, n + 1))

        @block.gpsimd
        def _(pool):
            link = chained(pool, s_pool)
            pool.dma_start(ln_row[:, 0, :], A["ln_in_g"].partition_broadcast(P)).then_inc(ld_ln, 16)
            pool.dma_start(ln_row[:, 1, :], A["ln_in_b"].partition_broadcast(P)).then_inc(ld_ln, 16)
            link(pool.memset(ident[:], 0.0))
            pool.affine_select(out=ident[:], in_=ident[:], compare_op=ALU.not_equal, fill=1.0, base=0,
                               pattern=[[-1, P]], channel_multiplier=1).then_inc(s_const, 1)
            link(pool.memset(Jm[:], 0.0))
            link(pool.affine_select(out=Jm[:], in_=Jm[:], compare_op=ALU.not_equal, fill=-1.0, base=-NS,
                                    pattern=[[-1, P]], channel_multiplier=1))
            pool.affine_select(out=Jm[:], in_=Jm[:], compare_op=ALU.not_equal, fill=1.0, base=NS,
                               pattern=[[-1, P]], channel_multiplier=1).then_inc(s_const, 1)
            pool.memset(Dg[:], 0.0).then_inc(dg_zero, 1)
            pool.wait_ge(dg_zero, 1)
            pool.wait_ge(kt_ready, 1)
            for j in range(CH):
                pool.dma_start(Dg[NC * j:NC * (j + 1), :, NC * j:P], Kt[:, :, 0:P - NC * j]).then_inc(dg_done, 16)
            pool.wait_ge(dg_done, 16 * CH)

        @block.scalar
        def _(act):
            link = chained(act, t_act)
            act.dma_start(c16[0:KT, :], A["c_prompt"].rearrange("a (k p) -> (a k) p", p=P)).then_inc(ld_c, 16)
            act.dma_start(c16[KT:2 * KT, :], A["c_sample"].rearrange("a (k p) -> (a k) p", p=P)).then_inc(ld_c, 16)
            act.dma_start(bada[:], A["b_ada"].rearrange("a (k p) -> (a k) p", p=P)).then_inc(ld_b, 16)
            act.dma_start(q[:, 0, :], A["s5_a_re"][0]).then_inc(ld_q, 16)
            act.dma_start(q[:, 1, :], A["s5_a_im"][0]).then_inc(ld_q, 16)
            act.dma_start(ldt[:], A["s5_log_dt"].rearrange("a g -> g a")).then_inc(ld_q, 16)
            act.dma_start(x_tok[:, 0:NT - 1, :], A["x_prompt"][0].rearrange("(t p) d -> p t d", p=P)).then_inc(ld_x, 16)
            act.dma_start(x_tok[0:LS, NT - 1, :], A["x_sample"][0]).then_inc(ld_x, 16)
            b_re, b_im = (A[n][0].rearrange("g p n -> p g n") for n in ("s5_b_re", "s5_b_im"))
            act.dma_start(V[0:NS], b_re).then_inc(ld_v, 16)
            act.dma_start(V[NS:P], b_im).then_inc(ld_v, 16)
            act.dma_start(JV[NS:P], b_re).then_inc(ld_v, 16)
            act.dma_start(JV[0:NS], b_im).then_inc(ld_v, 16)
            c_re, c_im = (A[n][0].rearrange("(t g) n p -> (g n) t p", t=4) for n in ("s5_c_re", "s5_c_im"))
            act.dma_start(cs[:, :, 0, 0, :], c_re).then_inc(ld_cs, 16)
            act.dma_start(cs[:, :, 1, 1, :], c_re).then_inc(ld_cs, 16)
            act.dma_start(cs[:, :, 0, 1, :], c_im).then_inc(ld_cs, 16)
            act.dma_start(d16[:], A["s5_d"].rearrange("a (g n) -> (a n) g", n=NC), allow_slow_non_contiguous=True).then_inc(ld_d, 16)
            act.wait_ge(ld_c, 32)
            nc.scalar.activation(c16[:], c16[:], ACT.Silu).then_inc(c_silu, 1)
            act.wait_ge(ld_q, 48)
            nc.scalar.activation(dt_[:], ldt[:], ACT.Exp).then_inc(dt_ready, 1)
            act.wait_ge(ang_ready, 1)
            nc.scalar.activation(q[:, 3, :], q[:, 2, :], ACT.Exp).then_inc(trig_ready, 1)
            nc.scalar.activation(q[:, 7, :], q[:, 5, :], ACT.Sin).then_inc(trig_ready, 1)
            nc.scalar.activation(q[:, 8, :], q[:, 6, :], ACT.Sin).then_inc(trig_ready, 1)
            act.wait_ge(cs_turned, 1)
            nc.scalar.copy(V2[:].rearrange("p v g n -> p v (g n)"), PS[:, 4:6, :]).then_inc(cs_copied, 1)
            for r in range(G // 4):
                act.wait_ge(tb_turned, r + 1)
                nc.scalar.copy(TB[:, 4 * r:4 * r + 4, :], PS[:, 2 + r % 2, :].rearrange("p (g s) -> p g s", g=4)).then_inc(tb_copied, 1)
            for r in range(G // 4):
                act.wait_ge(k_done, r + 1)
                nc.scalar.copy(Kt[:, 4 * r:4 * r + 4, :], PS[0:NC, 6 + r % 2, :].rearrange("p (g s) -> p g s", g=4)).then_inc(k_copied, 1)
            act.wait_ge(var_ready, NT)
            act.wait_ge(s_one, 2)
            for ti, r in enumerate(ROWS):
                nc.scalar.activation(std[0:r, ti:ti + 1], mv[0:r, ti, 1:2], ACT.Sqrt, bias=one_p[0:r, 1:2]).then_inc(std_ready, 1)
            act.wait_ge(modT_ready, 1)
            act.dma_start(mod_rows.rearrange("s (k p) -> (s k) p", p=P), modT[:]).then_inc(mod_sent, 16)
            act.wait_ge(mod_sent, 16)

        @block.vector
        def _(dve):
            link = chained(dve, t_dve)
            vec = nc.vector

            def done(ins, sem, value):
                ins.then_inc(sem, 1)
                dve.wait_ge(sem, value)

            vec.memset(one_p[:, 0:1], 1.0).then_inc(s_one, 1)
            vec.memset(one_p[:, 1:2], EPS).then_inc(s_one, 1)
            dve.wait_ge(c_turned, 1)
            vec.tensor_copy(cT[:], PS[:, 1, 0:2 * KT]).then_inc(c_ready, 1)

            are, aim, ard, mag, th, ang, hang, sn, shalf, a_r, a_i, den, nr, t0, t1, cosn, vr, vi, t2 = (
                q[:, k, :] for k in range(19))
            dve.wait_ge(dt_ready, 1)
            link(vec.tensor_scalar(ard, are, dt_[:, 0:1], None, ALU.mult))
            link(vec.tensor_scalar(th, aim, dt_[:, 0:1], None, ALU.mult))
            link(vec.tensor_scalar(qi[:], th, 1.0 / (2 * math.pi), None, ALU.mult))
            link(vec.tensor_copy(t0, qi[:]))
            p1 = 6.28125
            p2 = float(int((2 * math.pi - p1) * 2 ** 22)) / 2 ** 22
            p3 = 2 * math.pi - p1 - p2
            link(vec.scalar_tensor_tensor(out=ang, in0=t0, scalar=-p1, in1=th, op0=ALU.mult, op1=ALU.add))
            link(vec.scalar_tensor_tensor(out=ang, in0=t0, scalar=-p2, in1=ang, op0=ALU.mult, op1=ALU.add))
            link(vec.scalar_tensor_tensor(out=ang, in0=t0, scalar=-p3, in1=ang, op0=ALU.mult, op1=ALU.add))
            link(vec.tensor_scalar(ang, ang, 3.1415925, -3.1415925, ALU.min, ALU.max))
            vec.tensor_scalar(hang, ang, 0.5, None, ALU.mult).then_inc(ang_ready, 1)
            dve.wait_ge(trig_ready, 3)
            link(vec.tensor_tensor(t0, shalf, shalf, ALU.mult))
            link(vec.tensor_scalar(cosn, t0, -2.0, 1.0, ALU.mult, ALU.add))
            link(vec.tensor_tensor(a_r, mag, cosn, ALU.mult))
            link(vec.tensor_tensor(a_i, mag, sn, ALU.mult))

            def cmul(outr, outi, xr, xi, yr, yi, u, v):
                link(vec.tensor_tensor(u, xr, yr, ALU.mult))
                link(vec.tensor_tensor(v, xi, yi, ALU.mult))
                link(vec.tensor_tensor(t2, xr, yi, ALU.mult))
                link(vec.tensor_tensor(outi, xi, yr, ALU.mult))
                link(vec.tensor_tensor(outi, outi, t2, ALU.add))
                link(vec.tensor_tensor(outr, u, v, ALU.subtract))

            fr, fi = M[:, 0, 0, :], M[:, 1, 0, :]
            link(vec.tensor_tensor(t0, are, are, ALU.mult))
            link(vec.tensor_tensor(t1, aim, aim, ALU.mult))
            link(vec.tensor_tensor(t0, t0, t1, ALU.add))
            link(vec.reciprocal(den, t0))
            link(vec.tensor_scalar(nr, a_r, -1.0, None, ALU.add))
            link(vec.tensor_tensor(t0, nr, are, ALU.mult))
            link(vec.tensor_tensor(t1, a_i, aim, ALU.mult))
            link(vec.tensor_tensor(t0, t0, t1, ALU.add))
            link(vec.tensor_tensor(fr, t0, den, ALU.mult))
            link(vec.tensor_tensor(t0, a_i, are, ALU.mult))
            link(vec.tensor_tensor(t1, nr, aim, ALU.mult))
            link(vec.tensor_tensor(t0, t0, t1, ALU.subtract))
            link(vec.tensor_tensor(fi, t0, den, ALU.mult))
            link(vec.tensor_copy(vr, cosn))
            link(vec.tensor_copy(vi, sn))
            link(vec.tensor_tensor(nr, mag, mag, ALU.mult))
            for _ in range(2):
                cmul(vr, vi, vr, vi, vr, vi, t0, t1)
                link(vec.tensor_tensor(nr, nr, nr, ALU.mult))
            cmul(M[:, 2, 0, :], M[:, 3, 0, :], vr, vi, vr, vi, t0, t1)
            link(vec.tensor_copy(M[:, 4, 0, :], nr))
            pr = [M[:, 5 + k, 0, :] for k in range(CH + 1)]
            pi = [M[:, 14 + k, 0, :] for k in range(CH + 1)]
            link(vec.memset(pr[0], 1.0))
            link(vec.memset(pi[0], 0.0))
            link(vec.tensor_copy(pr[1], a_r))
            link(vec.tensor_copy(pi[1], a_i))
            for k in range(2, CH + 1):
                cmul(pr[k], pi[k], pr[k // 2], pi[k // 2], pr[k - k // 2], pi[k - k // 2], t0, t1)
            vec.tensor_copy(M[:, :, 1, :], M[:, :, 0, :]).then_inc(m_ready, 1)
            dve.wait_ge(ld_cs, 48)
            link(vec.tensor_scalar(cs[:, :, 0, 1, :], cs[:, :, 0, 1, :], -1.0, None, ALU.mult))
            link(vec.tensor_copy(cs[:, :, 1, 0, :], cs[:, :, 0, 1, :]))
            vec.tensor_scalar(cs[:, :, 1, 1, :], cs[:, :, 1, 1, :], -1.0, None, ALU.mult).then_inc(cs_ready, 1)
            dve.wait_ge(m_turned, 1)
            link(vec.tensor_copy(s5c[:, 0:16, :], PS[:, 2, :].rearrange("p (k g) -> p k g", g=G)))
            link(vec.tensor_copy(phase[:], PS[:, 2, 2 * G:5 * G].rearrange("p (k g) -> p k g", g=G)))
            done(vec.tensor_copy(s5c[:, 16:23, :], PS[:, 3, 0:7 * G].rearrange("p (k g) -> p k g", g=G)), m_copied, 1)

            def per_group(k):
                return s5c[:, k, :].unsqueeze(2).to_broadcast((P, G, NC))

            dve.wait_ge(ld_v, 64)
            link(vec.tensor_scalar(JV[0:NS], JV[0:NS], -1.0, None, ALU.mult))
            link(vec.tensor_tensor(V[:], V[:], per_group(0), ALU.mult))
            link(vec.tensor_tensor(JV[:], JV[:], per_group(1), ALU.mult))
            done(vec.tensor_tensor(V[:], V[:], JV[:], ALU.add), bb_ready, 1)
            dve.wait_ge(jb_done, 1)
            link(vec.tensor_copy(JB[:].rearrange("p g n -> p (g n)"), PS[:, 1, :]))
            for j in range(CH):
                link(vec.tensor_tensor(tmp[:], V[:], per_group(5 + CH - 1 - j), ALU.mult))
                link(vec.tensor_tensor(tmp2[:], JB[:], per_group(14 + CH - 1 - j), ALU.mult))
                done(vec.tensor_tensor(TBs[:, :, j, :], tmp[:], tmp2[:], ALU.add), tbs_ready, j + 1)
            dve.wait_ge(cs_copied, 1)
            for k in range(CH + 1):
                link(vec.tensor_tensor(tmp[:], V2[:, 0], per_group(5 + k), ALU.mult))
                link(vec.tensor_tensor(tmp2[:], V2[:, 1], per_group(14 + k), ALU.mult))
                done(vec.tensor_tensor(CA[:, :, k, :], tmp[:], tmp2[:], ALU.add), ca_ready, k + 1)
            dve.wait_ge(ld_d, 16)
            link(vec.tensor_tensor(dd[:], ident[0:NC, 0:NC].unsqueeze(1).to_broadcast((NC, G, NC)),
                                   d16[:].unsqueeze(2).to_broadcast((NC, G, NC)), ALU.mult))
            dve.wait_ge(k_copied, G // 4)
            vec.tensor_tensor(Kt[:, :, 0:NC], Kt[:, :, 0:NC], dd[:], ALU.add).then_inc(kt_ready, 1)

            dve.wait_ge(ld_x, 32)
            for ti, r in enumerate(ROWS):
                for h in range(2):
                    link(vec.bn_stats(stats[0:r, ti, h, :], x_tok[0:r, ti, 512 * h:512 * (h + 1)]))
                done(vec.bn_aggr(mv[0:r, ti, :], stats[0:r, ti].rearrange("p a b -> p (a b)")), var_ready, ti + 1)
            dve.wait_ge(ld_ln, 32)
            for ti, r in enumerate(ROWS):
                dve.wait_ge(std_ready, ti + 1)
                link(vec.reciprocal(std[0:r, ti:ti + 1], std[0:r, ti:ti + 1]))
                x = x_tok[0:r, ti, :]
                link(vec.tensor_scalar(x, x, mv[0:r, ti, 0:1], std[0:r, ti:ti + 1], ALU.subtract, ALU.mult))
                link(vec.tensor_tensor(x, x, ln_row[0:r, 0, :], ALU.mult))
                link(vec.tensor_tensor(x, x, ln_row[0:r, 1, :], ALU.add))

            dve.wait_ge(mod_done, 1)
            link(vec.tensor_copy(bcol[:], PS[:, 1, 0:6 * KT]))
            link(vec.tensor_tensor(mod[:], PS[:, 0, 0:2 * 6 * KT].rearrange("p (s k) -> p s k", s=2),
                                   bcol[:].unsqueeze(1).to_broadcast((P, 2, 6 * KT)), ALU.add))
            for k in (1, 2, 4, 5):
                m = mod[:, :, k * KT:(k + 1) * KT]
                ins = vec.tensor_scalar(m, m, 1.0, None, ALU.add)
                ins.then_inc(mod_sum, 1)
            dve.wait_ge(modT_turned, 1)
            vec.tensor_copy(modT[:], PS[0:2 * 6 * KT, 1, 0:P]).then_inc(modT_ready, 1)

        @block.tensor
        def _(pe):
            mm, tr = nc.tensor.matmul, nc.tensor.transpose
            pe.wait_ge(s_const, 2)
            pe.wait_ge(c_silu, 1)
            tr(PS[:, 1, 0:2 * KT], c16[:], ident[0:2 * KT, 0:2 * KT]).then_inc(c_turned, 1)
            pe.wait_ge(c_ready, 1)

            def ada(first, last):
                for n in range(first, last):
                    wait_dense(pe, n)
                    for t in range(CW // P):
                        for k in range(KT):
                            o = n * (CW // P) + t
                            ins = mm(PS[:, 0, o:o + 6 * KT + 1:6 * KT], wide(n)[:, k, P * t:P * (t + 1)], cT[:, k::KT],
                                     start=(n == 0 and t == 0 and k == 0), stop=(k == KT - 1), skip_group_check=True)
                    ins.then_inc(ada_used, 1)

            ada(0, 6)
            pe.wait_ge(m_ready, 1)
            for k in range(23):
                ins = tr(PS[:, 2 + k // 16, G * (k % 16):G * (k % 16 + 1)],
                         M[:, k].rearrange("g a s -> g (a s)"), ident[0:G, 0:G])
            ins.then_inc(m_turned, 1)
            pe.wait_ge(cs_ready, 1)
            for v in range(2):
                for t in range(4):
                    ins = tr(PS[:, 4 + v, P * t:P * (t + 1)], cs[:, t, v].rearrange("r a s -> r (a s)"), ident[:])
            ins.then_inc(cs_turned, 1)
            ada(6, 10)
            pe.wait_ge(bb_ready, 1)
            mm(PS[:, 1, :], Jm[:], V[:].rearrange("p g n -> p (g n)"), start=True, stop=True).then_inc(jb_done, 1)
            ada(10, 14)
            pe.wait_ge(tbs_ready, CH)
            pe.wait_ge(m_copied, 1)
            for r in range(G // 4):
                if r >= 2:
                    pe.wait_ge(tb_copied, r - 1)
                for g in range(4):
                    ins = tr(PS[:, 2 + r % 2, P * g:P * (g + 1)], TBs[:, 4 * r + g].rearrange("p j n -> p (j n)"), ident[:])
                ins.then_inc(tb_turned, 1)
            ada(14, 20)
            pe.wait_ge(ca_ready, CH + 1)
            for r in range(G // 4):
                if r >= 2:
                    pe.wait_ge(k_copied, r - 1)
                for g in range(4):
                    ins = mm(PS[0:NC, 6 + r % 2, P * g:P * (g + 1)], V[:, 4 * r + g, :],
                             CA[:, 4 * r + g, 0:CH, :].rearrange("p k n -> p (k n)"), start=True, stop=True)
                ins.then_inc(k_done, 1)
            ada(20, N_ADA)
            pe.wait_ge(ld_b, 16)
            tr(PS[:, 1, 0:6 * KT], bada[:], ident[0:6 * KT, 0:6 * KT]).then_inc(mod_done, 1)
            pe.wait_ge(mod_sum, 4)
            tr(PS[0:2 * 6 * KT, 1, 0:P], mod[:].rearrange("p s k -> p (s k)"), ident[:]).then_inc(modT_turned, 1)


def stage_project(nc, A, env):
    PS, ident, x_tok, mod, phase, projT = (env[k] for k in ("PS", "ident", "x_tok", "mod", "phase", "projT"))
    spare, sem = env["spare"], env["sem"]
    stream_dense, wait_dense, wide = env["stream_dense"], env["wait_dense"], env["wide"]
    cosT, sinT, decay = spare(0, P, G, POS), spare(2240, P, G, POS), spare(4480, P, G, POS)
    hT = spare(6720, P, KT, T)
    pa, pb = spare(11072, P, G, 32), spare(12096, P, G, 32)
    wr, wi, wt = spare(13120, P, G), spare(13152, P, G), spare(13184, P, G)
    x_turned, h_ready, proj_done, proj_copied, t_dve = (sem(n) for n in ("x_turned", "h_ready", "proj_done", "proj_copied", "p_dve"))
    with nc.Block() as block:
        @block.sync
        def _(sp):
            stream_dense(sp, N_ADA + PRE_RING, PRE, lambda n: sp.wait_ge(proj_done, 2 * (n - N_ADA + 1)))

        @block.tensor
        def _(pe):
            for ti, r in enumerate(ROWS):
                if ti >= 2:
                    pe.wait_ge(h_ready, ti - 1)
                b = 4 + 2 * (ti % 2)
                for k in range(KT):
                    ins = nc.tensor.transpose(PS[:, b + k // 4, P * (k % 4):P * (k % 4) + r],
                                              x_tok[0:r, ti, P * k:P * (k + 1)], ident[0:r, 0:r])
                ins.then_inc(x_turned, 1)
            pe.wait_ge(h_ready, NT)
            for ct in range(2 * KT):
                n = N_ADA + ct // 2
                if ct % 2 == 0:
                    wait_dense(pe, n)
                b = 2 * (ct % 4)
                if ct >= 4:
                    pe.wait_ge(proj_copied, ct - 3)
                for k in range(KT):
                    for h in range(2):
                        ins = nc.tensor.matmul(PS[:, b + h, 0:HALF], wide(n)[:, k, P * (ct % 2):P * (ct % 2 + 1)],
                                               hT[:, k, HALF * h:HALF * (h + 1)], start=(k == 0), stop=(k == KT - 1))
                ins.then_inc(proj_done, 1)

        @block.scalar
        def _(act):
            for ct in range(2 * KT):
                act.wait_ge(proj_done, ct + 1)
                b = 2 * (ct % 4)
                nc.scalar.activation(projT[:, ct, :].rearrange("p (h t) -> p h t", h=2), PS[:, b:b + 2, 0:HALF], ACT.Copy,
                                     scale=DH ** -0.5 if 4 <= ct < 8 else 1.0).then_inc(proj_copied, 1)

        @block.vector
        def _(dve):
            link = chained(dve, t_dve)
            vec = nc.vector
            for ti, r in enumerate(ROWS):
                dve.wait_ge(x_turned, ti + 1)
                s, b = ti // (NT - 1), 4 + 2 * (ti % 2)
                for k in range(KT):
                    ins = vec.tensor_scalar(hT[:, k, P * ti:P * ti + r], PS[:, b + k // 4, P * (k % 4):P * (k % 4) + r],
                                            mod[:, s, KT + k:KT + k + 1], mod[:, s, k:k + 1], ALU.mult, ALU.add)
                ins.then_inc(h_ready, 1)
            link(vec.tensor_copy(wr, phase[:, 0, :]))
            link(vec.tensor_copy(wi, phase[:, 1, :]))
            link(vec.memset(cosT[:, :, 0:1], 1.0))
            link(vec.memset(sinT[:, :, 0:1], 0.0))
            m = 1
            while m < CP:
                a, b = pa[:, :, 0:m], pb[:, :, 0:m]
                br, bi = (w.unsqueeze(2).to_broadcast((P, G, m)) for w in (wr, wi))
                c0, s0 = cosT[:, :, 0:m], sinT[:, :, 0:m]
                c1, s1 = cosT[:, :, m:2 * m], sinT[:, :, m:2 * m]
                link(vec.tensor_tensor(a, c0, br, ALU.mult))
                link(vec.tensor_tensor(b, s0, bi, ALU.mult))
                link(vec.tensor_tensor(c1, a, b, ALU.subtract))
                link(vec.tensor_tensor(a, c0, bi, ALU.mult))
                link(vec.tensor_tensor(b, s0, br, ALU.mult))
                link(vec.tensor_tensor(s1, a, b, ALU.add))
                link(vec.tensor_tensor(wt, wr, wi, ALU.mult))
                link(vec.tensor_tensor(wr, wr, wr, ALU.mult))
                link(vec.tensor_tensor(wi, wi, wi, ALU.mult))
                link(vec.tensor_tensor(wr, wr, wi, ALU.subtract))
                link(vec.tensor_scalar(wi, wt, 2.0, None, ALU.mult))
                m *= 2
            link(vec.tensor_copy(cosT[:, :, CP:CP + 1], wr.unsqueeze(2)))
            link(vec.tensor_copy(sinT[:, :, CP:CP + 1], wi.unsqueeze(2)))
            link(vec.tensor_copy(cosT[:, :, CP + 1:POS], cosT[:, :, 0:CS + 1]))
            link(vec.tensor_copy(sinT[:, :, CP + 1:POS], sinT[:, :, 0:CS + 1]))
            link(vec.tensor_copy(decay, phase[:, 2, :].unsqueeze(2).to_broadcast((P, G, POS))))
            link(vec.memset(decay[:, :, 0:1], 0.0))
            link(vec.memset(decay[:, :, CP + 1:CP + 2], 0.0))


def stage_s5(nc, A, O, env):
    PS, ident, projT, TB, CA, Dg, Jm = (env[k] for k in ("PS", "ident", "projT", "TB", "CA", "Dg", "Jm"))
    spare, sem = env["spare"], env["sem"]
    cosT, sinT, decay = spare(0, P, G * POS), spare(2240, P, G * POS), spare(4480, P, G * POS)
    Ug = spare(6720, P, G, C)
    Uc = spare(8896, C, G, CH, NC)
    Sx = spare(8896, P, G, POS)
    Sf = spare(8896, P, G * POS)
    w1, w1f = spare(11136, P, G, POS), spare(11136, P, G * POS)
    Xp = spare(8896, P, G, C)
    Gc = spare(0, C, CH, S5W)
    gT = spare(11136, P, 4, T)
    wglu = spare(13376, P, 4, S5W)
    sg = spare(4096, P, T)
    s0 = spare(15424, G, 2, NS)
    Xf = spare(15552, P, 2, G)
    fin = spare(15616, G, 2, 2, NS)
    bglu = spare(15872, P, 4)
    (ld_s, ld_w, uc_turned, uc_copied, ug_turned, ug_copied, s_done, s_copied, x0_turned, sx_ready, j_done, w_ready,
     j2_done, x_ready, f_turned, f_copied, s_sent, y_done, y_copied, g_turned, g_copied, z_done, z_sig, z_used, t_dve, bg_turned) = (
        sem("s5_" + n) for n in ("ld_s", "ld_w", "uc_turned", "uc_copied", "ug_turned", "ug_copied", "s_done", "s_copied", "x0_turned",
                                 "sx_ready", "j_done", "w_ready", "j2_done", "x_ready", "f_turned", "f_copied", "s_sent", "y_done",
                                 "y_copied", "g_turned", "g_copied", "z_done", "z_sig", "z_used", "dve", "bg"))
    with nc.Block() as block:
        @block.sync
        def _(sp):
            sp.dma_start(s0[:, 0, :], A["state_s5_re"][0, 0]).then_inc(ld_s, 16)
            sp.dma_start(s0[:, 1, :], A["state_s5_im"][0, 0]).then_inc(ld_s, 16)
            sp.dma_start(bglu, A["s5_b_glu"].rearrange("a (c p) -> p (a c)", p=P), allow_slow_non_contiguous=True).then_inc(ld_w, 16)
            sp.dma_start(wglu, A["s5_w_glu"][0].rearrange("(k p) c -> p k c", p=P)).then_inc(ld_w, 16)
            sp.wait_ge(f_copied, 1)
            for s, (re, im) in enumerate((("s5_re_p", "s5_im_p"), ("s5_re_s", "s5_im_s"))):
                sp.dma_start(O[re][0, 0], fin[:, s, 0, :]).then_inc(s_sent, 16)
                sp.dma_start(O[im][0, 0], fin[:, s, 1, :]).then_inc(s_sent, 16)
            sp.wait_ge(s_sent, 64)

        @block.tensor
        def _(pe):
            mm, tr = nc.tensor.matmul, nc.tensor.transpose
            for j in range(CH):
                for c in range(4):
                    ins = tr(PS[0:C, j, P * c:P * (c + 1)], projT[:, c, j::CH], ident[:])
                ins.then_inc(uc_turned, 1)
            pe.wait_ge(uc_copied, CH)
            for r in range(8):
                for g in range(4):
                    ins = tr(PS[:, r, C * g:C * (g + 1)], Uc[:, 4 * r + g].rearrange("c j n -> c (j n)"), ident[0:C, 0:C])
                ins.then_inc(ug_turned, 1)
            for r in range(8):
                pe.wait_ge(ug_copied, r + 1)
                for g in range(4):
                    ins = mm(PS[:, r, C * g:C * (g + 1)], TB[:, 4 * r + g, :], Ug[:, 4 * r + g, :], start=True, stop=True)
                ins.then_inc(s_done, 1)
            pe.wait_ge(ld_s, 32)
            pe.wait_ge(s_copied, 1)
            tr(PS[:, 0, 0:G], s0.rearrange("g a s -> g (a s)"), ident[0:G, 0:G]).then_inc(x0_turned, 1)
            pe.wait_ge(sx_ready, 1)
            for b in range(5):
                ins = mm(PS[:, 1 + b, 0:448], Jm[:], Sf[:, 448 * b:448 * (b + 1)], start=True, stop=True)
            ins.then_inc(j_done, 1)
            pe.wait_ge(w_ready, 1)
            for b in range(5):
                ins = mm(PS[:, 1 + b, 0:448], Jm[:], w1f[:, 448 * b:448 * (b + 1)], start=True, stop=True)
            ins.then_inc(j2_done, 1)
            pe.wait_ge(x_ready, 1)
            for s in range(2):
                ins = tr(PS[0:G, 0, P * s:P * (s + 1)], Xf[:, s, :], ident[:])
            ins.then_inc(f_turned, 1)
            for r in range(8):
                b = 6 + r % 2
                if r >= 2:
                    pe.wait_ge(y_copied, r - 1)
                for g in range(4):
                    o = PS[0:C, b, P * g:P * (g + 1)]
                    mm(o, Ug[:, 4 * r + g, :], Dg[:, 4 * r + g, :], start=True, stop=False)
                    ins = mm(o, Xp[:, 4 * r + g, :], CA[:, 4 * r + g, 1:CH + 1, :].rearrange("p k n -> p (k n)"), start=False, stop=True)
                ins.then_inc(y_done, 1)
            pe.wait_ge(y_copied, 8)
            for c in range(4):
                for h in range(2):
                    b = 1 + (2 * c + h) % 4
                    if 2 * c + h >= 4:
                        pe.wait_ge(g_copied, 2 * c + h - 3)
                    for i in range(4):
                        ins = tr(PS[:, b, C * i:C * (i + 1)], Gc[:, 4 * h + i, P * c:P * (c + 1)], ident[0:C, 0:C])
                    ins.then_inc(g_turned, 1)
            pe.wait_ge(g_copied, 8)
            pe.wait_ge(ld_w, 32)
            for ct in range(4):
                b = 2 * (ct % 2)
                if ct >= 2:
                    pe.wait_ge(z_sig, ct - 1)
                for k in range(4):
                    for h in range(2):
                        ins = mm(PS[:, b + h, 0:HALF], wglu[:, k, P * ct:P * (ct + 1)], gT[:, k, HALF * h:HALF * (h + 1)],
                                 start=(k == 0), stop=(k == 3))
                ins.then_inc(z_done, 1)

        @block.scalar
        def _(act):
            for j in range(CH):
                act.wait_ge(uc_turned, j + 1)
                nc.scalar.copy(Uc[:, :, j, :], PS[0:C, j, :].rearrange("c (g n) -> c g n", n=NC)).then_inc(uc_copied, 1)
            for r in range(8):
                act.wait_ge(ug_turned, r + 1)
                nc.scalar.copy(Ug[:, 4 * r:4 * r + 4, :], PS[:, r, 0:4 * C].rearrange("p (g c) -> p g c", g=4)).then_inc(ug_copied, 1)
            for r in range(8):
                act.wait_ge(y_done, r + 1)
                nc.scalar.activation(Gc[:, :, 64 * r:64 * (r + 1)].rearrange("c i (g n) -> c g i n", g=4),
                                     PS[0:C, 6 + r % 2, :].rearrange("c (g i n) -> c g i n", g=4, i=CH),
                                     ACT.Gelu_apprx_tanh).then_inc(y_copied, 1)
            for ct in range(4):
                act.wait_ge(z_done, ct + 1)
                act.wait_ge(ld_w, 32)
                if ct >= 1:
                    act.wait_ge(z_used, ct)
                b = 2 * (ct % 2)
                nc.scalar.activation(sg.rearrange("p (h t) -> p h t", h=2), PS[:, b:b + 2, 0:HALF], ACT.Sigmoid,
                                     bias=bglu[:, ct:ct + 1]).then_inc(z_sig, 1)

        @block.vector
        def _(dve):
            link = chained(dve, t_dve)
            vec = nc.vector
            dve.wait_ge(ug_copied, 8)
            for r in range(8):
                dve.wait_ge(ug_turned, 8)
                dve.wait_ge(s_done, r + 1)
                src = PS[:, r, 0:4 * C].rearrange("p (g c) -> p g c", g=4)
                vec.tensor_copy(Sx[:, 4 * r:4 * r + 4, 1:CP + 1], src[:, :, 0:CP])
                vec.tensor_copy(Sx[:, 4 * r:4 * r + 4, CP + 2:POS], src[:, :, CP:C]).then_inc(s_copied, 1)
            vec.memset(Sx[:, :, 0:1], 0.0)
            dve.wait_ge(x0_turned, 1)
            vec.tensor_copy(Sx[:, :, CP + 1:CP + 2], PS[:, 0, 0:G].unsqueeze(2)).then_inc(sx_ready, 1)
            dve.wait_ge(sx_ready, 1)
            dve.wait_ge(j_done, 1)
            jp = PS[:, 1:6, 0:448]
            link(vec.tensor_tensor(w1f, cosT, Sf, ALU.mult))
            link(vec.tensor_tensor(Sf.rearrange("p (a b) -> p a b", a=5), jp, sinT.rearrange("p (a b) -> p a b", a=5), ALU.mult))
            link(vec.tensor_tensor(Sf, w1f, Sf, ALU.subtract))
            vec.tensor_tensor_scan(w1f, decay, Sf, 0.0, ALU.mult, ALU.add).then_inc(w_ready, 1)
            dve.wait_ge(w_ready, 1)
            dve.wait_ge(j2_done, 1)
            link(vec.tensor_tensor(decay.rearrange("p (a b) -> p a b", a=5), jp, sinT.rearrange("p (a b) -> p a b", a=5), ALU.mult))
            link(vec.tensor_tensor(w1f, cosT, w1f, ALU.mult))
            dk = decay.rearrange("p (g c) -> p g c", g=G)
            vec.tensor_tensor(Xp[:, :, 0:CP], w1[:, :, 0:CP], dk[:, :, 0:CP], ALU.add)
            vec.tensor_tensor(Xp[:, :, CP:C], w1[:, :, CP + 1:POS - 1], dk[:, :, CP + 1:POS - 1], ALU.add)
            vec.tensor_tensor(Xf[:, 0, :], w1[:, :, CP], dk[:, :, CP], ALU.add)
            vec.tensor_tensor(Xf[:, 1, :], w1[:, :, POS - 1], dk[:, :, POS - 1], ALU.add).then_inc(x_ready, 1)
            dve.wait_ge(f_turned, 1)
            vec.tensor_copy(fin, PS[0:G, 0, 0:2 * P].rearrange("g (s a n) -> g s a n", s=2, a=2)).then_inc(f_copied, 1)
            for c in range(4):
                for h in range(2):
                    m = 2 * c + h
                    dve.wait_ge(g_turned, m + 1)
                    vec.tensor_copy(gT[:, c, :].rearrange("p (c i) -> p i c", i=CH)[:, 4 * h:4 * h + 4, :],
                                    PS[:, 1 + m % 4, 0:4 * C].rearrange("p (i c) -> p i c", i=4)).then_inc(g_copied, 1)
            dve.wait_ge(g_copied, 8)
            for ct in range(4):
                dve.wait_ge(z_sig, ct + 1)
                vec.tensor_tensor(projT[:, ct, :], gT[:, ct, :], sg, ALU.mult).then_inc(z_used, 1)


def stage_attention(nc, A, O, env):
    PS, ident, projT = (env[k] for k in ("PS", "ident", "projT"))
    spare, sem = env["spare"], env["sem"]
    W = 1280
    OFF = [0, 512, 1024, 896]
    v_tok, k_tok = spare(0, P, NT, 512), spare(2560, P, NT, 512)
    kc, vc = spare(5120, P, 2, H, DH), spare(6144, P, 2, H, DH)
    kcT = spare(7168, P, 4, PAST)
    soft = [spare(8192 + 2560 * b, P, W) for b in range(2)]
    wts = [spare(9472 + 2560 * b, P, W) for b in range(2)]
    ntri, nones = spare(13312, P, P), spare(13440, P, P)
    (ld_kc, ld_vc, a_const, tok_turned, tok_copied, kv_sent, kc_turned, kc_copied, z_done, abs_done, exp_done, ln_done, soft_ready,
     soft_masked, cum_done, w_done, w_masked, pv_done, o_copied, a_pool) = (
        sem("at_" + n) for n in ("ld_kc", "ld_vc", "const", "tok_turned", "tok_copied", "kv_sent", "kc_turned", "kc_copied", "z", "abs",
                                 "exp", "ln", "soft", "soft_m", "cum", "w", "w_m", "pv", "o", "pool"))
    zero, y_dram = spare(13568, P, D), env["y_dram"]
    zero_ok, y_zeroed = sem("at_zero_ok"), sem("at_y_zeroed")
    units = H + 1
    NW = LS * H // 2

    def bank(u):
        return 3 * (u % 2)

    def flat(u):
        return PS[:, bank(u):bank(u) + 3, :].rearrange("p b c -> p (b c)")

    def spans(u):
        return [(P, 0, W)] if u < H else [s for b in (0, 512) for s in ((P, b, 2 * NW), (LS, b + 2 * NW, NW))]

    with nc.Block() as block:
        @block.sync
        def _(sp):
            sp.wait_ge(zero_ok, 1)
            for j in range(OVF):
                sp.dma_start(y_dram[P * (E + j):P * (E + j + 1), :], zero).then_inc(y_zeroed, 16)
            sp.dma_start(kc[:, 0], A["cache_k"][0, 0][:, 0:P].rearrange("h p d -> p h d")).then_inc(ld_kc, 16)
            sp.dma_start(kc[:, 1], A["cache_k"][0, 0][:, P:2 * P].rearrange("h p d -> p h d")).then_inc(ld_kc, 16)
            sp.dma_start(vc[:, 0], A["cache_v"][0, 0][:, 0:P].rearrange("h p d -> p h d")).then_inc(ld_vc, 16)
            sp.dma_start(vc[:, 1], A["cache_v"][0, 0][:, P:2 * P].rearrange("h p d -> p h d")).then_inc(ld_vc, 16)
            for m in range(2 * NT):
                ti, src, out = m % NT, (k_tok, v_tok)[m // NT], ("k", "v")[m // NT]
                sp.wait_ge(tok_copied, m + 1)
                if ti < NT - 1:
                    dst = O[out + "_p"][0, 0][:, P * ti:P * (ti + 1)]
                else:
                    dst = O[out + "_s"][0, 0]
                sp.dma_start(dst.rearrange("h p d -> p h d"),
                             src[0:ROWS[ti], ti, :].rearrange("p (h d) -> p h d", h=H)).then_inc(kv_sent, 16)
            sp.wait_ge(kv_sent, 32 * NT)
            sp.wait_ge(y_zeroed, 16 * OVF)

        @block.gpsimd
        def _(pool):
            link = chained(pool, a_pool)
            pool.memset(zero, 0.0).then_inc(zero_ok, 1)
            link(pool.memset(ntri, -1.0))
            pool.affine_select(out=ntri, in_=ntri, compare_op=ALU.is_ge, fill=0.0, base=0,
                               pattern=[[-1, P]], channel_multiplier=1).then_inc(a_const, 1)
            pool.memset(nones, -1.0).then_inc(a_const, 1)

            def mask(t, u, sem):
                if u < H:
                    for a in range(4):
                        v = t[:, OFF[a]:OFF[a] + P]
                        ins = pool.affine_select(out=v, in_=v, compare_op=ALU.is_gt, fill=0.0, base=0,
                                                 pattern=[[1, P]], channel_multiplier=-1)
                else:
                    for b in (0, 512):
                        v = t[0:LS, b + 2 * NW:b + 3 * NW].rearrange("p (h c) -> p h c", c=LS)
                        ins = pool.affine_select(out=v, in_=v, compare_op=ALU.is_gt, fill=0.0, base=0,
                                                 pattern=[[0, H // 2], [1, LS]], channel_multiplier=-1)
                ins.then_inc(sem, 1)

            for u in range(units + 1):
                if u < units:
                    pool.wait_ge(soft_ready, u + 1)
                    mask(soft[u % 2], u, soft_masked)
                if u >= 1:
                    pool.wait_ge(w_done, u)
                    mask(wts[(u - 1) % 2], u - 1, w_masked)

        @block.tensor
        def _(pe):
            mm, tr = nc.tensor.matmul, nc.tensor.transpose
            for m in range(2 * NT):
                ti, c0 = m % NT, (8, 12)[m // NT]
                if m >= 4:
                    pe.wait_ge(tok_copied, m - 3)
                for c in range(4):
                    ins = tr(PS[0:ROWS[ti], m % 4, P * c:P * (c + 1)], projT[:, c0 + c, P * ti:P * ti + ROWS[ti]], ident[:])
                ins.then_inc(tok_turned, 1)
            pe.wait_ge(ld_kc, 32)
            for hp in range(4):
                for t in range(2):
                    ins = tr(PS[:, 4 + hp // 2, PAST * (hp % 2) + P * t:PAST * (hp % 2) + P * (t + 1)],
                             kc[:, t, 2 * hp:2 * hp + 2, :].rearrange("p h d -> p (h d)"), ident[:])
            ins.then_inc(kc_turned, 1)
            pe.wait_ge(tok_copied, 2 * NT)
            pe.wait_ge(kc_copied, 1)
            pe.wait_ge(a_const, 2)

            def scores(u):
                if u >= 2:
                    pe.wait_ge(w_done, u - 1)
                if u < H:
                    o, c = DH * (u % 2), u // 2
                    for a in range(4):
                        ins = mm(flat(u)[:, OFF[a]:OFF[a] + LP - P * a], projT[o:o + DH, 8 + c, P * a:P * (a + 1)],
                                 projT[o:o + DH, 4 + c, P * a:LP], start=(a != 3), stop=True, skip_group_check=True)
                else:
                    for h in range(H):
                        o, c = DH * (h % 2), h // 2
                        qs = projT[o:o + DH, 4 + c, LP:T]
                        col = 512 * (h % 2) + LS * c
                        for t in range(2):
                            mm(flat(u)[:, col + NW * t:col + NW * t + LS], kcT[o:o + DH, c, P * t:P * (t + 1)], qs,
                               start=(h < 2 and t == 0), stop=True, skip_group_check=True)
                        ins = mm(flat(u)[0:LS, col + 2 * NW:col + 2 * NW + LS], projT[o:o + DH, 8 + c, LP:T], qs,
                                 start=False, stop=True, skip_group_check=True)
                ins.then_inc(z_done, 1)

            def later_keys(u):
                pe.wait_ge(soft_masked, u + 1)
                s = soft[u % 2]
                if u < H:
                    for a in range(4):
                        for b in range(a, 4):
                            n = LP - P * b
                            o = OFF[a] + P * (b - a)
                            ins = mm(flat(u)[:, o:o + n], (ntri if a == b else nones), s[:, OFF[b]:OFF[b] + n],
                                     start=False, stop=True, skip_group_check=True)
                else:
                    for b in (0, 512):
                        new = s[0:LS, b + 2 * NW:b + 3 * NW]
                        for t in range(2):
                            o = flat(u)[:, b + NW * t:b + NW * (t + 1)]
                            mm(o, ntri, s[:, b + NW * t:b + NW * (t + 1)], start=False, stop=True, skip_group_check=True)
                            mm(o, nones[0:LS, :], new, start=False, stop=True, skip_group_check=True)
                        mm(flat(u)[:, b:b + NW], nones, s[:, b + NW:b + 2 * NW], start=False, stop=True, skip_group_check=True)
                        ins = mm(flat(u)[0:LS, b + 2 * NW:b + 3 * NW], ntri[0:LS, 0:LS], new, start=False, stop=True, skip_group_check=True)
                ins.then_inc(cum_done, 1)

            def values(u):
                pe.wait_ge(w_masked, u + 1)
                if u >= 2:
                    pe.wait_ge(o_copied, u - 1)
                w = wts[u % 2]
                if u < H:
                    o = DH * (u % 2)
                    for a in range(4):
                        n = LP - P * a
                        ins = mm(PS[o:o + DH, 6 + u % 2, P * a:LP], v_tok[:, a, DH * u:DH * (u + 1)], w[:, OFF[a]:OFF[a] + n],
                                 start=(a == 0), stop=(a == 3), skip_group_check=True)
                else:
                    pe.wait_ge(ld_vc, 32)
                    for h in range(H):
                        o = PS[DH * (h % 2):DH * (h % 2) + DH, 6 + u % 2, LS * (h // 2):LS * (h // 2 + 1)]
                        col = 512 * (h % 2) + LS * (h // 2)
                        for t in range(2):
                            mm(o, vc[:, t, h, :], w[:, col + NW * t:col + NW * t + LS], start=(t == 0), stop=False)
                        ins = mm(o, v_tok[0:LS, NT - 1, DH * h:DH * (h + 1)], w[0:LS, col + 2 * NW:col + 2 * NW + LS],
                                 start=False, stop=True)
                ins.then_inc(pv_done, 1)

            scores(0)
            for u in range(units):
                if u + 1 < units:
                    scores(u + 1)
                later_keys(u)
                if u >= 1:
                    values(u - 1)
            values(units - 1)

        @block.scalar
        def _(act):
            for m in range(2 * NT):
                act.wait_ge(tok_turned, m + 1)
                r, dst = ROWS[m % NT], (k_tok, v_tok)[m // NT]
                nc.scalar.copy(dst[0:r, m % NT, :], PS[0:r, m % 4, :]).then_inc(tok_copied, 1)
            act.wait_ge(kc_turned, 1)
            nc.scalar.copy(kcT.rearrange("p (b h) t -> p b (h t)", b=2), PS[:, 4:6, :]).then_inc(kc_copied, 1)

            def weights(u):
                act.wait_ge(cum_done, u + 1)
                for p, o, n in spans(u):
                    ins = nc.scalar.activation(wts[u % 2][0:p, o:o + n], flat(u)[0:p, o:o + n], ACT.Exp)
                ins.then_inc(w_done, 1)

            for u in range(units):
                act.wait_ge(z_done, u + 1)
                if u >= 2:
                    act.wait_ge(pv_done, u - 1)
                for p, o, n in spans(u):
                    ins = nc.scalar.activation(wts[u % 2][0:p, o:o + n], flat(u)[0:p, o:o + n], ACT.Abs)
                ins.then_inc(abs_done, 1)
                act.wait_ge(abs_done, u + 1)
                for p, o, n in spans(u):
                    ins = nc.scalar.activation(wts[u % 2][0:p, o:o + n], wts[u % 2][0:p, o:o + n], ACT.Exp, scale=-1.0)
                ins.then_inc(exp_done, 1)
                act.wait_ge(exp_done, u + 1)
                for p, o, n in spans(u):
                    ins = nc.scalar.activation(wts[u % 2][0:p, o:o + n], wts[u % 2][0:p, o:o + n], ACT.Ln, bias=1.0)
                ins.then_inc(ln_done, 1)
                if u >= 1:
                    weights(u - 1)
            weights(units - 1)

        @block.vector
        def _(dve):
            vec = nc.vector

            def output(u):
                dve.wait_ge(pv_done, u + 1)
                if u < H:
                    o = DH * (u % 2)
                    vec.tensor_copy(projT[o:o + DH, 4 + u // 2, 0:LP], PS[o:o + DH, 6 + u % 2, :]).then_inc(o_copied, 1)
                else:
                    vec.tensor_copy(projT[:, 4:8, LP:T], PS[:, 6 + u % 2, 0:LS * 4].rearrange("p (c q) -> p c q", c=4)).then_inc(o_copied, 1)

            for u in range(units):
                dve.wait_ge(ln_done, u + 1)
                if u >= 2:
                    dve.wait_ge(cum_done, u - 1)
                for p, o, n in spans(u):
                    ins = vec.scalar_tensor_tensor(out=soft[u % 2][0:p, o:o + n], in0=flat(u)[0:p, o:o + n], scalar=0.0,
                                                   in1=wts[u % 2][0:p, o:o + n], op0=ALU.max, op1=ALU.add)
                ins.then_inc(soft_ready, 1)
                if u >= 1:
                    output(u - 1)
            output(units - 1)


def layer_norm(vec, link, x, stats, mv, std, g, b, std_wait):
    for h in range(2):
        link(vec.bn_stats(stats[:, h, :], x[:, 512 * h:512 * (h + 1)]))
    vec.bn_aggr(mv, stats.rearrange("p a b -> p (a b)")).then_inc(std_wait[0], 1)
    std_wait[1]()
    link(vec.reciprocal(std, std))
    link(vec.tensor_scalar(x, x, mv[:, 0:1], std, ALU.subtract, ALU.mult))
    link(vec.tensor_tensor(x, x, g, ALU.mult))
    link(vec.tensor_tensor(x, x, b, ALU.add))


def moe_chunk(A, e, slot):
    if slot < 8:
        w, c = A["w_gate_up"][0], 512 * (slot // 4) + (FF if slot % 4 >= 2 else 0)
    else:
        w, c = A["w_down"][0], 512 * ((slot - 8) // 2)
    r = 512 * (slot % 2)
    return w[bass.ds(e, 1), r:r + 512, c:c + 512].rearrange("e (k p) c -> p (e k) c", p=P)


def stage_mix(nc, A, env):
    PS, ident, x_tok, one_p, mod, projT = (env[k] for k in ("PS", "ident", "x_tok", "one_p", "mod", "projT"))
    posblk, gates, gate_of, yrow, ovf, sel96, bias3 = (env[k] for k in ("posblk", "gates", "gate_of", "yrow", "ovf", "sel96", "bias3"))
    TB, CA, Dg, ring, ring_full = (env[k] for k in ("TB", "CA", "Dg", "ring", "ring_full"))
    sem, wait_dense, wide, mod_rows, h2_dram = env["sem"], env["wait_dense"], env["wide"], env["mod_rows"], env["h2_dram"]

    def room(t, *shape):
        flat = t[:].rearrange("p " + " ".join("abcd"[:len(t.shape) - 1]) + " -> p (" + " ".join("abcd"[:len(t.shape) - 1]) + ")")
        at = [0]

        def take(parts, *dims):
            n = math.prod(dims)
            v = flat[0:parts, at[0]:at[0] + n]
            at[0] += n
            assert at[0] <= flat.shape[1]
            names = "abcde"[:len(dims)]
            return v if len(dims) == 1 else v.rearrange(f"p ({' '.join(names)}) -> p {' '.join(names)}", **dict(zip(names, dims)))
        return take
    t_ca, t_tb, t_dg = room(CA), room(TB), room(Dg)
    mixT = t_ca(P, KT, T)
    h2 = [t_tb(P, D) for _ in range(2)]
    h2T = [t_tb(P, KT, P) for _ in range(2)]
    sc2, sh2 = t_dg(P, 2, D), t_dg(P, 2, D)
    ln1 = projT[:, 8:12, :].rearrange("p a b -> p (a b)")[:, 0:2 * D].rearrange("p (a b) -> p a b", a=2)
    braw = projT[:, 12:16, :].rearrange("p a b -> p (a b)")[0:3 * E, 0:2 * FF]
    st = ExitStack()
    with st:
        o = (RING - 1 - PRE_RING) * 2048
        spare = env["spare"]
        wr = spare(o, P, KT, E)
        br = spare(o + 256, P, E)
        small = spare(o + 288, P, NT, 16)
        lg = spare(o + 368, P, NT, E)
        top = spare(o + 528, P, NT, 8)
        topi = spare(o + 568, P, NT, 8).bitcast(U32)
        gi = spare(o + 608, P, 2, E).bitcast(I32)
        (m_rows, m_w, mix_done, mix_scaled, mix_turned, m_var, m_std, h2_ready, h2_sent, h2_turned, h2_copied, lg_done, lg_ready,
         m_dve, m_ld_bias, m_pool, h2_sent1) = (
            sem("mx_" + n) for n in ("rows", "w", "done", "scaled", "turned", "var", "std", "h2", "h2_sent", "h2_turned", "h2_copied",
                                     "lg", "lg_ready", "dve", "ld_bias", "pool", "h2_sent1"))
        with nc.Block() as block:
            @block.sync
            def _(sp):
                for s in range(2):
                    sp.dma_start(sc2[:, s, :], mod_rows[s, 4 * D:5 * D].partition_broadcast(P)).then_inc(m_rows, 16)
                    sp.dma_start(sh2[:, s, :], mod_rows[s, 3 * D:4 * D].partition_broadcast(P)).then_inc(m_rows, 16)
                sp.dma_start(ln1[:, 0, :], A["ln1_g"][0].partition_broadcast(P)).then_inc(m_rows, 16)
                sp.dma_start(ln1[:, 1, :], A["ln1_b"][0].partition_broadcast(P)).then_inc(m_rows, 16)
                sp.dma_start(wr, A["w_router"][0].rearrange("(k p) e -> p k e", p=P)).then_inc(m_w, 16)
                sp.dma_start(br, A["b_router"][0].partition_broadcast(P)).then_inc(m_w, 16)
                for k in range(3):
                    sp.dma_start(braw[E * k:E * (k + 1), :], A["b_gate_up"][0]).then_inc(m_ld_bias, 16)
                for slot in range(PRE_RING, RING - 1):
                    sp.dma_start(ring[:, slot, :].rearrange("p (k c) -> p k c", k=4), moe_chunk(A, 0, slot)).then_inc(ring_full[slot], 16)
                for slot in range(PRE_RING):
                    sp.wait_ge(mix_done, 2 * (slot + 1))
                    sp.dma_start(ring[:, slot, :].rearrange("p (k c) -> p k c", k=4), moe_chunk(A, 0, slot)).then_inc(ring_full[slot], 16)
                for ti, r in enumerate(ROWS):
                    sp.wait_ge(h2_ready, ti + 1)
                    sp.dma_start(h2_dram[P * ti:P * ti + r, :], h2[ti % 2][0:r, :]).then_inc((h2_sent, h2_sent1)[ti % 2], 16)
                sp.wait_ge(h2_sent, 16 * ((NT + 1) // 2))
                sp.wait_ge(h2_sent1, 16 * (NT // 2))

            @block.tensor
            def _(pe):
                mm, tr = nc.tensor.matmul, nc.tensor.transpose
                for ct in range(KT):
                    n = N_ADA + N_IN + ct // 2
                    wait_dense(pe, n)
                    b = 2 * (ct % 4)
                    if ct >= 4:
                        pe.wait_ge(mix_scaled, ct - 3)
                    for k in range(KT):
                        for h in range(2):
                            ins = mm(PS[:, b + h, 0:HALF], wide(n)[:, k, P * (ct % 2):P * (ct % 2 + 1)],
                                     projT[:, k, HALF * h:HALF * (h + 1)], start=(k == 0), stop=(k == KT - 1))
                    ins.then_inc(mix_done, 1)
                pe.wait_ge(mix_scaled, KT)

                def turn_mix(ti):
                    r, b = ROWS[ti], 2 * (ti % 2)
                    if ti >= 2:
                        pe.wait_ge(m_var, ti - 1)
                    for k in range(KT):
                        ins = tr(PS[0:r, b + k // 4, P * (k % 4):P * (k % 4 + 1)], mixT[:, k, P * ti:P * ti + r], ident[:])
                    ins.then_inc(mix_turned, 1)

                def route(ti):
                    r, b = ROWS[ti], 4
                    pe.wait_ge(h2_ready, ti + 1)
                    if ti >= 1:
                        pe.wait_ge(h2_copied, ti)
                    for k in range(KT):
                        ins = tr(PS[:, b + k // 4, P * (k % 4):P * (k % 4) + r], h2[ti % 2][0:r, P * k:P * (k + 1)], ident[0:r, 0:r])
                    ins.then_inc(h2_turned, 1)
                    pe.wait_ge(h2_copied, ti + 1)
                    if ti == 0:
                        pe.wait_ge(m_w, 32)
                    if ti >= 2:
                        pe.wait_ge(lg_ready, ti - 1)
                    for k in range(KT):
                        ins = mm(PS[0:r, 6 + ti % 2, 0:E], h2T[ti % 2][:, k, 0:r], wr[:, k, :], start=(k == 0), stop=(k == KT - 1))
                    ins.then_inc(lg_done, 1)

                turn_mix(0)
                for ti in range(NT):
                    if ti + 1 < NT:
                        turn_mix(ti + 1)
                    route(ti)

            @block.scalar
            def _(act):
                for ct in range(KT):
                    act.wait_ge(mix_done, ct + 1)
                    b = 2 * (ct % 4)
                    gp, gs = (mod[:, s, 2 * KT + ct:2 * KT + ct + 1] for s in range(2))
                    nc.scalar.activation(mixT[:, ct, 0:HALF], PS[:, b, 0:HALF], ACT.Copy, scale=gp)
                    nc.scalar.activation(mixT[:, ct, HALF:LP], PS[:, b + 1, 0:LP - HALF], ACT.Copy, scale=gp)
                    nc.scalar.activation(mixT[:, ct, LP:T], PS[:, b + 1, LP - HALF:HALF], ACT.Copy, scale=gs).then_inc(mix_scaled, 1)
                for ti, r in enumerate(ROWS):
                    act.wait_ge(m_var, ti + 1)
                    nc.scalar.activation(small[0:r, ti, 14:15], small[0:r, ti, 13:14], ACT.Sqrt, bias=one_p[0:r, 1:2]).then_inc(m_std, 1)
                    act.wait_ge(h2_turned, ti + 1)
                    if ti >= 2:
                        act.wait_ge(lg_done, ti - 1)
                    for k in range(2):
                        ins = nc.scalar.copy(h2T[ti % 2][:, 4 * k:4 * k + 4, 0:r],
                                             PS[:, 4 + k, :].rearrange("p (a b) -> p a b", a=4)[:, :, 0:r])
                    ins.then_inc(h2_copied, 1)

            @block.vector
            def _(dve):
                link = chained(dve, m_dve)
                vec = nc.vector
                link(vec.memset(lg[:, NT - 1, :], 0.0))
                dve.wait_ge(m_rows, 96)
                for ti, r in enumerate(ROWS):
                    x = x_tok[0:r, ti, :]
                    sq = small[0:r, ti]
                    dve.wait_ge(mix_turned, ti + 1)
                    link(vec.scalar_tensor_tensor(out=x, in0=x, scalar=DN_ALPHA, in1=PS[0:r, 2 * (ti % 2):2 * (ti % 2) + 2, :].rearrange("p a b -> p (a b)"),
                                                  op0=ALU.mult, op1=ALU.add))
                    layer_norm(vec, link, x, sq[:, 0:12].rearrange("p (a b) -> p a b", a=2), sq[:, 12:14], sq[:, 14:15],
                               ln1[0:r, 0, :], ln1[0:r, 1, :], (m_var, lambda: dve.wait_ge(m_std, ti + 1)))
                    if ti >= 2:
                        dve.wait_ge((h2_sent, h2_sent1)[ti % 2], 16 * (ti // 2))
                        dve.wait_ge(h2_turned, ti - 1)
                    s = ti // (NT - 1)
                    y = h2[ti % 2][0:r, :]
                    link(vec.tensor_tensor(y, x, sc2[0:r, s, :], ALU.mult))
                    vec.tensor_tensor(y, y, sh2[0:r, s, :], ALU.add).then_inc(h2_ready, 1)
                    if ti >= 1:
                        dve.wait_ge(lg_done, ti)
                        rr = ROWS[ti - 1]
                        vec.tensor_tensor(lg[0:rr, ti - 1, :], PS[0:rr, 6 + (ti - 1) % 2, 0:E], br[0:rr, :], ALU.add).then_inc(lg_ready, 1)
                dve.wait_ge(lg_done, NT)
                vec.tensor_tensor(lg[0:LS, NT - 1, :], PS[0:LS, 6 + (NT - 1) % 2, 0:E], br[0:LS, :], ALU.add).then_inc(lg_ready, 1)
                dve.wait_ge(lg_ready, NT)
                for ti in range(NT):
                    link(vec.max(top[:, ti, :], lg[:, ti, :]))
                    link(vec.max_index(topi[:, ti, :], top[:, ti, :], lg[:, ti, :]))
                dve.wait_ge(m_ld_bias, 48)
                link(vec.tensor_copy(bias3[:], braw))
                for k in (1, 2):
                    for g in range(k, 3):
                        q = slice(E * g, E * (g + 1))
                        link(vec.tensor_tensor(braw[q, :], braw[q, :], bias3[q, :], ALU.subtract))
                        link(vec.tensor_copy(bias3[q, :], braw[q, :]))

        stage_plan(nc, env, top, topi, gi)


def stage_plan(nc, env, top, topi, gi):
    PS, ident = env["PS"], env["ident"]
    posblk, gates, gate_of, yrow, ovf, sel96 = (env[k] for k in ("posblk", "gates", "gate_of", "yrow", "ovf", "sel96"))
    sem = env["sem"]
    t_tb = env["TB"][:].rearrange("p a b -> p (a b)")
    t_dg = env["Dg"][:].rearrange("p a b -> p (a b)")
    t_ca = env["CA"][:].rearrange("p a b c -> p (a b c)")
    hot = t_tb[:, 0:NT * TOPK * E].rearrange("p (t k e) -> p t k e", t=NT, k=TOPK)
    hot2 = t_tb[:, 1024:1024 + NT * TOPK * E].rearrange("p (t k e) -> p t k e", t=NT, k=TOPK)
    big = t_ca[:, 0:NT * OVF * E].rearrange("p (t j e) -> p t j e", t=NT, j=OVF)
    f = [t_dg[:, NT * E * k:NT * E * (k + 1)].rearrange("p (t e) -> p t e", t=NT) for k in range(8)]
    mask, rank, rb, row, t0, t1 = f[0:6]
    o = 8 * NT * E
    ie, inc, exc, nov, cnt, ones32, c0, c1 = (t_dg[:, o + E * k:o + E * (k + 1)] for k in range(8))
    o += 8 * E
    em, em2, em3 = (t_dg[:, o + OVF * E * k:o + OVF * E * (k + 1)].rearrange("p (j e) -> p j e", j=OVF) for k in range(3))
    o += 3 * OVF * E
    ij, cj, ej = (t_dg[:, o + OVF * k:o + OVF * (k + 1)] for k in range(3))
    o += 3 * OVF
    rep3 = t_dg[:, o:o + 6 * E].rearrange("p (a k e) -> p a k e", a=2, k=3)
    o += 6 * E
    bnd = t_dg[:, o:o + 2]
    su, on = t_tb[:, 2048:2048 + P], t_tb[:, 2048 + P:2048 + 2 * P]
    topf, ex, tot = t_tb[:, 2560:2600].rearrange("p (t k) -> p t k", t=NT), t_tb[:, 2600:2640].rearrange("p (t k) -> p t k", t=NT), t_tb[:, 2640:2645]
    p_pool, p_cst, p_mask, p_rank, p_exp, p_ex, p_bnd, p_bnd2, p_dve, p_iota = (
        sem("pl_" + n) for n in ("pool", "cst", "mask", "rank", "exp", "ex", "bnd", "bnd2", "dve", "iota"))
    with nc.Block() as block:
        @block.gpsimd
        def _(pool):
            link = chained(pool, p_pool)
            pool.iota(gi[:, 0, :], pattern=[[1, E]], base=0, channel_multiplier=0).then_inc(p_iota, 1)
            link(pool.memset(su, 1.0))
            pool.affine_select(out=su, in_=su, compare_op=ALU.is_gt, fill=0.0, base=0,
                               pattern=[[1, P]], channel_multiplier=-1).then_inc(p_cst, 1)
            pool.memset(on, 1.0).then_inc(p_cst, 1)

        @block.scalar
        def _(act):
            act.wait_ge(p_exp, 1)
            nc.scalar.activation(ex[:, :, 0:TOPK], ex[:, :, 0:TOPK], ACT.Exp).then_inc(p_ex, 1)

        @block.tensor
        def _(pe):
            pe.wait_ge(p_cst, 2)
            pe.wait_ge(p_mask, 1)
            for ti in range(NT):
                for tj in range(ti + 1):
                    nc.tensor.matmul(PS[:, 0, E * ti:E * (ti + 1)], su if tj == ti else on, mask[:, tj, :],
                                     start=(tj == 0), stop=(tj == ti))
            for tj in range(NT):
                ins = nc.tensor.matmul(PS[:, 0, E * NT:E * (NT + 1)], on, mask[:, tj, :], start=(tj == 0), stop=(tj == NT - 1))
            ins.then_inc(p_rank, 1)
            pe.wait_ge(p_bnd, 1)
            for k in range(2):
                ins = nc.tensor.transpose(PS[0:3 * E, 1, P * k:P * (k + 1)], rep3[:, k].rearrange("p k e -> p (k e)"), ident[:])
            ins.then_inc(p_bnd2, 1)

        @block.vector
        def _(dve):
            link = chained(dve, p_dve)
            vec = nc.vector

            def tt(out, a, b, op):
                link(vec.tensor_tensor(out, a, b, op))

            def over_tokens(v):
                return v.unsqueeze(1).to_broadcast((P, NT, E))

            tt(ex[:, :, 0:TOPK], top[:, :, 0:TOPK], top[:, :, 0:1].to_broadcast((P, NT, TOPK)), ALU.subtract)
            dve.sem_inc(p_exp, 1)
            link(vec.tensor_copy(topf, topi[:]))
            dve.wait_ge(p_iota, 1)
            link(vec.tensor_copy(ie, gi[:, 0, :]))
            tt(hot, ie.unsqueeze(1).unsqueeze(1).to_broadcast((P, NT, TOPK, E)),
               topf[:, :, 0:TOPK].unsqueeze(3).to_broadcast((P, NT, TOPK, E)), ALU.is_equal)
            link(vec.memset(mask[:, NT - 1, :], 0.0))
            link(vec.tensor_reduce(mask[:, 0:NT - 1, :], hot[:, 0:NT - 1].rearrange("p t k e -> p t e k"), AX.X, ALU.add))
            vec.tensor_reduce(mask[0:LS, NT - 1, :], hot[0:LS, NT - 1].rearrange("p k e -> p e k"), AX.X, ALU.add).then_inc(p_mask, 1)
            dve.wait_ge(p_ex, 1)
            link(vec.tensor_reduce(tot, ex[:, :, 0:TOPK], AX.X, ALU.add))
            link(vec.reciprocal(tot, tot))
            tt(gates[:], ex[:, :, 0:TOPK], tot.unsqueeze(2).to_broadcast((P, NT, TOPK)), ALU.mult)
            tt(hot2, hot, gates[:].unsqueeze(3).to_broadcast((P, NT, TOPK, E)), ALU.mult)
            link(vec.tensor_reduce(gate_of[:], hot2.rearrange("p t k e -> p t e k"), AX.X, ALU.add))
            dve.wait_ge(p_rank, 1)
            link(vec.tensor_copy(rank, PS[:, 0, 0:NT * E].rearrange("p (t e) -> p t e", t=NT)))
            link(vec.tensor_copy(cnt, PS[:, 0, NT * E:(NT + 1) * E]))
            link(vec.scalar_tensor_tensor(out=t0, in0=rank, scalar=1.0, in1=mask, op0=ALU.add, op1=ALU.mult))
            link(vec.tensor_scalar(posblk[:, :, 0:E], t0, -1.0, None, ALU.add))
            link(vec.tensor_scalar(rb, rank, float(P), None, ALU.is_ge))
            link(vec.tensor_scalar(nov, cnt, float(P), None, ALU.is_gt))
            for b in range(2, NT):
                link(vec.scalar_tensor_tensor(out=rb, in0=rank, scalar=float(P * b), in1=rb, op0=ALU.is_ge, op1=ALU.add))
                link(vec.scalar_tensor_tensor(out=nov, in0=cnt, scalar=float(P * b), in1=nov, op0=ALU.is_gt, op1=ALU.add))
            link(vec.memset(ones32, 1.0))
            link(vec.tensor_tensor_scan(inc, ones32, nov, 0.0, ALU.mult, ALU.add))
            tt(exc, inc, nov, ALU.subtract)
            link(vec.tensor_copy(rep3[:, 0], exc.unsqueeze(1).to_broadcast((P, 3, E))))
            vec.tensor_copy(rep3[:, 1], inc.unsqueeze(1).to_broadcast((P, 3, E))).then_inc(p_bnd, 1)
            tt(c0, exc, ie, ALU.subtract)
            link(vec.tensor_scalar(c0, c0, float(E - 1), None, ALU.add))
            tt(t0, rb, over_tokens(c0), ALU.add)
            link(vec.scalar_tensor_tensor(out=t0, in0=rb, scalar=0.0, in1=t0, op0=ALU.is_gt, op1=ALU.mult))
            tt(t0, t0, over_tokens(ie), ALU.add)
            tt(t0, t0, rb, ALU.subtract)
            link(vec.scalar_tensor_tensor(out=row, in0=t0, scalar=float(P), in1=rank, op0=ALU.mult, op1=ALU.add))
            tt(hot2, hot, row.unsqueeze(2).to_broadcast((P, NT, TOPK, E)), ALU.mult)
            link(vec.tensor_reduce(t1[:, :, 0:TOPK], hot2, AX.X, ALU.add))
            link(vec.tensor_copy(yrow[:], t1[:, :, 0:TOPK]))
            link(vec.tensor_copy(ij, ie[:, 0:OVF]))
            bj = ij.unsqueeze(2).to_broadcast((P, OVF, E))

            def over_j(v):
                return v.unsqueeze(1).to_broadcast((P, OVF, E))
            tt(em, over_j(exc), bj, ALU.is_le)
            tt(em2, over_j(inc), bj, ALU.is_gt)
            tt(em, em, em2, ALU.mult)
            tt(em2, em, over_j(ie), ALU.mult)
            link(vec.tensor_reduce(ej, em2, AX.X, ALU.add))
            link(vec.tensor_copy(ovf[:, 1:1 + OVF], ej))
            link(vec.tensor_copy(ovf[:, 0:1], inc[:, E - 1:E]))
            link(vec.tensor_scalar(em3, over_j(exc), float(P), 1.0 - P, ALU.mult, ALU.add))
            link(vec.scalar_tensor_tensor(out=em3, in0=bj, scalar=-float(P), in1=em3, op0=ALU.mult, op1=ALU.add))
            tt(em3, em, em3, ALU.mult)
            link(vec.tensor_reduce(cj, em3, AX.X, ALU.add))
            for ti in range(NT):
                tt(big[:, ti], em, posblk[:, ti, 0:E].unsqueeze(1).to_broadcast((P, OVF, E)), ALU.mult)
            link(vec.tensor_reduce(posblk[:, :, E:NB], big, AX.X, ALU.add))
            link(vec.scalar_tensor_tensor(out=posblk[:, :, E:NB], in0=posblk[:, :, E:NB], scalar=-1.0,
                                          in1=cj.unsqueeze(1).to_broadcast((P, NT, OVF)), op0=ALU.add, op1=ALU.add))
            for k in range(3):
                link(vec.tensor_copy(sel96[E * k:E * (k + 1), 0:E], ident[E * k:E * (k + 1), E * k:E * (k + 1)]))
            dve.wait_ge(p_bnd2, 1)
            link(vec.tensor_copy(bnd[0:3 * E], PS[0:3 * E, 1, 0:P + 1:P]))
            sj = sel96[:, E:NB]
            link(vec.tensor_scalar(sj, ij[0:3 * E], bnd[0:3 * E, 0:1], None, ALU.is_ge))
            link(vec.scalar_tensor_tensor(out=sj, in0=ij[0:3 * E], scalar=bnd[0:3 * E, 1:2], in1=sj, op0=ALU.is_lt, op1=ALU.mult))


def stage_moe(nc, A, env):
    PS, ident, ring, ring_full = (env[k] for k in ("PS", "ident", "ring", "ring_full"))
    posblk, ovf, sel96, bias3 = (env[k] for k in ("posblk", "ovf", "sel96", "bias3"))
    h2_dram, y_dram, sem = env["h2_dram"], env["y_dram"], env["sem"]
    st = ExitStack()
    with st:
        def sb(name, shape, dt=F32):
            return st.enter_context(nc.sbuf_tensor(name, shape, dt))
        slots = sb("slots", [P, P])
        tok2 = sb("tok2", [P, NT, 2], BF16)
        it = sb("moe_iota", [P, P + NT * 2], I32)
        pick = sb("pick", [P, 2, NT, P], BF16)
        hotb = sb("hotb", [3 * E, 2, P], BF16)
        rowi = sb("rowi", [P, 2], U32)
        X = sb("X", [P, 2, D])
        XT = sb("XT", [P, 2, KT, P])
        g_, u_, s_ = (sb(n, [P, 512]) for n in ("g_", "u_", "s_"))
        h_ = sb("h_", [P, 2, 512])
        hT = sb("hT_", [P, KT, P])
        y_ = sb("y_", [P, 2, D])
        (iota_ok, cst_ok, hot_ok, pick_ok, num_ok, idx_ok, x_full0, x_full1, xt_done, xt_ok, g_ok, u_ok, s_ok, m_ok, hA, hB,
         hAt, hBt, hAc, hBc, y_ok, y_sent0, y_sent1, used_a, used_b, used_d) = (
            sem("e_" + n) for n in ("iota", "cst", "hot", "pick", "num", "idx", "x_full0", "x_full1", "xt", "xt_ok", "g", "u", "s", "m",
                                    "hA", "hB", "hAt", "hBt", "hAc", "hBc", "y", "y_sent0", "y_sent1", "used_a", "used_b", "used_d"))
        x_full, y_sent = (x_full0, x_full1), (y_sent0, y_sent1)

        def blocks(eng, first, last, head, body):
            head(first)
            if first == 0:
                body(0, 0, 2)
                body(1, 1, 2)
                first = 2
            with eng.Fori(0, (last - first) // 2) as n:
                for q in range(2):
                    body(n * 2 + (first + q), q, 2)
            body(last - 1, 0, 1)
            body(last, 1, 0)

        def all_blocks(eng, head, body):
            blocks(eng, 0, E - 1, head, body)
            n = eng.value_load(ovf[0:1, 0:1], min_val=0, max_val=OVF)
            with eng.If(n > 0):
                blocks(eng, E, NB - 1, head, body)

        def at_least(eng, sem, value):
            if not isinstance(value, int) or value > 0:
                eng.wait_ge(sem, value)

        def weights(slot):
            return ring[:, slot, :].rearrange("p (k c) -> p k c", k=4)

        with nc.Block() as block:
            @block.sync
            def _(sp):
                def load(e, i, first, used):
                    for slot in range(first, first + 4):
                        sp.wait_ge(used, i * 4 + (slot - first - 3))
                        sp.dma_start(weights(slot), moe_chunk(A, e, slot)).then_inc(ring_full[slot], 16)

                sp.dma_start(weights(RING - 1), moe_chunk(A, 0, RING - 1)).then_inc(ring_full[RING - 1], 16)
                load(1, 1, 0, used_a)
                with sp.Fori(0, E - 2) as n:
                    load(n + 1, n + 1, 4, used_b)
                    load(n + 2, n + 2, 0, used_a)
                    load(n + 1, n + 1, 8, used_d)
                load(E - 1, E - 1, 4, used_b)
                load(E - 1, E - 1, 8, used_d)
                n = sp.value_load(ovf[0:1, 0:1], min_val=0, max_val=OVF)
                with sp.If(n > 0):
                    with sp.Fori(0, OVF) as j:
                        e = sp.value_load(ovf[0:1, bass.ds(j + 1, 1)], min_val=0, max_val=E - 1)
                        load(e, j + E, 0, used_a)
                        load(e, j + E, 4, used_b)
                        load(e, j + E, 8, used_d)

            @block.gpsimd
            def _(pool):
                pool.iota(it[:, 0:P], pattern=[[1, P]], base=0, channel_multiplier=0).then_inc(iota_ok, 1)
                v = it[:, P:P + 2 * NT].rearrange("p (t a) -> p t a", a=2)
                pool.iota(v[:, :, 0:1], pattern=[[P, NT], [1, 1]], base=0, channel_multiplier=0).then_inc(iota_ok, 1)
                pool.iota(v[:, :, 1:2], pattern=[[0, NT], [1, 1]], base=0, channel_multiplier=1).then_inc(iota_ok, 1)

                def gather(i, q, reused):
                    pool.wait_ge(idx_ok, i + 1)
                    if reused:
                        pool.wait_ge(xt_done, i * 2 - 2)
                    pool.nop(nofuse=True)
                    pool.indirect_dma_start(out=X[:, q, :], out_offset=None, in_=h2_dram,
                                            in_offset=bass.IndirectOffsetOnAxis(ap=rowi[:, q:q + 1], axis=0)).then_inc(x_full[q], 16)

                def head(first):
                    gather(first, 0, first > 0)
                    gather(first + 1, 1, first > 0)

                def body(i, q, later):
                    if later == 2:
                        gather(i + 2, q, True)
                all_blocks(pool, head, body)

            @block.tensor
            def _(pe):
                mm, tr = nc.tensor.matmul, nc.tensor.transpose

                def number(i, q):
                    pe.wait_ge(pick_ok, i + 1)
                    for ti in range(NT):
                        ins = mm(PS[:, 6, 0:2], pick[:, q, ti, :], tok2[:, ti, :], start=(ti == 0), stop=(ti == NT - 1))
                    ins.then_inc(num_ok, 1)

                def turn_x(i, q):
                    pe.wait_ge(x_full[q], (i - q) * 8 + 16)
                    pe.wait_ge(idx_ok, i + 1)
                    at_least(pe, hBc, i - 1)
                    for k in range(KT):
                        ins = tr(PS[:, 6 + k // 4, P * (k % 4):P * (k % 4 + 1)], X[:, q, P * k:P * (k + 1)], ident[:])
                        if k % 4 == 3:
                            ins.then_inc(xt_done, 1)

                def turn_h(i, half, ready, done):
                    pe.wait_ge(ready, i + 1)
                    for k in range(4):
                        ins = tr(PS[:, 6 + half, P * k:P * (k + 1)], h_[:, half, P * k:P * (k + 1)], ident[:])
                    ins.then_inc(done, 1)

                def up(i, q, half, p, used):
                    o, slot = PS[:, 2 * half + p, :], 4 * half + 2 * p
                    mm(o, hotb[:, q, :], bias3[:, FF * p + 512 * half:FF * p + 512 * half + 512], start=True, stop=False)
                    for k in range(KT):
                        s = slot + k // 4
                        if k % 4 == 0:
                            pe.wait_ge(ring_full[s], i * 16 + 16 * (1 + (PRE // PRE_RING if s < PRE_RING else 0)))
                        ins = mm(o, XT[:, q, k, :], weights(s)[:, k % 4, :], start=False, stop=(k == KT - 1))
                        if k % 4 == 3:
                            ins.then_inc(used, 1)

                def first_half(i, q, between):
                    pe.wait_ge(xt_ok, i * 2 + 2)
                    pe.wait_ge(hot_ok, i + 1)
                    at_least(pe, hA, i)
                    up(i, q, 0, 0, used_a)
                    between()
                    up(i, q, 0, 1, used_a)

                def down(i):
                    pe.wait_ge(hAc, i + 1)
                    pe.wait_ge(hBc, i + 1)
                    at_least(pe, y_ok, i * 2)
                    for half in range(2):
                        for k in range(KT):
                            s = 8 + 2 * half + k // 4
                            if k % 4 == 0:
                                pe.wait_ge(ring_full[s], i * 16 + 16)
                            ins = mm(PS[:, 4 + half, :], hT[:, k, :], weights(s)[:, k % 4, :], start=(k == 0), stop=(k == KT - 1))
                            if k % 4 == 3:
                                ins.then_inc(used_d, 1)

                def head(first):
                    number(first, 0)
                    pe.wait_ge(idx_ok, first + 1)
                    number(first + 1, 1)
                    pe.wait_ge(idx_ok, first + 2)
                    turn_x(first, 0)
                    first_half(first, 0, lambda: None)

                def body(i, q, later):
                    if later:
                        turn_x(i + 1, 1 - q)
                        pe.wait_ge(xt_ok, i * 2 + 3)
                    turn_h(i, 0, hA, hAt)
                    at_least(pe, hB, i)
                    up(i, q, 1, 0, used_b)
                    up(i, q, 1, 1, used_b)
                    if later == 2:
                        pe.wait_ge(hAc, i + 1)
                        number(i + 2, q)

                    def second_h():
                        if later:
                            pe.wait_ge(xt_ok, i * 2 + 4)
                        turn_h(i, 1, hB, hBt)
                    if later:
                        first_half(i + 1, 1 - q, second_h)
                    else:
                        second_h()
                    down(i)

                pe.wait_ge(cst_ok, 2)
                all_blocks(pe, head, body)

            @block.scalar
            def _(act):
                def xt(i, q):
                    for k in range(2):
                        act.wait_ge(xt_done, i * 2 + (k + 1))
                        nc.scalar.copy(XT[:, q, 4 * k:4 * k + 4, :], PS[:, 6 + k, :].rearrange("p (a b) -> p a b", a=4)).then_inc(xt_ok, 1)

                def ht(i, half, turned, done):
                    act.wait_ge(turned, i + 1)
                    at_least(act, used_d, i * 4)
                    nc.scalar.copy(hT[:, 4 * half:4 * half + 4, :], PS[:, 6 + half, :].rearrange("p (a b) -> p a b", a=4)).then_inc(done, 1)

                def sigmoid(n):
                    act.wait_ge(g_ok, n + 1)
                    nc.scalar.activation(s_[:], g_[:], ACT.Sigmoid, scale=SW_ALPHA).then_inc(s_ok, 1)

                def y(i, q):
                    at_least(act, y_sent[q], (i - q) * 8)
                    for half in range(2):
                        act.wait_ge(used_d, i * 4 + 2 * (half + 1))
                        nc.scalar.copy(y_[:, q, 512 * half:512 * (half + 1)], PS[:, 4 + half, :]).then_inc(y_ok, 1)
                    act.wait_ge(y_ok, i * 2 + 2)
                    act.dma_start(y_dram[bass.ts(i, P), :], y_[:, q, :]).then_inc(y_sent[q], 16)

                def head(first):
                    xt(first, 0)
                    sigmoid(2 * first)

                def body(i, q, later):
                    if later:
                        xt(i + 1, 1 - q)
                    ht(i, 0, hAt, hAc)
                    sigmoid(i * 2 + 1)
                    ht(i, 1, hBt, hBc)
                    if later:
                        sigmoid(i * 2 + 2)
                    y(i, q)
                    if later == 0:
                        for s in y_sent:
                            act.wait_ge(s, 8 * (i + 1))
                all_blocks(act, head, body)

            @block.vector
            def _(dve):
                vec = nc.vector

                def hot(i, q):
                    vec.tensor_copy(hotb[:, q, :], sel96[:, bass.ds(i, 1)].to_broadcast((3 * E, P))).then_inc(hot_ok, 1)

                def choose(i, q):
                    for ti in range(NT):
                        ins = vec.tensor_scalar(pick[:, q, ti, :], slots[:], posblk[:, ti, bass.ds(i, 1)], None, ALU.is_equal)
                    ins.then_inc(pick_ok, 1)

                def index(i, q):
                    dve.wait_ge(num_ok, i + 1)
                    with nc.allow_low_precision(reason="a sum of two whole numbers below 2^24, exact as an integer"):
                        vec.tensor_reduce(rowi[:, q:q + 1], PS[:, 6, 0:2], AX.X, ALU.add).then_inc(idx_ok, 1)

                def swiglu(n, half, gate_done, up_done, h_free, done):
                    gate_done()
                    vec.tensor_scalar(g_[:], PS[:, 2 * half, :], LIMIT, None, ALU.min).then_inc(g_ok, 1)
                    up_done()
                    vec.tensor_scalar(u_[:], PS[:, 2 * half + 1, :], -LIMIT, LIMIT, ALU.max, ALU.min).then_inc(u_ok, 1)
                    dve.wait_ge(u_ok, n + 1)
                    vec.scalar_tensor_tensor(out=u_[:], in0=u_[:], scalar=1.0, in1=g_[:], op0=ALU.add, op1=ALU.mult).then_inc(m_ok, 1)
                    dve.wait_ge(m_ok, n + 1)
                    dve.wait_ge(s_ok, n + 1)
                    h_free()
                    vec.tensor_tensor(h_[:, half, :], u_[:], s_[:], ALU.mult).then_inc(done, 1)

                def half_a(i):
                    swiglu(i * 2, 0, lambda: dve.wait_ge(used_a, i * 4 + 2), lambda: dve.wait_ge(used_a, i * 4 + 4),
                           lambda: at_least(dve, hAt, i), hA)

                def half_b(i):
                    swiglu(i * 2 + 1, 1, lambda: dve.wait_ge(used_b, i * 4 + 2), lambda: dve.wait_ge(used_b, i * 4 + 4),
                           lambda: at_least(dve, hBt, i), hB)

                def head(first):
                    if first:
                        dve.wait_ge(used_b, 4 * first)
                        dve.wait_ge(x_full[1], 8 * first)
                        dve.wait_ge(x_full[0], 8 * first)
                    hot(first, 0)
                    choose(first, 0)
                    choose(first + 1, 1)
                    index(first, 0)
                    index(first + 1, 1)
                    half_a(first)

                def body(i, q, later):
                    if later:
                        at_least(dve, used_b, i * 4)
                        hot(i + 1, 1 - q)
                    if later == 2:
                        choose(i + 2, q)
                    half_b(i)
                    if later == 2:
                        dve.wait_ge(x_full[q], (i - q) * 8 + 16)
                        index(i + 2, q)
                    if later:
                        half_a(i + 1)

                dve.wait_ge(iota_ok, 3)
                vec.tensor_copy(slots[:], it[:, 0:P]).then_inc(cst_ok, 1)
                vec.tensor_copy(tok2[:].rearrange("p t a -> p (t a)"), it[:, P:P + 2 * NT]).then_inc(cst_ok, 1)
                dve.wait_ge(cst_ok, 2)
                all_blocks(dve, head, body)


def stage_output(nc, A, O, env):
    PS, ident, x_tok, one_p = (env[k] for k in ("PS", "ident", "x_tok", "one_p"))
    gates, gate_of, yrow, y_dram, mod_rows, sem = (env[k] for k in ("gates", "gate_of", "yrow", "y_dram", "mod_rows", "sem"))
    st = ExitStack()
    with st:
        def sb(name, shape, dt=F32):
            return st.enter_context(nc.sbuf_tensor(name, shape, dt))
        bd = sb("bd", [E, D])
        gT = sb("gT_", [E, NT, P])
        diag = sb("diag", [P, 2, TOPK, P])
        Y = sb("Y", [P, 2, TOPK, D])
        ln2 = sb("ln2", [P, 2, D])
        g2 = sb("g2", [P, 2, D])
        gated = sb("gated", [P, D])
        small = sb("out_small", [P, NT, 16])
        (o_rows, o_bd, o_y0, o_y1, o_gt, o_gtc, o_diag, o_sum, o_gated, o_var, o_std, o_x, o_sent, o_dve) = (
            sem("o_" + n) for n in ("rows", "bd", "y0", "y1", "gt", "gtc", "diag", "sum", "gated", "var", "std", "x", "sent", "dve"))
        o_y = (o_y0, o_y1)
        with nc.Block() as block:
            @block.gpsimd
            def _(pool):
                for ti, r in enumerate(ROWS):
                    if ti >= 2:
                        pool.wait_ge(o_sum, ti - 1)
                    for k in range(TOPK):
                        pool.indirect_dma_start(out=Y[0:r, ti % 2, k, :], out_offset=None, in_=y_dram,
                                                in_offset=bass.IndirectOffsetOnAxis(ap=yrow[0:r, ti, k:k + 1], axis=0)).then_inc(o_y[ti % 2], 16)

            @block.sync
            def _(sp):
                sp.dma_start(bd[:], A["b_down"][0]).then_inc(o_bd, 16)
                sp.dma_start(ln2[:, 0, :], A["ln2_g"][0].partition_broadcast(P)).then_inc(o_rows, 16)
                sp.dma_start(ln2[:, 1, :], A["ln2_b"][0].partition_broadcast(P)).then_inc(o_rows, 16)
                for s in range(2):
                    sp.dma_start(g2[:, s, :], mod_rows[s, 5 * D:6 * D].partition_broadcast(P)).then_inc(o_rows, 16)
                for ti, r in enumerate(ROWS):
                    sp.wait_ge(o_x, ti + 1)
                    dst = O["y_p"][0][P * ti:P * (ti + 1)] if ti < NT - 1 else O["y_s"][0]
                    sp.dma_start(dst, x_tok[0:r, ti, :]).then_inc(o_sent, 16)
                sp.wait_ge(o_sent, 16 * NT)

            @block.tensor
            def _(pe):
                mm = nc.tensor.matmul
                for ti, r in enumerate(ROWS):
                    ins = nc.tensor.transpose(PS[0:E, 4 + ti // 4, P * (ti % 4):P * (ti % 4) + r], gate_of[0:r, ti, :], ident[0:r, 0:r])
                ins.then_inc(o_gt, 1)
                pe.wait_ge(o_gtc, 2)
                pe.wait_ge(o_bd, 16)
                for ti, r in enumerate(ROWS):
                    b = 2 * (ti % 2)
                    if ti >= 2:
                        pe.wait_ge(o_gated, ti - 1)
                    for h in range(2):
                        mm(PS[0:r, b + h, :], gT[:, ti, 0:r], bd[:, 512 * h:512 * (h + 1)], start=True, stop=False)
                    pe.wait_ge(o_diag, ti + 1)
                    pe.wait_ge(o_y[ti % 2], 64 * (ti // 2 + 1))
                    for k in range(TOPK):
                        for h in range(2):
                            ins = mm(PS[0:r, b + h, :], diag[0:r, ti % 2, k, 0:r], Y[0:r, ti % 2, k, 512 * h:512 * (h + 1)],
                                     start=False, stop=(k == TOPK - 1))
                    ins.then_inc(o_sum, 1)

            @block.scalar
            def _(act):
                for ti, r in enumerate(ROWS):
                    act.wait_ge(o_var, ti + 1)
                    nc.scalar.activation(small[0:r, ti, 14:15], small[0:r, ti, 13:14], ACT.Sqrt, bias=one_p[0:r, 1:2]).then_inc(o_std, 1)

            @block.vector
            def _(dve):
                link = chained(dve, o_dve)
                vec = nc.vector
                dve.wait_ge(o_gt, 1)
                vec.tensor_copy(gT[:, 0:NT - 1, :], PS[0:E, 4, :].rearrange("e (t p) -> e t p", t=NT - 1)).then_inc(o_gtc, 1)
                vec.tensor_copy(gT[:, NT - 1, 0:LS], PS[0:E, 5, 0:LS]).then_inc(o_gtc, 1)

                def diagonals(ti):
                    r = ROWS[ti]
                    if ti >= 2:
                        dve.wait_ge(o_sum, ti - 1)
                    for k in range(TOPK):
                        ins = vec.tensor_scalar(diag[0:r, ti % 2, k, 0:r], ident[0:r, 0:r], gates[0:r, ti, k:k + 1], None, ALU.mult)
                    ins.then_inc(o_diag, 1)
                diagonals(0)
                dve.wait_ge(o_rows, 64)
                for ti, r in enumerate(ROWS):
                    if ti + 1 < NT:
                        diagonals(ti + 1)
                    s, b = ti // (NT - 1), 2 * (ti % 2)
                    x, sq = x_tok[0:r, ti, :], small[0:r, ti]
                    dve.wait_ge(o_sum, ti + 1)
                    t = gated[0:r, :]
                    vec.tensor_tensor(t, PS[0:r, b:b + 2, :].rearrange("p a b -> p (a b)"), g2[0:r, s, :], ALU.mult).then_inc(o_gated, 1)
                    dve.wait_ge(o_gated, ti + 1)
                    link(vec.scalar_tensor_tensor(out=x, in0=x, scalar=DN_ALPHA, in1=t, op0=ALU.mult, op1=ALU.add))
                    layer_norm(vec, link, x, sq[:, 0:12].rearrange("p (a b) -> p a b", a=2), sq[:, 12:14], sq[:, 14:15],
                               ln2[0:r, 0, :], ln2[0:r, 1, :], (o_var, lambda: dve.wait_ge(o_std, ti + 1)))
                    dve.sem_inc(o_x, 1)


_INS = ['x_prompt', 'x_sample', 'cache_k', 'cache_v', 'state_s5_re', 'state_s5_im', 'c_prompt', 'c_sample',
        'ln_in_g', 'ln_in_b', 'w_ada', 'b_ada', 'w_in', 's5_a_re', 's5_a_im', 's5_log_dt', 's5_b_re', 's5_b_im',
        's5_c_re', 's5_c_im', 's5_d', 's5_w_glu', 's5_b_glu', 'w_out', 'ln1_g', 'ln1_b', 'w_router', 'b_router',
        'w_gate_up', 'b_gate_up', 'w_down', 'b_down', 'ln2_g', 'ln2_b']
_OUTS = [('y_p', (1, LP, D)), ('y_s', (1, LS, D)), ('k_p', (1, 1, H, LP, DH)), ('v_p', (1, 1, H, LP, DH)),
         ('s5_re_p', (1, 1, G, NS)), ('s5_im_p', (1, 1, G, NS)), ('k_s', (1, 1, H, LS, DH)), ('v_s', (1, 1, H, LS, DH)),
         ('s5_re_s', (1, 1, G, NS)), ('s5_im_s', (1, 1, G, NS))]


def kernel(**inputs):
    import numpy as _np
    import concourse.bacc as _bacc
    from concourse import mybir as _mybir
    from concourse.bass_utils import run_bass_kernel_spmd as _run

    nc = _bacc.Bacc("TRN2", target_bir_lowering=False, num_devices=1)
    arrays, ins, outs = {}, {}, {}
    for name in _INS:
        a = _np.ascontiguousarray(inputs[name])
        arrays[f"in_{name}_dram"] = a
        ins[name] = nc.dram_tensor(f"in_{name}_dram", a.shape, _mybir.dt.from_np(a.dtype), kind="ExternalInput").ap()
    for name, shape in _OUTS:
        outs[name] = nc.dram_tensor(f"out_{name}_dram", shape, F32, kind="ExternalOutput").ap()
    build(nc, ins, outs)
    r = _run(nc, [arrays], core_ids=[0])
    return tuple(r.results[0][f"out_{name}_dram"] for name, _ in _OUTS)
```

```python
import math
from contextlib import ExitStack

import concourse.bass as bass
from concourse import mybir

F32 = mybir.dt.float32
BF16 = mybir.dt.bfloat16
F32R = mybir.dt.float32r
I32 = mybir.dt.int32
U32 = mybir.dt.uint32
ALU = mybir.AluOpType
ACT = mybir.ActivationFunctionType
AX = mybir.AxisListType

P = 128
D = 1024
KT = D // P
LP, LS, PAST = 512, 32, 256
T = LP + LS
HALF = T // 2
NT = LP // P + 1
ROWS = [P] * (NT - 1) + [LS]
H, DH = 8, 64
G, NC, NS = 32, 16, 64
CH = 8
CP, CS = LP // CH, LS // CH
C = CP + CS
POS = CP + 1 + CS + 1
S5W = G * NC
E, TOPK = 32, 4
FF = D
EPS = 1e-5
DN_ALPHA = 2 ** 0.25
LIMIT, SW_ALPHA = 7.0, 1.702
CW = 256
PRE_RING = 4
RING = 6
LENT = 16384
N_ADA, N_IN, N_OUT = 6 * D // CW, 2 * D // CW, D // CW
PRE = N_ADA + N_IN + N_OUT
OVF = 16
NB = E + OVF
assert PRE % PRE_RING == 0 and N_OUT == PRE_RING


def chained(eng, sem):
    n = [0]

    def link(ins):
        n[0] += 1
        ins.then_inc(sem, 1)
        eng.wait_ge(sem, n[0])
    return link


def build(nc, A, O):
    top = ExitStack()
    with top:
        stage_sems = []

        def sem(name, lasting=False):
            s = nc.alloc_semaphore(name=name)
            if not lasting:
                stage_sems.append(s)
            return s

        def end_stage():
            nc.clear_and_free_semaphores(stage_sems)
            stage_sems.clear()
            nc.all_engine_barrier()

        def keep(name, shape, dt=F32):
            return top.enter_context(nc.sbuf_tensor(name, shape, dt))

        def scratch(name, shape, dt=F32):
            return nc.dram_tensor(name, shape, dt, kind="Internal").ap()

        PS = top.enter_context(nc.psum_tensor("PS", [P, 8, 512], F32))
        ring = keep("ring", [P, PRE_RING, 2048])
        ring_full = [sem(f"ring_full{s}", True) for s in range(RING)]
        ident = keep("ident", [P, P])
        x_tok = keep("x_tok", [P, NT, D])
        one_p = keep("one_p", [P, 2])
        posblk = keep("posblk", [P, NT, NB])
        gates = keep("gates", [P, NT, TOPK])
        gate_of = keep("gate_of", [P, NT, E])
        yrow = keep("yrow", [P, NT, TOPK], U32)
        ovf = keep("ovf", [P, 1 + OVF], I32)
        sel96 = keep("sel96", [3 * E, NB])
        bias3 = keep("bias3", [3 * E, 2 * FF], BF16)
        mod_raw = scratch("mod_raw", (2, 6 * D))
        mod_rows = scratch("mod_rows", (2, 6 * D))
        h2_dram = scratch("h2_dram", (T, D))
        y_dram = scratch("y_dram", (NB * P, D))

        def spare(offset, parts, *dims):
            size = math.prod(dims)
            assert offset + size <= LENT
            v = room[0:parts, offset:offset + size]
            names = "abcde"[:len(dims)]
            if len(dims) == 1:
                return v
            return v.rearrange(f"p ({' '.join(names)}) -> p {' '.join(names)}", **dict(zip(names, dims)))

        def wide(n):
            return ring[:, n % PRE_RING, :].rearrange("p (k c) -> p k c", k=KT)

        def dense_source(n):
            for w, first, count in ((A["w_ada"], 0, N_ADA), (A["w_in"], N_ADA, N_IN), (A["w_out"], N_ADA + N_IN, N_OUT)):
                if n < first + count:
                    c = n - first
                    return w[0, :, c * CW:(c + 1) * CW].rearrange("(k p) c -> p k c", p=P)

        def stream_dense(sp, first, last, wait_used):
            for n in range(first, last):
                if n >= PRE_RING:
                    wait_used(n - PRE_RING)
                sp.dma_start(wide(n), dense_source(n)).then_inc(ring_full[n % PRE_RING], 16)

        def wait_dense(pe, n):
            pe.wait_ge(ring_full[n % PRE_RING], 16 * (n // PRE_RING + 1))

        mid = ExitStack()
        pj = ExitStack()
        with mid:
            def hold(name, shape, dt=F32):
                return mid.enter_context(nc.sbuf_tensor(name, shape, dt))
            room = hold("room", [P, LENT])
            mod = hold("mod", [P, 2, 6 * KT])
            TB = hold("TB", [P, G, P])
            CA = hold("CA", [P, G, CH + 1, NC])
            Dg = hold("Dg", [P, G, P])
            Jm = hold("Jm", [P, P])
            phase = hold("phase", [P, 3, G])
            env = dict(locals())
            stage_tables(nc, A, env)
            env["projT"] = hold("projT", [P, 2 * KT, T])
            end_stage()
            stage_project(nc, A, env)
            end_stage()
            stage_s5(nc, A, O, env)
            end_stage()
            stage_attention(nc, A, O, env)
            end_stage()
            stage_mix(nc, A, env)
            end_stage()
        stage_moe(nc, A, env)
        end_stage()
        stage_output(nc, A, O, env)


def stage_tables(nc, A, env):
    PS, ident, x_tok, one_p, mod = (env[k] for k in ("PS", "ident", "x_tok", "one_p", "mod"))
    TB, CA, Dg, Jm, phase = (env[k] for k in ("TB", "CA", "Dg", "Jm", "phase"))
    mod_raw, mod_rows, sem = env["mod_raw"], env["mod_rows"], env["sem"]
    ada_used, ada_copied = sem("ada_used"), sem("ada_copied")
    ada_sent = [sem(f"ada_sent{b}") for b in range(3)]
    ADA_BANK = (0, 6, 7)
    spare = env["spare"]
    stream_dense, wait_dense, wide = env["stream_dense"], env["wait_dense"], env["wide"]
    st = ExitStack()
    with st:
        def sb(name, shape, dt=F32):
            return st.enter_context(nc.sbuf_tensor(name, shape, dt))
        c16 = sb("c16", [2 * KT, P])
        cT = sb("cT", [P, 2 * KT])
        bada = sb("bada", [2 * 6 * KT, P])
        modT = sb("modT", [2 * 6 * KT, P])
        ada_row = [spare(14784 + 512 * b, 2, 512) for b in range(3)]
        ln_row = spare(12000, P, 2, D)
        stats = sb("stats", [P, NT, 2, 6])
        mv = sb("mv", [P, NT, 2])
        std = sb("std", [P, NT])
        q = sb("q", [G, 24, NS])
        qi = sb("qi", [G, NS], I32)
        ldt = sb("ldt", [G, 1])
        dt_ = sb("dt_", [G, 1])
        M = spare(8192, G, 23, 2, NS)
        s5c = spare(14048, P, 23, G)
        V = sb("V", [P, G, NC])
        JV = sb("JV", [P, G, NC])
        tmp = sb("tmp", [P, G, NC])
        tmp2 = sb("tmp2", [P, G, NC])
        cs = sb("cs", [P, 4, 2, 2, NS])
        V2 = sb("V2", [P, 2, G, NC])
        JB = sb("JB", [P, G, NC])
        TBs = spare(0, P, G, CH, NC)
        Kt = spare(4096, NC, G, P)
        d16 = sb("d16", [NC, G])
        dd = sb("dd", [NC, G, NC])
        pt, pt2 = spare(8192, P, G, NC), spare(8704, P, G, NC)

        ld_x, ld_c, ld_b, ld_ln, ld_q, ld_v, ld_cs, ld_d, ld_raw, raw_summed, x_normal = (
            sem(n) for n in ("ld_x", "ld_c", "ld_b", "ld_ln", "ld_q", "ld_v", "ld_cs", "ld_d", "ld_raw", "raw_summed", "x_normal"))
        s_pool, s_const, s_one = sem("t_pool"), sem("t_const"), sem("t_one")
        c_silu, c_turned, c_ready = sem("c_silu"), sem("c_turned"), sem("c_ready")
        mod_done, bada_turned, mod_sum, modT_turned, modT_ready, mod_sent = (sem(n) for n in ("mod_done", "bada_turned", "mod_sum", "modT_turned", "modT_ready", "mod_sent"))
        var_ready, std_ready = sem("var_ready"), sem("std_ready")
        t_dve, t_act = sem("t_dve"), sem("t_act")
        dt_ready, ang_ready, trig_ready = sem("dt_ready"), sem("ang_ready"), sem("trig_ready")
        m_ready, m_turned, m_copied = sem("m_ready"), sem("m_turned"), sem("m_copied")
        cs_ready, cs_turned, cs_copied = sem("cs_ready"), sem("cs_turned"), sem("cs_copied")
        bb_ready, jb_done, tbs_ready, tb_turned, tb_copied = (sem(n) for n in ("bb_ready", "jb_done", "tbs_ready", "tb_turned", "tb_copied"))
        ca_ready, k_done, k_copied, kt_ready, dg_zero, dg_done = (sem(n) for n in ("ca_ready", "k_done", "k_copied", "kt_ready", "dg_zero", "dg_done"))

        block = st.enter_context(nc.Block())

        @block.sync
        def _(sp):
            stream_dense(sp, 0, N_ADA + PRE_RING, lambda n: sp.wait_ge(ada_used, n + 1))

        @block.gpsimd
        def _(pool):
            link = chained(pool, s_pool)
            pool.dma_start(ln_row[:, 0, :], A["ln_in_g"].partition_broadcast(P)).then_inc(ld_ln, 16)
            pool.dma_start(ln_row[:, 1, :], A["ln_in_b"].partition_broadcast(P)).then_inc(ld_ln, 16)
            link(pool.memset(ident[:], 0.0))
            pool.affine_select(out=ident[:], in_=ident[:], compare_op=ALU.not_equal, fill=1.0, base=0,
                               pattern=[[-1, P]], channel_multiplier=1).then_inc(s_const, 1)
            link(pool.memset(Jm[:], 0.0))
            link(pool.affine_select(out=Jm[:], in_=Jm[:], compare_op=ALU.not_equal, fill=-1.0, base=-NS,
                                    pattern=[[-1, P]], channel_multiplier=1))
            pool.affine_select(out=Jm[:], in_=Jm[:], compare_op=ALU.not_equal, fill=1.0, base=NS,
                               pattern=[[-1, P]], channel_multiplier=1).then_inc(s_const, 1)
            pool.memset(Dg[:], 0.0).then_inc(dg_zero, 1)
            pool.wait_ge(ld_ln, 32)
            for ti, r in enumerate(ROWS):
                pool.wait_ge(x_normal, ti + 1)
                x = x_tok[0:r, ti, :]
                link(nc.gpsimd.tensor_tensor(x, x, ln_row[0:r, 0, :], ALU.mult))
                link(nc.gpsimd.tensor_tensor(x, x, ln_row[0:r, 1, :], ALU.add))
            pool.wait_ge(m_copied, 1)
            pool.wait_ge(cs_copied, 1)
            for k in range(CH + 1):
                re, im = (s5c[:, first + k, :].unsqueeze(2).to_broadcast((P, G, NC)) for first in (5, 14))
                link(nc.gpsimd.tensor_tensor(pt, V2[:, 0], re, ALU.mult))
                link(nc.gpsimd.tensor_tensor(pt2, V2[:, 1], im, ALU.mult))
                nc.gpsimd.tensor_tensor(CA[:, :, k, :], pt, pt2, ALU.add).then_inc(ca_ready, 1)
                pool.wait_ge(ca_ready, k + 1)
            pool.wait_ge(dg_zero, 1)
            pool.wait_ge(kt_ready, 1)
            for j in range(CH):
                pool.dma_start(Dg[NC * j:NC * (j + 1), :, NC * j:P], Kt[:, :, 0:P - NC * j]).then_inc(dg_done, 16)
            pool.wait_ge(dg_done, 16 * CH)

        @block.scalar
        def _(act):
            link = chained(act, t_act)
            act.dma_start(c16[0:KT, :], A["c_prompt"].rearrange("a (k p) -> (a k) p", p=P)).then_inc(ld_c, 16)
            act.dma_start(c16[KT:2 * KT, :], A["c_sample"].rearrange("a (k p) -> (a k) p", p=P)).then_inc(ld_c, 16)
            for s in range(2):
                act.dma_start(bada[6 * KT * s:6 * KT * (s + 1), :], A["b_ada"].rearrange("a (k p) -> (a k) p", p=P)).then_inc(ld_b, 16)
            act.dma_start(q[:, 0, :], A["s5_a_re"][0]).then_inc(ld_q, 16)
            act.dma_start(q[:, 1, :], A["s5_a_im"][0]).then_inc(ld_q, 16)
            act.dma_start(ldt[:], A["s5_log_dt"].rearrange("a g -> g a")).then_inc(ld_q, 16)
            act.dma_start(x_tok[:, 0:NT - 1, :], A["x_prompt"][0].rearrange("(t p) d -> p t d", p=P)).then_inc(ld_x, 16)
            act.dma_start(x_tok[0:LS, NT - 1, :], A["x_sample"][0]).then_inc(ld_x, 16)
            b_re, b_im = (A[n][0].rearrange("g p n -> p g n") for n in ("s5_b_re", "s5_b_im"))
            act.dma_start(V[0:NS], b_re).then_inc(ld_v, 16)
            act.dma_start(V[NS:P], b_im).then_inc(ld_v, 16)
            act.dma_start(JV[NS:P], b_re).then_inc(ld_v, 16)
            act.dma_start(JV[0:NS], b_im).then_inc(ld_v, 16)
            c_re, c_im = (A[n][0].rearrange("(t g) n p -> (g n) t p", t=4) for n in ("s5_c_re", "s5_c_im"))
            act.dma_start(cs[:, :, 0, 0, :], c_re).then_inc(ld_cs, 16)
            act.dma_start(cs[:, :, 1, 1, :], c_re).then_inc(ld_cs, 16)
            act.dma_start(cs[:, :, 0, 1, :], c_im).then_inc(ld_cs, 16)
            act.dma_start(d16[:], A["s5_d"].rearrange("a (g n) -> (a n) g", n=NC), allow_slow_non_contiguous=True).then_inc(ld_d, 16)
            act.wait_ge(ld_c, 32)
            nc.scalar.activation(c16[:], c16[:], ACT.Silu).then_inc(c_silu, 1)
            act.wait_ge(ld_q, 48)
            nc.scalar.activation(dt_[:], ldt[:], ACT.Exp).then_inc(dt_ready, 1)
            act.wait_ge(ang_ready, 1)
            nc.scalar.activation(q[:, 3, :], q[:, 2, :], ACT.Exp).then_inc(trig_ready, 1)
            nc.scalar.activation(q[:, 7, :], q[:, 5, :], ACT.Sin).then_inc(trig_ready, 1)
            nc.scalar.activation(q[:, 8, :], q[:, 6, :], ACT.Sin).then_inc(trig_ready, 1)

            def ada_out(first, last):
                for m in range(first, last):
                    b = m % 3
                    act.wait_ge(ada_used, 2 * m + 2)
                    if m >= 3:
                        act.wait_ge(ada_sent[b], 16 * (m // 3))
                    nc.scalar.copy(ada_row[b], PS[0:2, ADA_BANK[b], :]).then_inc(ada_copied, 1)
                    act.wait_ge(ada_copied, m + 1)
                    act.dma_start(mod_raw[:, 512 * m:512 * (m + 1)], ada_row[b]).then_inc(ada_sent[b], 16)

            ada_out(0, 5)
            act.wait_ge(cs_turned, 1)
            nc.scalar.copy(V2[:].rearrange("p v g n -> p v (g n)"), PS[:, 4:6, :]).then_inc(cs_copied, 1)
            act.wait_ge(var_ready, NT)
            act.wait_ge(s_one, 2)
            for ti, r in enumerate(ROWS):
                nc.scalar.activation(std[0:r, ti:ti + 1], mv[0:r, ti, 1:2], ACT.Sqrt, bias=one_p[0:r, 1:2]).then_inc(std_ready, 1)
            ada_out(5, 8)
            for r in range(G // 4):
                act.wait_ge(tb_turned, r + 1)
                nc.scalar.copy(TB[:, 4 * r:4 * r + 4, :], PS[:, 2 + r % 2, :].rearrange("p (g s) -> p g s", g=4)).then_inc(tb_copied, 1)
            ada_out(8, 11)
            for r in range(G // 4):
                act.wait_ge(k_done, r + 1)
                nc.scalar.copy(Kt[:, 4 * r:4 * r + 4, :], PS[0:NC, 4 + r % 2, :].rearrange("p (g s) -> p g s", g=4)).then_inc(k_copied, 1)
            ada_out(11, 12)
            for b in range(3):
                act.wait_ge(ada_sent[b], 16 * 4)
            act.dma_start(modT[:], mod_raw.rearrange("s (k p) -> (s k) p", p=P)).then_inc(ld_raw, 16)
            act.wait_ge(modT_ready, 1)
            act.dma_start(mod_rows.rearrange("s (k p) -> (s k) p", p=P), modT[:]).then_inc(mod_sent, 16)
            act.wait_ge(mod_sent, 16)

        @block.vector
        def _(dve):
            link = chained(dve, t_dve)
            vec = nc.vector

            def done(ins, sem, value):
                ins.then_inc(sem, 1)
                dve.wait_ge(sem, value)

            vec.memset(one_p[:, 0:1], 1.0).then_inc(s_one, 1)
            vec.memset(one_p[:, 1:2], EPS).then_inc(s_one, 1)
            dve.wait_ge(c_turned, 1)
            vec.tensor_copy(cT[:], PS[:, 1, 0:2 * KT]).then_inc(c_ready, 1)

            are, aim, ard, mag, th, ang, hang, sn, shalf, a_r, a_i, den, nr, t0, t1, cosn, vr, vi, t2 = (
                q[:, k, :] for k in range(19))
            dve.wait_ge(dt_ready, 1)
            link(vec.tensor_scalar(ard, are, dt_[:, 0:1], None, ALU.mult))
            link(vec.tensor_scalar(th, aim, dt_[:, 0:1], None, ALU.mult))
            link(vec.tensor_scalar(qi[:], th, 1.0 / (2 * math.pi), None, ALU.mult))
            link(vec.tensor_copy(t0, qi[:]))
            p1 = 6.28125
            p2 = float(int((2 * math.pi - p1) * 2 ** 22)) / 2 ** 22
            p3 = 2 * math.pi - p1 - p2
            link(vec.scalar_tensor_tensor(out=ang, in0=t0, scalar=-p1, in1=th, op0=ALU.mult, op1=ALU.add))
            link(vec.scalar_tensor_tensor(out=ang, in0=t0, scalar=-p2, in1=ang, op0=ALU.mult, op1=ALU.add))
            link(vec.scalar_tensor_tensor(out=ang, in0=t0, scalar=-p3, in1=ang, op0=ALU.mult, op1=ALU.add))
            link(vec.tensor_scalar(ang, ang, 3.1415925, -3.1415925, ALU.min, ALU.max))
            vec.tensor_scalar(hang, ang, 0.5, None, ALU.mult).then_inc(ang_ready, 1)
            dve.wait_ge(trig_ready, 3)
            link(vec.tensor_tensor(t0, shalf, shalf, ALU.mult))
            link(vec.tensor_scalar(cosn, t0, -2.0, 1.0, ALU.mult, ALU.add))
            link(vec.tensor_tensor(a_r, mag, cosn, ALU.mult))
            link(vec.tensor_tensor(a_i, mag, sn, ALU.mult))

            def cmul(outr, outi, xr, xi, yr, yi, u, v):
                link(vec.tensor_tensor(u, xr, yr, ALU.mult))
                link(vec.tensor_tensor(v, xi, yi, ALU.mult))
                link(vec.tensor_tensor(t2, xr, yi, ALU.mult))
                link(vec.tensor_tensor(outi, xi, yr, ALU.mult))
                link(vec.tensor_tensor(outi, outi, t2, ALU.add))
                link(vec.tensor_tensor(outr, u, v, ALU.subtract))

            fr, fi = M[:, 0, 0, :], M[:, 1, 0, :]
            link(vec.tensor_tensor(t0, are, are, ALU.mult))
            link(vec.tensor_tensor(t1, aim, aim, ALU.mult))
            link(vec.tensor_tensor(t0, t0, t1, ALU.add))
            link(vec.reciprocal(den, t0))
            link(vec.tensor_scalar(nr, a_r, -1.0, None, ALU.add))
            link(vec.tensor_tensor(t0, nr, are, ALU.mult))
            link(vec.tensor_tensor(t1, a_i, aim, ALU.mult))
            link(vec.tensor_tensor(t0, t0, t1, ALU.add))
            link(vec.tensor_tensor(fr, t0, den, ALU.mult))
            link(vec.tensor_tensor(t0, a_i, are, ALU.mult))
            link(vec.tensor_tensor(t1, nr, aim, ALU.mult))
            link(vec.tensor_tensor(t0, t0, t1, ALU.subtract))
            link(vec.tensor_tensor(fi, t0, den, ALU.mult))
            link(vec.tensor_copy(vr, cosn))
            link(vec.tensor_copy(vi, sn))
            link(vec.tensor_tensor(nr, mag, mag, ALU.mult))
            for _ in range(2):
                cmul(vr, vi, vr, vi, vr, vi, t0, t1)
                link(vec.tensor_tensor(nr, nr, nr, ALU.mult))
            cmul(M[:, 2, 0, :], M[:, 3, 0, :], vr, vi, vr, vi, t0, t1)
            link(vec.tensor_copy(M[:, 4, 0, :], nr))
            pr = [M[:, 5 + k, 0, :] for k in range(CH + 1)]
            pi = [M[:, 14 + k, 0, :] for k in range(CH + 1)]
            link(vec.memset(pr[0], 1.0))
            link(vec.memset(pi[0], 0.0))
            link(vec.tensor_copy(pr[1], a_r))
            link(vec.tensor_copy(pi[1], a_i))
            for k in range(2, CH + 1):
                cmul(pr[k], pi[k], pr[k // 2], pi[k // 2], pr[k - k // 2], pi[k - k // 2], t0, t1)
            vec.tensor_copy(M[:, :, 1, :], M[:, :, 0, :]).then_inc(m_ready, 1)
            dve.wait_ge(ld_cs, 48)
            link(vec.tensor_scalar(cs[:, :, 0, 1, :], cs[:, :, 0, 1, :], -1.0, None, ALU.mult))
            link(vec.tensor_copy(cs[:, :, 1, 0, :], cs[:, :, 0, 1, :]))
            vec.tensor_scalar(cs[:, :, 1, 1, :], cs[:, :, 1, 1, :], -1.0, None, ALU.mult).then_inc(cs_ready, 1)
            dve.wait_ge(ld_x, 32)
            for ti, r in enumerate(ROWS):
                for h in range(2):
                    link(vec.bn_stats(stats[0:r, ti, h, :], x_tok[0:r, ti, 512 * h:512 * (h + 1)]))
                done(vec.bn_aggr(mv[0:r, ti, :], stats[0:r, ti].rearrange("p a b -> p (a b)")), var_ready, ti + 1)
            for ti, r in enumerate(ROWS):
                dve.wait_ge(std_ready, ti + 1)
                link(vec.reciprocal(std[0:r, ti:ti + 1], std[0:r, ti:ti + 1]))
                x = x_tok[0:r, ti, :]
                vec.tensor_scalar(x, x, mv[0:r, ti, 0:1], std[0:r, ti:ti + 1], ALU.subtract, ALU.mult).then_inc(x_normal, 1)
            dve.wait_ge(m_turned, 1)
            link(vec.tensor_copy(s5c[:, 0:16, :], PS[:, 2, :].rearrange("p (k g) -> p k g", g=G)))
            link(vec.tensor_copy(phase[:], PS[:, 2, 2 * G:5 * G].rearrange("p (k g) -> p k g", g=G)))
            done(vec.tensor_copy(s5c[:, 16:23, :], PS[:, 3, 0:7 * G].rearrange("p (k g) -> p k g", g=G)), m_copied, 1)

            def per_group(k):
                return s5c[:, k, :].unsqueeze(2).to_broadcast((P, G, NC))

            dve.wait_ge(ld_v, 64)
            link(vec.tensor_scalar(JV[0:NS], JV[0:NS], -1.0, None, ALU.mult))
            link(vec.tensor_tensor(V[:], V[:], per_group(0), ALU.mult))
            link(vec.tensor_tensor(JV[:], JV[:], per_group(1), ALU.mult))
            done(vec.tensor_tensor(V[:], V[:], JV[:], ALU.add), bb_ready, 1)
            dve.wait_ge(jb_done, 1)
            link(vec.tensor_copy(JB[:].rearrange("p g n -> p (g n)"), PS[:, 1, :]))
            for j in range(CH):
                link(vec.tensor_tensor(tmp[:], V[:], per_group(5 + CH - 1 - j), ALU.mult))
                link(vec.tensor_tensor(tmp2[:], JB[:], per_group(14 + CH - 1 - j), ALU.mult))
                done(vec.tensor_tensor(TBs[:, :, j, :], tmp[:], tmp2[:], ALU.add), tbs_ready, j + 1)
            dve.wait_ge(ld_d, 16)
            link(vec.tensor_tensor(dd[:], ident[0:NC, 0:NC].unsqueeze(1).to_broadcast((NC, G, NC)),
                                   d16[:].unsqueeze(2).to_broadcast((NC, G, NC)), ALU.mult))
            dve.wait_ge(k_copied, G // 4)
            vec.tensor_tensor(Kt[:, :, 0:NC], Kt[:, :, 0:NC], dd[:], ALU.add).then_inc(kt_ready, 1)
            dve.wait_ge(ld_b, 32)
            dve.wait_ge(ld_raw, 16)
            vec.tensor_tensor(modT[:], modT[:], bada[:], ALU.add).then_inc(raw_summed, 1)
            dve.wait_ge(mod_done, 1)
            link(vec.tensor_copy(mod[:].rearrange("p s k -> p (s k)"), PS[:, 1, 0:2 * 6 * KT]))
            for k in (1, 2, 4, 5):
                m = mod[:, :, k * KT:(k + 1) * KT]
                ins = vec.tensor_scalar(m, m, 1.0, None, ALU.add)
                ins.then_inc(mod_sum, 1)
            dve.wait_ge(modT_turned, 1)
            vec.tensor_copy(modT[:], PS[0:2 * 6 * KT, 1, 0:P]).then_inc(modT_ready, 1)

        @block.tensor
        def _(pe):
            mm, tr = nc.tensor.matmul, nc.tensor.transpose
            pe.wait_ge(s_const, 2)
            pe.wait_ge(c_silu, 1)
            tr(PS[:, 1, 0:2 * KT], c16[:], ident[0:2 * KT, 0:2 * KT]).then_inc(c_turned, 1)
            pe.wait_ge(c_ready, 1)

            def ada(first, last):
                for n in range(2 * first, 2 * last):
                    if n >= 6 and n % 2 == 0:
                        pe.wait_ge(ada_copied, n // 2 - 2)
                    wait_dense(pe, n)
                    for k in range(KT):
                        ins = mm(PS[0:2, ADA_BANK[n // 2 % 3], CW * (n % 2):CW * (n % 2 + 1)], cT[:, k::KT], wide(n)[:, k, :],
                                 start=(k == 0), stop=(k == KT - 1))
                    ins.then_inc(ada_used, 1)

            ada(0, 5)
            pe.wait_ge(m_ready, 1)
            for k in range(23):
                ins = tr(PS[:, 2 + k // 16, G * (k % 16):G * (k % 16 + 1)],
                         M[:, k].rearrange("g a s -> g (a s)"), ident[0:G, 0:G])
            ins.then_inc(m_turned, 1)
            pe.wait_ge(cs_ready, 1)
            for v in range(2):
                for t in range(4):
                    ins = tr(PS[:, 4 + v, P * t:P * (t + 1)], cs[:, t, v].rearrange("r a s -> r (a s)"), ident[:])
            ins.then_inc(cs_turned, 1)
            ada(5, 6)
            pe.wait_ge(bb_ready, 1)
            mm(PS[:, 1, :], Jm[:], V[:].rearrange("p g n -> p (g n)"), start=True, stop=True).then_inc(jb_done, 1)
            ada(6, 8)
            pe.wait_ge(tbs_ready, CH)
            pe.wait_ge(m_copied, 1)
            for r in range(G // 4):
                if r >= 2:
                    pe.wait_ge(tb_copied, r - 1)
                for g in range(4):
                    ins = tr(PS[:, 2 + r % 2, P * g:P * (g + 1)], TBs[:, 4 * r + g].rearrange("p j n -> p (j n)"), ident[:])
                ins.then_inc(tb_turned, 1)
            ada(8, 11)
            pe.wait_ge(ca_ready, CH + 1)
            for r in range(G // 4):
                if r >= 2:
                    pe.wait_ge(k_copied, r - 1)
                for g in range(4):
                    ins = mm(PS[0:NC, 4 + r % 2, P * g:P * (g + 1)], V[:, 4 * r + g, :],
                             CA[:, 4 * r + g, 0:CH, :].rearrange("p k n -> p (k n)"), start=True, stop=True)
                ins.then_inc(k_done, 1)
            ada(11, 12)
            pe.wait_ge(raw_summed, 1)
            tr(PS[:, 1, 0:2 * 6 * KT], modT[:], ident[0:2 * 6 * KT, 0:2 * 6 * KT]).then_inc(mod_done, 1)
            pe.wait_ge(mod_sum, 4)
            tr(PS[0:2 * 6 * KT, 1, 0:P], mod[:].rearrange("p s k -> p (s k)"), ident[:]).then_inc(modT_turned, 1)


def stage_project(nc, A, env):
    PS, ident, x_tok, mod, phase, projT = (env[k] for k in ("PS", "ident", "x_tok", "mod", "phase", "projT"))
    spare, sem = env["spare"], env["sem"]
    stream_dense, wait_dense, wide = env["stream_dense"], env["wait_dense"], env["wide"]
    cosT, sinT, decay = spare(0, P, G, POS), spare(2240, P, G, POS), spare(4480, P, G, POS)
    hT = spare(6720, P, KT, T)
    pa, pb = spare(11072, P, G, 32), spare(12096, P, G, 32)
    wr, wi, wt = spare(13120, P, G), spare(13152, P, G), spare(13184, P, G)
    x_turned, h_ready, proj_done, proj_copied, t_dve = (sem(n) for n in ("x_turned", "h_ready", "proj_done", "proj_copied", "p_dve"))
    with nc.Block() as block:
        @block.sync
        def _(sp):
            stream_dense(sp, N_ADA + PRE_RING, PRE, lambda n: sp.wait_ge(proj_done, 2 * (n - N_ADA + 1)))

        @block.tensor
        def _(pe):
            for ti, r in enumerate(ROWS):
                if ti >= 2:
                    pe.wait_ge(h_ready, ti - 1)
                b = 4 + 2 * (ti % 2)
                for k in range(KT):
                    ins = nc.tensor.transpose(PS[:, b + k // 4, P * (k % 4):P * (k % 4) + r],
                                              x_tok[0:r, ti, P * k:P * (k + 1)], ident[0:r, 0:r])
                ins.then_inc(x_turned, 1)
            pe.wait_ge(h_ready, NT)
            for ct in range(2 * KT):
                n = N_ADA + ct // 2
                if ct % 2 == 0:
                    wait_dense(pe, n)
                b = 2 * (ct % 4)
                if ct >= 4:
                    pe.wait_ge(proj_copied, ct - 3)
                for k in range(KT):
                    for h in range(2):
                        ins = nc.tensor.matmul(PS[:, b + h, 0:HALF], wide(n)[:, k, P * (ct % 2):P * (ct % 2 + 1)],
                                               hT[:, k, HALF * h:HALF * (h + 1)], start=(k == 0), stop=(k == KT - 1))
                ins.then_inc(proj_done, 1)

        @block.scalar
        def _(act):
            for ct in range(2 * KT):
                act.wait_ge(proj_done, ct + 1)
                b = 2 * (ct % 4)
                nc.scalar.activation(projT[:, ct, :].rearrange("p (h t) -> p h t", h=2), PS[:, b:b + 2, 0:HALF], ACT.Copy,
                                     scale=DH ** -0.5 if 4 <= ct < 8 else 1.0).then_inc(proj_copied, 1)

        @block.vector
        def _(dve):
            link = chained(dve, t_dve)
            vec = nc.vector
            for ti, r in enumerate(ROWS):
                dve.wait_ge(x_turned, ti + 1)
                s, b = ti // (NT - 1), 4 + 2 * (ti % 2)
                for k in range(KT):
                    ins = vec.tensor_scalar(hT[:, k, P * ti:P * ti + r], PS[:, b + k // 4, P * (k % 4):P * (k % 4) + r],
                                            mod[:, s, KT + k:KT + k + 1], mod[:, s, k:k + 1], ALU.mult, ALU.add)
                ins.then_inc(h_ready, 1)
            link(vec.tensor_copy(wr, phase[:, 0, :]))
            link(vec.tensor_copy(wi, phase[:, 1, :]))
            link(vec.memset(cosT[:, :, 0:1], 1.0))
            link(vec.memset(sinT[:, :, 0:1], 0.0))
            m = 1
            while m < CP:
                a, b = pa[:, :, 0:m], pb[:, :, 0:m]
                br, bi = (w.unsqueeze(2).to_broadcast((P, G, m)) for w in (wr, wi))
                c0, s0 = cosT[:, :, 0:m], sinT[:, :, 0:m]
                c1, s1 = cosT[:, :, m:2 * m], sinT[:, :, m:2 * m]
                link(vec.tensor_tensor(a, c0, br, ALU.mult))
                link(vec.tensor_tensor(b, s0, bi, ALU.mult))
                link(vec.tensor_tensor(c1, a, b, ALU.subtract))
                link(vec.tensor_tensor(a, c0, bi, ALU.mult))
                link(vec.tensor_tensor(b, s0, br, ALU.mult))
                link(vec.tensor_tensor(s1, a, b, ALU.add))
                link(vec.tensor_tensor(wt, wr, wi, ALU.mult))
                link(vec.tensor_tensor(wr, wr, wr, ALU.mult))
                link(vec.tensor_tensor(wi, wi, wi, ALU.mult))
                link(vec.tensor_tensor(wr, wr, wi, ALU.subtract))
                link(vec.tensor_scalar(wi, wt, 2.0, None, ALU.mult))
                m *= 2
            link(vec.tensor_copy(cosT[:, :, CP:CP + 1], wr.unsqueeze(2)))
            link(vec.tensor_copy(sinT[:, :, CP:CP + 1], wi.unsqueeze(2)))
            link(vec.tensor_copy(cosT[:, :, CP + 1:POS], cosT[:, :, 0:CS + 1]))
            link(vec.tensor_copy(sinT[:, :, CP + 1:POS], sinT[:, :, 0:CS + 1]))
            link(vec.tensor_copy(decay, phase[:, 2, :].unsqueeze(2).to_broadcast((P, G, POS))))
            link(vec.memset(decay[:, :, 0:1], 0.0))
            link(vec.memset(decay[:, :, CP + 1:CP + 2], 0.0))


def stage_s5(nc, A, O, env):
    PS, ident, projT, TB, CA, Dg, Jm = (env[k] for k in ("PS", "ident", "projT", "TB", "CA", "Dg", "Jm"))
    spare, sem = env["spare"], env["sem"]
    cosT, sinT, decay = spare(0, P, G * POS), spare(2240, P, G * POS), spare(4480, P, G * POS)
    Ug = spare(6720, P, G, C)
    Uc = spare(8896, C, G, CH, NC)
    Sx = spare(8896, P, G, POS)
    Sf = spare(8896, P, G * POS)
    w1, w1f = spare(11136, P, G, POS), spare(11136, P, G * POS)
    Xp = spare(4480, P, G, C)
    Gc = spare(0, C, CH, S5W)
    gT = spare(11136, P, 4, T)
    wglu = spare(13376, P, 4, S5W)
    sg = spare(8896, P, T)
    s0 = spare(15424, G, 2, NS)
    Xf = spare(15552, P, 2, G)
    fin = spare(15616, G, 2, 2, NS)
    bglu = spare(15872, P, 4)
    (ld_s, ld_w, uc_turned, uc_copied, ug_turned, ug_copied, s_done, s_copied, x0_turned, sx_ready, j_done, w_ready,
     j2_done, x_ready, f_turned, f_copied, s_sent, y_done, y_copied, g_turned, g_copied, z_done, z_sig, z_used, t_dve, bg_turned) = (
        sem("s5_" + n) for n in ("ld_s", "ld_w", "uc_turned", "uc_copied", "ug_turned", "ug_copied", "s_done", "s_copied", "x0_turned",
                                 "sx_ready", "j_done", "w_ready", "j2_done", "x_ready", "f_turned", "f_copied", "s_sent", "y_done",
                                 "y_copied", "g_turned", "g_copied", "z_done", "z_sig", "z_used", "dve", "bg"))
    with nc.Block() as block:
        @block.sync
        def _(sp):
            sp.dma_start(s0[:, 0, :], A["state_s5_re"][0, 0]).then_inc(ld_s, 16)
            sp.dma_start(s0[:, 1, :], A["state_s5_im"][0, 0]).then_inc(ld_s, 16)
            sp.dma_start(bglu, A["s5_b_glu"].rearrange("a (c p) -> p (a c)", p=P), allow_slow_non_contiguous=True).then_inc(ld_w, 16)
            sp.dma_start(wglu, A["s5_w_glu"][0].rearrange("(k p) c -> p k c", p=P)).then_inc(ld_w, 16)
            sp.wait_ge(f_copied, 1)
            for s, (re, im) in enumerate((("s5_re_p", "s5_im_p"), ("s5_re_s", "s5_im_s"))):
                sp.dma_start(O[re][0, 0], fin[:, s, 0, :]).then_inc(s_sent, 16)
                sp.dma_start(O[im][0, 0], fin[:, s, 1, :]).then_inc(s_sent, 16)
            sp.wait_ge(s_sent, 64)

        @block.tensor
        def _(pe):
            mm, tr = nc.tensor.matmul, nc.tensor.transpose
            for j in range(CH):
                for c in range(4):
                    ins = tr(PS[0:C, j, P * c:P * (c + 1)], projT[:, c, j::CH], ident[:])
                ins.then_inc(uc_turned, 1)
            pe.wait_ge(uc_copied, CH)
            for r in range(8):
                for g in range(4):
                    ins = tr(PS[:, r, C * g:C * (g + 1)], Uc[:, 4 * r + g].rearrange("c j n -> c (j n)"), ident[0:C, 0:C])
                ins.then_inc(ug_turned, 1)
            for r in range(8):
                pe.wait_ge(ug_copied, r + 1)
                for g in range(4):
                    ins = mm(PS[:, r, C * g:C * (g + 1)], TB[:, 4 * r + g, :], Ug[:, 4 * r + g, :], start=True, stop=True)
                ins.then_inc(s_done, 1)
            pe.wait_ge(ld_s, 32)
            pe.wait_ge(s_copied, 1)
            tr(PS[:, 0, 0:G], s0.rearrange("g a s -> g (a s)"), ident[0:G, 0:G]).then_inc(x0_turned, 1)
            pe.wait_ge(sx_ready, 1)
            for b in range(5):
                ins = mm(PS[:, 1 + b, 0:448], Jm[:], Sf[:, 448 * b:448 * (b + 1)], start=True, stop=True)
            ins.then_inc(j_done, 1)
            pe.wait_ge(w_ready, 1)
            for b in range(5):
                ins = mm(PS[:, 1 + b, 0:448], Jm[:], w1f[:, 448 * b:448 * (b + 1)], start=True, stop=True)
            ins.then_inc(j2_done, 1)
            pe.wait_ge(x_ready, 1)
            for s in range(2):
                ins = tr(PS[0:G, 0, P * s:P * (s + 1)], Xf[:, s, :], ident[:])
            ins.then_inc(f_turned, 1)
            for r in range(8):
                b = 6 + r % 2
                if r >= 2:
                    pe.wait_ge(y_copied, r - 1)
                for g in range(4):
                    o = PS[0:C, b, P * g:P * (g + 1)]
                    mm(o, Ug[:, 4 * r + g, :], Dg[:, 4 * r + g, :], start=True, stop=False)
                    ins = mm(o, Xp[:, 4 * r + g, :], CA[:, 4 * r + g, 1:CH + 1, :].rearrange("p k n -> p (k n)"), start=False, stop=True)
                ins.then_inc(y_done, 1)
            pe.wait_ge(y_copied, 8)
            for c in range(4):
                for h in range(2):
                    b = 1 + (2 * c + h) % 4
                    if 2 * c + h >= 4:
                        pe.wait_ge(g_copied, 2 * c + h - 3)
                    for i in range(4):
                        ins = tr(PS[:, b, C * i:C * (i + 1)], Gc[:, 4 * h + i, P * c:P * (c + 1)], ident[0:C, 0:C])
                    ins.then_inc(g_turned, 1)
            pe.wait_ge(g_copied, 8)
            pe.wait_ge(ld_w, 32)
            for ct in range(4):
                b = 2 * (ct % 2)
                if ct >= 2:
                    pe.wait_ge(z_sig, ct - 1)
                for k in range(4):
                    for h in range(2):
                        ins = mm(PS[:, b + h, 0:HALF], wglu[:, k, P * ct:P * (ct + 1)], gT[:, k, HALF * h:HALF * (h + 1)],
                                 start=(k == 0), stop=(k == 3))
                ins.then_inc(z_done, 1)

        @block.scalar
        def _(act):
            for j in range(CH):
                act.wait_ge(uc_turned, j + 1)
                nc.scalar.copy(Uc[:, :, j, :], PS[0:C, j, :].rearrange("c (g n) -> c g n", n=NC)).then_inc(uc_copied, 1)
            for r in range(8):
                act.wait_ge(ug_turned, r + 1)
                nc.scalar.copy(Ug[:, 4 * r:4 * r + 4, :], PS[:, r, 0:4 * C].rearrange("p (g c) -> p g c", g=4)).then_inc(ug_copied, 1)
            for r in range(8):
                act.wait_ge(y_done, r + 1)
                nc.scalar.activation(Gc[:, :, 64 * r:64 * (r + 1)].rearrange("c i (g n) -> c g i n", g=4),
                                     PS[0:C, 6 + r % 2, :].rearrange("c (g i n) -> c g i n", g=4, i=CH),
                                     ACT.Gelu_apprx_tanh).then_inc(y_copied, 1)
            for ct in range(4):
                act.wait_ge(z_done, ct + 1)
                act.wait_ge(ld_w, 32)
                if ct >= 1:
                    act.wait_ge(z_used, ct)
                b = 2 * (ct % 2)
                nc.scalar.activation(sg.rearrange("p (h t) -> p h t", h=2), PS[:, b:b + 2, 0:HALF], ACT.Sigmoid,
                                     bias=bglu[:, ct:ct + 1]).then_inc(z_sig, 1)

        @block.vector
        def _(dve):
            link = chained(dve, t_dve)
            vec = nc.vector
            dve.wait_ge(ug_copied, 8)
            for r in range(8):
                dve.wait_ge(ug_turned, 8)
                dve.wait_ge(s_done, r + 1)
                src = PS[:, r, 0:4 * C].rearrange("p (g c) -> p g c", g=4)
                vec.tensor_copy(Sx[:, 4 * r:4 * r + 4, 1:CP + 1], src[:, :, 0:CP])
                vec.tensor_copy(Sx[:, 4 * r:4 * r + 4, CP + 2:POS], src[:, :, CP:C]).then_inc(s_copied, 1)
            vec.memset(Sx[:, :, 0:1], 0.0)
            dve.wait_ge(x0_turned, 1)
            vec.tensor_copy(Sx[:, :, CP + 1:CP + 2], PS[:, 0, 0:G].unsqueeze(2)).then_inc(sx_ready, 1)
            dve.wait_ge(sx_ready, 1)
            link(vec.tensor_tensor(w1f, cosT, Sf, ALU.mult))
            dve.wait_ge(j_done, 1)
            jp = PS[:, 1:6, 0:448]
            link(vec.tensor_tensor(Sf.rearrange("p (a b) -> p a b", a=5), jp, sinT.rearrange("p (a b) -> p a b", a=5), ALU.mult))
            link(vec.tensor_tensor(Sf, w1f, Sf, ALU.subtract))
            vec.tensor_tensor_scan(w1f, decay, Sf, 0.0, ALU.mult, ALU.add).then_inc(w_ready, 1)
            dve.wait_ge(w_ready, 1)
            link(vec.tensor_tensor(Sf, cosT, w1f, ALU.mult))
            dve.wait_ge(j2_done, 1)
            link(vec.tensor_tensor(w1f.rearrange("p (a b) -> p a b", a=5), jp, sinT.rearrange("p (a b) -> p a b", a=5), ALU.mult))
            vec.tensor_tensor(Xp[:, :, 0:CP], w1[:, :, 0:CP], Sx[:, :, 0:CP], ALU.add)
            vec.tensor_tensor(Xp[:, :, CP:C], w1[:, :, CP + 1:POS - 1], Sx[:, :, CP + 1:POS - 1], ALU.add)
            vec.tensor_tensor(Xf[:, 0, :], w1[:, :, CP], Sx[:, :, CP], ALU.add)
            vec.tensor_tensor(Xf[:, 1, :], w1[:, :, POS - 1], Sx[:, :, POS - 1], ALU.add).then_inc(x_ready, 1)
            dve.wait_ge(f_turned, 1)
            vec.tensor_copy(fin, PS[0:G, 0, 0:2 * P].rearrange("g (s a n) -> g s a n", s=2, a=2)).then_inc(f_copied, 1)
            for c in range(4):
                for h in range(2):
                    m = 2 * c + h
                    dve.wait_ge(g_turned, m + 1)
                    vec.tensor_copy(gT[:, c, :].rearrange("p (c i) -> p i c", i=CH)[:, 4 * h:4 * h + 4, :],
                                    PS[:, 1 + m % 4, 0:4 * C].rearrange("p (i c) -> p i c", i=4)).then_inc(g_copied, 1)
            dve.wait_ge(g_copied, 8)
            for ct in range(4):
                dve.wait_ge(z_sig, ct + 1)
                vec.tensor_tensor(projT[:, ct, :], gT[:, ct, :], sg, ALU.mult).then_inc(z_used, 1)


def stage_attention(nc, A, O, env):
    PS, ident, projT = (env[k] for k in ("PS", "ident", "projT"))
    spare, sem = env["spare"], env["sem"]
    W = 1280
    OFF = [0, 512, 1024, 896]
    v_tok, k_tok = spare(0, P, NT, 512), spare(2560, P, NT, 512)
    kc, vc = spare(5120, P, 2, H, DH), spare(6144, P, 2, H, DH)
    kcT = spare(7168, P, 4, PAST)
    soft = [spare(8192 + 1280 * b, P, W) for b in range(2)]
    wts = [spare(10752 + 1280 * b, P, W) for b in range(3)]
    ntri, nones = spare(14592, P, P), spare(14720, P, P)
    (ld_kc, ld_vc, a_const, tok_turned, tok_copied, kv_sent, kc_turned, kc_copied, z_done, abs_done, exp_done, ln_done, soft_ready,
     soft_masked, cum_done, w_done, w_masked, pv_done, o_copied, a_pool) = (
        sem("at_" + n) for n in ("ld_kc", "ld_vc", "const", "tok_turned", "tok_copied", "kv_sent", "kc_turned", "kc_copied", "z", "abs",
                                 "exp", "ln", "soft", "soft_m", "cum", "w", "w_m", "pv", "o", "pool"))
    zero, y_dram = spare(14848, P, D), env["y_dram"]
    zero_ok, y_zeroed = sem("at_zero_ok"), sem("at_y_zeroed")
    units = H + 1
    NW = LS * H // 2

    def bank(u):
        return 3 * (u % 2)

    def flat(u):
        return PS[:, bank(u):bank(u) + 3, :].rearrange("p b c -> p (b c)")

    def spans(u):
        return [(P, 0, W)] if u < H else [s for b in (0, 512) for s in ((P, b, 2 * NW), (LS, b + 2 * NW, NW))]

    with nc.Block() as block:
        @block.sync
        def _(sp):
            sp.dma_start(kc[:, 0], A["cache_k"][0, 0][:, 0:P].rearrange("h p d -> p h d")).then_inc(ld_kc, 16)
            sp.dma_start(kc[:, 1], A["cache_k"][0, 0][:, P:2 * P].rearrange("h p d -> p h d")).then_inc(ld_kc, 16)
            sp.dma_start(vc[:, 0], A["cache_v"][0, 0][:, 0:P].rearrange("h p d -> p h d")).then_inc(ld_vc, 16)
            sp.dma_start(vc[:, 1], A["cache_v"][0, 0][:, P:2 * P].rearrange("h p d -> p h d")).then_inc(ld_vc, 16)
            for m in range(2 * NT):
                ti, src, out = m % NT, (k_tok, v_tok)[m // NT], ("k", "v")[m // NT]
                sp.wait_ge(tok_copied, m + 1)
                if ti < NT - 1:
                    dst = O[out + "_p"][0, 0][:, P * ti:P * (ti + 1)]
                else:
                    dst = O[out + "_s"][0, 0]
                sp.dma_start(dst.rearrange("h p d -> p h d"),
                             src[0:ROWS[ti], ti, :].rearrange("p (h d) -> p h d", h=H)).then_inc(kv_sent, 16)
            sp.wait_ge(zero_ok, 1)
            for j in range(OVF):
                sp.dma_start(y_dram[P * (E + j):P * (E + j + 1), :], zero).then_inc(y_zeroed, 16)
            sp.wait_ge(kv_sent, 32 * NT)
            sp.wait_ge(y_zeroed, 16 * OVF)

        @block.gpsimd
        def _(pool):
            link = chained(pool, a_pool)
            pool.memset(zero, 0.0).then_inc(zero_ok, 1)
            link(pool.memset(ntri, -1.0))
            pool.affine_select(out=ntri, in_=ntri, compare_op=ALU.is_ge, fill=0.0, base=0,
                               pattern=[[-1, P]], channel_multiplier=1).then_inc(a_const, 1)
            pool.memset(nones, -1.0).then_inc(a_const, 1)

            def mask(t, u, sem):
                if u < H:
                    for a in range(4):
                        v = t[:, OFF[a]:OFF[a] + P]
                        ins = pool.affine_select(out=v, in_=v, compare_op=ALU.is_gt, fill=0.0, base=0,
                                                 pattern=[[1, P]], channel_multiplier=-1)
                else:
                    for b in (0, 512):
                        v = t[0:LS, b + 2 * NW:b + 3 * NW].rearrange("p (h c) -> p h c", c=LS)
                        ins = pool.affine_select(out=v, in_=v, compare_op=ALU.is_gt, fill=0.0, base=0,
                                                 pattern=[[0, H // 2], [1, LS]], channel_multiplier=-1)
                ins.then_inc(sem, 1)

            for u in range(units + 1):
                if u < units:
                    pool.wait_ge(soft_ready, u + 1)
                    mask(soft[u % 2], u, soft_masked)
                if u >= 1:
                    pool.wait_ge(w_done, u)
                    mask(wts[(u - 1) % 3], u - 1, w_masked)

        @block.tensor
        def _(pe):
            mm, tr = nc.tensor.matmul, nc.tensor.transpose
            for m in range(2 * NT):
                ti, c0 = m % NT, (8, 12)[m // NT]
                if m >= 4:
                    pe.wait_ge(tok_copied, m - 3)
                for c in range(4):
                    ins = tr(PS[0:ROWS[ti], m % 4, P * c:P * (c + 1)], projT[:, c0 + c, P * ti:P * ti + ROWS[ti]], ident[:])
                ins.then_inc(tok_turned, 1)
            pe.wait_ge(ld_kc, 32)
            for hp in range(4):
                for t in range(2):
                    ins = tr(PS[:, 4 + hp // 2, PAST * (hp % 2) + P * t:PAST * (hp % 2) + P * (t + 1)],
                             kc[:, t, 2 * hp:2 * hp + 2, :].rearrange("p h d -> p (h d)"), ident[:])
            ins.then_inc(kc_turned, 1)
            pe.wait_ge(tok_copied, 2 * NT)
            pe.wait_ge(kc_copied, 1)
            pe.wait_ge(a_const, 2)

            def scores(u):
                if u >= 2:
                    pe.wait_ge(w_done, u - 1)
                if u < H:
                    o, c = DH * (u % 2), u // 2
                    for a in range(4):
                        ins = mm(flat(u)[:, OFF[a]:OFF[a] + LP - P * a], projT[o:o + DH, 8 + c, P * a:P * (a + 1)],
                                 projT[o:o + DH, 4 + c, P * a:LP], start=(a != 3), stop=True, skip_group_check=True)
                else:
                    for h in range(H):
                        o, c = DH * (h % 2), h // 2
                        qs = projT[o:o + DH, 4 + c, LP:T]
                        col = 512 * (h % 2) + LS * c
                        for t in range(2):
                            mm(flat(u)[:, col + NW * t:col + NW * t + LS], kcT[o:o + DH, c, P * t:P * (t + 1)], qs,
                               start=(h < 2 and t == 0), stop=True, skip_group_check=True)
                        ins = mm(flat(u)[0:LS, col + 2 * NW:col + 2 * NW + LS], projT[o:o + DH, 8 + c, LP:T], qs,
                                 start=False, stop=True, skip_group_check=True)
                ins.then_inc(z_done, 1)

            def later_keys(u):
                pe.wait_ge(soft_masked, u + 1)
                s = soft[u % 2]
                if u < H:
                    for a in range(4):
                        for b in range(a, 4):
                            n = LP - P * b
                            o = OFF[a] + P * (b - a)
                            ins = mm(flat(u)[:, o:o + n], (ntri if a == b else nones), s[:, OFF[b]:OFF[b] + n],
                                     start=False, stop=True, skip_group_check=True)
                else:
                    for b in (0, 512):
                        new = s[0:LS, b + 2 * NW:b + 3 * NW]
                        for t in range(2):
                            o = flat(u)[:, b + NW * t:b + NW * (t + 1)]
                            mm(o, ntri, s[:, b + NW * t:b + NW * (t + 1)], start=False, stop=True, skip_group_check=True)
                            mm(o, nones[0:LS, :], new, start=False, stop=True, skip_group_check=True)
                        mm(flat(u)[:, b:b + NW], nones, s[:, b + NW:b + 2 * NW], start=False, stop=True, skip_group_check=True)
                        ins = mm(flat(u)[0:LS, b + 2 * NW:b + 3 * NW], ntri[0:LS, 0:LS], new, start=False, stop=True, skip_group_check=True)
                ins.then_inc(cum_done, 1)

            def values(u):
                pe.wait_ge(w_masked, u + 1)
                if u >= 2:
                    pe.wait_ge(o_copied, u - 1)
                w = wts[u % 3]
                if u < H:
                    o = DH * (u % 2)
                    for a in range(4):
                        n = LP - P * a
                        ins = mm(PS[o:o + DH, 6 + u % 2, P * a:LP], v_tok[:, a, DH * u:DH * (u + 1)], w[:, OFF[a]:OFF[a] + n],
                                 start=(a == 0), stop=(a == 3), skip_group_check=True)
                else:
                    pe.wait_ge(ld_vc, 32)
                    for h in range(H):
                        o = PS[DH * (h % 2):DH * (h % 2) + DH, 6 + u % 2, LS * (h // 2):LS * (h // 2 + 1)]
                        col = 512 * (h % 2) + LS * (h // 2)
                        for t in range(2):
                            mm(o, vc[:, t, h, :], w[:, col + NW * t:col + NW * t + LS], start=(t == 0), stop=False)
                        ins = mm(o, v_tok[0:LS, NT - 1, DH * h:DH * (h + 1)], w[0:LS, col + 2 * NW:col + 2 * NW + LS],
                                 start=False, stop=True)
                ins.then_inc(pv_done, 1)

            scores(0)
            for u in range(units):
                if u + 1 < units:
                    scores(u + 1)
                later_keys(u)
                if u >= 1:
                    values(u - 1)
            values(units - 1)

        @block.scalar
        def _(act):
            for m in range(2 * NT):
                act.wait_ge(tok_turned, m + 1)
                r, dst = ROWS[m % NT], (k_tok, v_tok)[m // NT]
                nc.scalar.copy(dst[0:r, m % NT, :], PS[0:r, m % 4, :]).then_inc(tok_copied, 1)
            act.wait_ge(kc_turned, 1)
            nc.scalar.copy(kcT.rearrange("p (b h) t -> p b (h t)", b=2), PS[:, 4:6, :]).then_inc(kc_copied, 1)

            def weights(u):
                act.wait_ge(cum_done, u + 1)
                for p, o, n in spans(u):
                    ins = nc.scalar.activation(wts[u % 3][0:p, o:o + n], flat(u)[0:p, o:o + n], ACT.Exp)
                ins.then_inc(w_done, 1)

            for u in range(units):
                act.wait_ge(z_done, u + 1)
                if u >= 3:
                    act.wait_ge(pv_done, u - 2)
                for p, o, n in spans(u):
                    ins = nc.scalar.activation(wts[u % 3][0:p, o:o + n], flat(u)[0:p, o:o + n], ACT.Abs)
                ins.then_inc(abs_done, 1)
                act.wait_ge(abs_done, u + 1)
                for p, o, n in spans(u):
                    ins = nc.scalar.activation(wts[u % 3][0:p, o:o + n], wts[u % 3][0:p, o:o + n], ACT.Exp, scale=-1.0)
                ins.then_inc(exp_done, 1)
                act.wait_ge(exp_done, u + 1)
                for p, o, n in spans(u):
                    ins = nc.scalar.activation(wts[u % 3][0:p, o:o + n], wts[u % 3][0:p, o:o + n], ACT.Ln, bias=1.0)
                ins.then_inc(ln_done, 1)
                if u >= 1:
                    weights(u - 1)
            weights(units - 1)

        @block.vector
        def _(dve):
            vec = nc.vector

            def output(u):
                dve.wait_ge(pv_done, u + 1)
                if u < H:
                    o = DH * (u % 2)
                    vec.tensor_copy(projT[o:o + DH, 4 + u // 2, 0:LP], PS[o:o + DH, 6 + u % 2, :]).then_inc(o_copied, 1)
                else:
                    vec.tensor_copy(projT[:, 4:8, LP:T], PS[:, 6 + u % 2, 0:LS * 4].rearrange("p (c q) -> p c q", c=4)).then_inc(o_copied, 1)

            for u in range(units):
                dve.wait_ge(ln_done, u + 1)
                if u >= 2:
                    dve.wait_ge(cum_done, u - 1)
                for p, o, n in spans(u):
                    ins = vec.scalar_tensor_tensor(out=soft[u % 2][0:p, o:o + n], in0=flat(u)[0:p, o:o + n], scalar=0.0,
                                                   in1=wts[u % 3][0:p, o:o + n], op0=ALU.max, op1=ALU.add)
                ins.then_inc(soft_ready, 1)
                if u >= 2:
                    output(u - 2)
            output(units - 2)
            output(units - 1)


def normalise(vec, link, x, stats, mv, std, std_wait):
    for h in range(2):
        link(vec.bn_stats(stats[:, h, :], x[:, 512 * h:512 * (h + 1)]))
    vec.bn_aggr(mv, stats.rearrange("p a b -> p (a b)")).then_inc(std_wait[0], 1)
    std_wait[1]()
    link(vec.reciprocal(std, std))
    return vec.tensor_scalar(x, x, mv[:, 0:1], std, ALU.subtract, ALU.mult)


def moe_chunk(A, e, slot):
    if slot < 8:
        w, c = A["w_gate_up"][0], 512 * (slot // 4) + (FF if slot % 4 >= 2 else 0)
    else:
        w, c = A["w_down"][0], 512 * ((slot - 8) // 2)
    r = 512 * (slot % 2)
    return w[bass.ds(e, 1), r:r + 512, c:c + 512].rearrange("e (k p) c -> p (e k) c", p=P)


def stage_mix(nc, A, env):
    PS, ident, x_tok, one_p, mod, projT = (env[k] for k in ("PS", "ident", "x_tok", "one_p", "mod", "projT"))
    posblk, gates, gate_of, yrow, ovf, sel96, bias3 = (env[k] for k in ("posblk", "gates", "gate_of", "yrow", "ovf", "sel96", "bias3"))
    TB, CA, Dg, ring, ring_full = (env[k] for k in ("TB", "CA", "Dg", "ring", "ring_full"))
    sem, wait_dense, wide, mod_rows, h2_dram = env["sem"], env["wait_dense"], env["wide"], env["mod_rows"], env["h2_dram"]

    def room(t, *shape):
        flat = t[:].rearrange("p " + " ".join("abcd"[:len(t.shape) - 1]) + " -> p (" + " ".join("abcd"[:len(t.shape) - 1]) + ")")
        at = [0]

        def take(parts, *dims):
            n = math.prod(dims)
            v = flat[0:parts, at[0]:at[0] + n]
            at[0] += n
            assert at[0] <= flat.shape[1]
            names = "abcde"[:len(dims)]
            return v if len(dims) == 1 else v.rearrange(f"p ({' '.join(names)}) -> p {' '.join(names)}", **dict(zip(names, dims)))
        return take
    t_ca, t_tb, t_dg = room(CA), room(TB), room(Dg)
    mixT = t_ca(P, KT, T)
    h2 = [t_tb(P, D) for _ in range(2)]
    h2T = [t_tb(P, KT, P) for _ in range(2)]
    sc2, sh2 = t_dg(P, 2, D), t_dg(P, 2, D)
    ln1 = projT[:, 8:12, :].rearrange("p a b -> p (a b)")[:, 0:2 * D].rearrange("p (a b) -> p a b", a=2)
    braw = projT[:, 12:16, :].rearrange("p a b -> p (a b)")[0:3 * E, 0:2 * FF]
    st = ExitStack()
    with st:
        o = LENT - 2048
        spare = env["spare"]
        wr = spare(o, P, KT, E)
        br = spare(o + 256, P, E)
        small = spare(o + 288, P, NT, 16)
        lg = spare(o + 368, P, NT, E)
        top = spare(o + 528, P, NT, 8)
        topi = spare(o + 568, P, NT, 8).bitcast(U32)
        gi = spare(o + 608, P, 2, E).bitcast(I32)
        (m_rows, m_w, mix_done, mix_scaled, mix_turned, m_var, m_std, h2_ready, h2_sent, h2_turned, h2_copied, lg_done, lg_ready,
         m_dve, m_ld_bias, m_pool, h2_sent1, m_x) = (
            sem("mx_" + n) for n in ("rows", "w", "done", "scaled", "turned", "var", "std", "h2", "h2_sent", "h2_turned", "h2_copied",
                                     "lg", "lg_ready", "dve", "ld_bias", "pool", "h2_sent1", "x"))
        with nc.Block() as block:
            @block.sync
            def _(sp):
                for k in range(3):
                    sp.dma_start(braw[E * k:E * (k + 1), :], A["b_gate_up"][0]).then_inc(m_ld_bias, 16)
                for s in range(2):
                    sp.dma_start(sc2[:, s, :], mod_rows[s, 4 * D:5 * D].partition_broadcast(P)).then_inc(m_rows, 16)
                    sp.dma_start(sh2[:, s, :], mod_rows[s, 3 * D:4 * D].partition_broadcast(P)).then_inc(m_rows, 16)
                sp.dma_start(ln1[:, 0, :], A["ln1_g"][0].partition_broadcast(P)).then_inc(m_rows, 16)
                sp.dma_start(ln1[:, 1, :], A["ln1_b"][0].partition_broadcast(P)).then_inc(m_rows, 16)
                sp.dma_start(wr, A["w_router"][0].rearrange("(k p) e -> p k e", p=P)).then_inc(m_w, 16)
                sp.dma_start(br, A["b_router"][0].partition_broadcast(P)).then_inc(m_w, 16)
                for slot in range(PRE_RING):
                    sp.wait_ge(mix_done, 2 * (slot + 1))
                    sp.dma_start(ring[:, slot, :].rearrange("p (k c) -> p k c", k=4), moe_chunk(A, 0, slot)).then_inc(ring_full[slot], 16)
                for ti, r in enumerate(ROWS):
                    sp.wait_ge(h2_ready, ti + 1)
                    sp.dma_start(h2_dram[P * ti:P * ti + r, :], h2[ti % 2][0:r, :]).then_inc((h2_sent, h2_sent1)[ti % 2], 16)
                sp.wait_ge(h2_sent, 16 * ((NT + 1) // 2))
                sp.wait_ge(h2_sent1, 16 * (NT // 2))

            @block.gpsimd
            def _(pool):
                link = chained(pool, m_pool)
                pool.wait_ge(m_rows, 96)
                for ti, r in enumerate(ROWS):
                    pool.wait_ge(m_x, ti + 1)
                    if ti >= 2:
                        pool.wait_ge((h2_sent, h2_sent1)[ti % 2], 16 * (ti // 2))
                        pool.wait_ge(h2_turned, ti - 1)
                    s = ti // (NT - 1)
                    y = h2[ti % 2][0:r, :]
                    link(nc.gpsimd.tensor_tensor(y, x_tok[0:r, ti, :], sc2[0:r, s, :], ALU.mult))
                    nc.gpsimd.tensor_tensor(y, y, sh2[0:r, s, :], ALU.add).then_inc(h2_ready, 1)

            @block.tensor
            def _(pe):
                mm, tr = nc.tensor.matmul, nc.tensor.transpose
                for ct in range(KT):
                    n = N_ADA + N_IN + ct // 2
                    wait_dense(pe, n)
                    b = 2 * (ct % 4)
                    if ct >= 4:
                        pe.wait_ge(mix_scaled, ct - 3)
                    for k in range(KT):
                        for h in range(2):
                            ins = mm(PS[:, b + h, 0:HALF], wide(n)[:, k, P * (ct % 2):P * (ct % 2 + 1)],
                                     projT[:, k, HALF * h:HALF * (h + 1)], start=(k == 0), stop=(k == KT - 1))
                    ins.then_inc(mix_done, 1)
                pe.wait_ge(mix_scaled, KT)

                def turn_mix(ti):
                    r, b = ROWS[ti], 2 * (ti % 2)
                    if ti >= 2:
                        pe.wait_ge(m_var, ti - 1)
                    for k in range(KT):
                        ins = tr(PS[0:r, b + k // 4, P * (k % 4):P * (k % 4 + 1)], mixT[:, k, P * ti:P * ti + r], ident[:])
                    ins.then_inc(mix_turned, 1)

                def route(ti):
                    r, b = ROWS[ti], 4
                    pe.wait_ge(h2_ready, ti + 1)
                    if ti >= 1:
                        pe.wait_ge(h2_copied, ti)
                    for k in range(KT):
                        ins = tr(PS[:, b + k // 4, P * (k % 4):P * (k % 4) + r], h2[ti % 2][0:r, P * k:P * (k + 1)], ident[0:r, 0:r])
                    ins.then_inc(h2_turned, 1)
                    pe.wait_ge(h2_copied, ti + 1)
                    if ti == 0:
                        pe.wait_ge(m_w, 32)
                    if ti >= 2:
                        pe.wait_ge(lg_ready, ti - 1)
                    for k in range(KT):
                        ins = mm(PS[0:r, 6 + ti % 2, 0:E], h2T[ti % 2][:, k, 0:r], wr[:, k, :], start=(k == 0), stop=(k == KT - 1))
                    ins.then_inc(lg_done, 1)

                turn_mix(0)
                for ti in range(NT):
                    if ti + 1 < NT:
                        turn_mix(ti + 1)
                    route(ti)

            @block.scalar
            def _(act):
                for ct in range(KT):
                    act.wait_ge(mix_done, ct + 1)
                    b = 2 * (ct % 4)
                    gp, gs = (mod[:, s, 2 * KT + ct:2 * KT + ct + 1] for s in range(2))
                    nc.scalar.activation(mixT[:, ct, 0:HALF], PS[:, b, 0:HALF], ACT.Copy, scale=gp)
                    nc.scalar.activation(mixT[:, ct, HALF:LP], PS[:, b + 1, 0:LP - HALF], ACT.Copy, scale=gp)
                    nc.scalar.activation(mixT[:, ct, LP:T], PS[:, b + 1, LP - HALF:HALF], ACT.Copy, scale=gs).then_inc(mix_scaled, 1)

                def root(ti):
                    r = ROWS[ti]
                    act.wait_ge(m_var, ti + 1)
                    nc.scalar.activation(small[0:r, ti, 14:15], small[0:r, ti, 13:14], ACT.Sqrt, bias=one_p[0:r, 1:2]).then_inc(m_std, 1)

                root(0)
                for ti, r in enumerate(ROWS):
                    if ti + 1 < NT:
                        root(ti + 1)
                    act.wait_ge(h2_turned, ti + 1)
                    if ti >= 2:
                        act.wait_ge(lg_done, ti - 1)
                    for k in range(2):
                        ins = nc.scalar.copy(h2T[ti % 2][:, 4 * k:4 * k + 4, 0:r],
                                             PS[:, 4 + k, :].rearrange("p (a b) -> p a b", a=4)[:, :, 0:r])
                    ins.then_inc(h2_copied, 1)

            @block.vector
            def _(dve):
                link = chained(dve, m_dve)
                vec = nc.vector
                link(vec.memset(lg[:, NT - 1, :], 0.0))
                dve.wait_ge(m_ld_bias, 48)
                link(vec.tensor_copy(bias3[:], braw))
                for k in (1, 2):
                    for g in range(k, 3):
                        q = slice(E * g, E * (g + 1))
                        link(vec.tensor_tensor(braw[q, :], braw[q, :], bias3[q, :], ALU.subtract))
                        link(vec.tensor_copy(bias3[q, :], braw[q, :]))
                dve.wait_ge(m_rows, 96)

                def logits(ti):
                    dve.wait_ge(lg_done, ti + 1)
                    r = ROWS[ti]
                    vec.tensor_tensor(lg[0:r, ti, :], PS[0:r, 6 + ti % 2, 0:E], br[0:r, :], ALU.add).then_inc(lg_ready, 1)

                for ti, r in enumerate(ROWS):
                    x = x_tok[0:r, ti, :]
                    sq = small[0:r, ti]
                    dve.wait_ge(mix_turned, ti + 1)
                    link(vec.scalar_tensor_tensor(out=x, in0=x, scalar=DN_ALPHA, in1=PS[0:r, 2 * (ti % 2):2 * (ti % 2) + 2, :].rearrange("p a b -> p (a b)"),
                                                  op0=ALU.mult, op1=ALU.add))
                    link(normalise(vec, link, x, sq[:, 0:12].rearrange("p (a b) -> p a b", a=2), sq[:, 12:14], sq[:, 14:15],
                                   (m_var, lambda: dve.wait_ge(m_std, ti + 1))))
                    link(vec.tensor_tensor(x, x, ln1[0:r, 0, :], ALU.mult))
                    vec.tensor_tensor(x, x, ln1[0:r, 1, :], ALU.add).then_inc(m_x, 1)
                    if ti >= 2:
                        logits(ti - 2)
                logits(NT - 2)
                logits(NT - 1)
                dve.wait_ge(lg_ready, NT)
                for ti in range(NT):
                    link(vec.max(top[:, ti, :], lg[:, ti, :]))
                    link(vec.max_index(topi[:, ti, :], top[:, ti, :], lg[:, ti, :]))

        stage_plan(nc, env, top, topi, gi)


def stage_plan(nc, env, top, topi, gi):
    PS, ident = env["PS"], env["ident"]
    posblk, gates, gate_of, yrow, ovf, sel96 = (env[k] for k in ("posblk", "gates", "gate_of", "yrow", "ovf", "sel96"))
    sem = env["sem"]
    t_tb = env["TB"][:].rearrange("p a b -> p (a b)")
    t_dg = env["Dg"][:].rearrange("p a b -> p (a b)")
    t_ca = env["CA"][:].rearrange("p a b c -> p (a b c)")
    hot = t_tb[:, 0:NT * TOPK * E].rearrange("p (t k e) -> p t k e", t=NT, k=TOPK)
    hot2 = t_tb[:, 1024:1024 + NT * TOPK * E].rearrange("p (t k e) -> p t k e", t=NT, k=TOPK)
    big = t_ca[:, 0:NT * OVF * E].rearrange("p (t j e) -> p t j e", t=NT, j=OVF)
    f = [t_dg[:, NT * E * k:NT * E * (k + 1)].rearrange("p (t e) -> p t e", t=NT) for k in range(8)]
    mask, rank, rb, row, t0, t1 = f[0:6]
    before = t_dg[:, NT * E * 6:NT * E * 6 + (NT + 1) * E].rearrange("p (t e) -> p t e", t=NT + 1)
    o = 8 * NT * E
    ie, inc, exc, nov, cnt, ones32, c0, c1 = (t_dg[:, o + E * k:o + E * (k + 1)] for k in range(8))
    o += 8 * E
    em, em2, em3 = (t_dg[:, o + OVF * E * k:o + OVF * E * (k + 1)].rearrange("p (j e) -> p j e", j=OVF) for k in range(3))
    o += 3 * OVF * E
    ij, cj, ej = (t_dg[:, o + OVF * k:o + OVF * (k + 1)] for k in range(3))
    o += 3 * OVF
    rep3 = t_dg[:, o:o + 6 * E].rearrange("p (a k e) -> p a k e", a=2, k=3)
    o += 6 * E
    bnd = t_dg[:, o:o + 2]
    su, on = t_tb[:, 2048:2048 + P], t_tb[:, 2048 + P:2048 + 2 * P]
    topf, ex, tot = t_tb[:, 2560:2600].rearrange("p (t k) -> p t k", t=NT), t_tb[:, 2600:2640].rearrange("p (t k) -> p t k", t=NT), t_tb[:, 2640:2645]
    p_pool, p_cst, p_mask, p_rank, p_exp, p_ex, p_bnd, p_bnd2, p_dve, p_iota = (
        sem("pl_" + n) for n in ("pool", "cst", "mask", "rank", "exp", "ex", "bnd", "bnd2", "dve", "iota"))
    with nc.Block() as block:
        @block.gpsimd
        def _(pool):
            link = chained(pool, p_pool)
            pool.iota(gi[:, 0, :], pattern=[[1, E]], base=0, channel_multiplier=0).then_inc(p_iota, 1)
            link(pool.memset(su, 1.0))
            pool.affine_select(out=su, in_=su, compare_op=ALU.is_gt, fill=0.0, base=0,
                               pattern=[[1, P]], channel_multiplier=-1).then_inc(p_cst, 1)
            pool.memset(on, 1.0).then_inc(p_cst, 1)

        @block.scalar
        def _(act):
            act.wait_ge(p_exp, 1)
            nc.scalar.activation(ex[:, :, 0:TOPK], ex[:, :, 0:TOPK], ACT.Exp).then_inc(p_ex, 1)

        @block.tensor
        def _(pe):
            pe.wait_ge(p_cst, 2)
            pe.wait_ge(p_mask, 1)
            nc.tensor.matmul(PS[:, 0, 0:(NT + 1) * E], on, before.rearrange("p t e -> p (t e)"), start=True, stop=False,
                             skip_group_check=True)
            nc.tensor.matmul(PS[:, 0, 0:NT * E], su, mask.rearrange("p t e -> p (t e)"), start=False, stop=True,
                             skip_group_check=True).then_inc(p_rank, 1)
            pe.wait_ge(p_bnd, 1)
            for k in range(2):
                ins = nc.tensor.transpose(PS[0:3 * E, 1, P * k:P * (k + 1)], rep3[:, k].rearrange("p k e -> p (k e)"), ident[:])
            ins.then_inc(p_bnd2, 1)

        @block.vector
        def _(dve):
            link = chained(dve, p_dve)
            vec = nc.vector

            def tt(out, a, b, op):
                link(vec.tensor_tensor(out, a, b, op))

            def over_tokens(v):
                return v.unsqueeze(1).to_broadcast((P, NT, E))

            tt(ex[:, :, 0:TOPK], top[:, :, 0:TOPK], top[:, :, 0:1].to_broadcast((P, NT, TOPK)), ALU.subtract)
            dve.sem_inc(p_exp, 1)
            link(vec.tensor_copy(topf, topi[:]))
            dve.wait_ge(p_iota, 1)
            link(vec.tensor_copy(ie, gi[:, 0, :]))
            tt(hot, ie.unsqueeze(1).unsqueeze(1).to_broadcast((P, NT, TOPK, E)),
               topf[:, :, 0:TOPK].unsqueeze(3).to_broadcast((P, NT, TOPK, E)), ALU.is_equal)
            link(vec.memset(mask[:, NT - 1, :], 0.0))
            link(vec.tensor_reduce(mask[:, 0:NT - 1, :], hot[:, 0:NT - 1].rearrange("p t k e -> p t e k"), AX.X, ALU.add))
            link(vec.tensor_reduce(mask[0:LS, NT - 1, :], hot[0:LS, NT - 1].rearrange("p k e -> p e k"), AX.X, ALU.add))
            link(vec.memset(before[:, 0, :], 0.0))
            for ti in range(NT):
                tt(before[:, ti + 1, :], before[:, ti, :], mask[:, ti, :], ALU.add)
            dve.sem_inc(p_mask, 1)
            dve.wait_ge(p_ex, 1)
            link(vec.tensor_reduce(tot, ex[:, :, 0:TOPK], AX.X, ALU.add))
            link(vec.reciprocal(tot, tot))
            tt(gates[:], ex[:, :, 0:TOPK], tot.unsqueeze(2).to_broadcast((P, NT, TOPK)), ALU.mult)
            tt(hot2, hot, gates[:].unsqueeze(3).to_broadcast((P, NT, TOPK, E)), ALU.mult)
            link(vec.tensor_reduce(gate_of[:], hot2.rearrange("p t k e -> p t e k"), AX.X, ALU.add))
            dve.wait_ge(p_rank, 1)
            link(vec.tensor_copy(rank, PS[:, 0, 0:NT * E].rearrange("p (t e) -> p t e", t=NT)))
            link(vec.tensor_copy(cnt, PS[:, 0, NT * E:(NT + 1) * E]))
            link(vec.scalar_tensor_tensor(out=t0, in0=rank, scalar=1.0, in1=mask, op0=ALU.add, op1=ALU.mult))
            link(vec.tensor_scalar(posblk[:, :, 0:E], t0, -1.0, None, ALU.add))
            link(vec.tensor_scalar(rb, rank, float(P), None, ALU.is_ge))
            link(vec.tensor_scalar(nov, cnt, float(P), None, ALU.is_gt))
            for b in range(2, NT):
                link(vec.scalar_tensor_tensor(out=rb, in0=rank, scalar=float(P * b), in1=rb, op0=ALU.is_ge, op1=ALU.add))
                link(vec.scalar_tensor_tensor(out=nov, in0=cnt, scalar=float(P * b), in1=nov, op0=ALU.is_gt, op1=ALU.add))
            link(vec.memset(ones32, 1.0))
            link(vec.tensor_tensor_scan(inc, ones32, nov, 0.0, ALU.mult, ALU.add))
            tt(exc, inc, nov, ALU.subtract)
            link(vec.tensor_copy(rep3[:, 0], exc.unsqueeze(1).to_broadcast((P, 3, E))))
            vec.tensor_copy(rep3[:, 1], inc.unsqueeze(1).to_broadcast((P, 3, E))).then_inc(p_bnd, 1)
            tt(c0, exc, ie, ALU.subtract)
            link(vec.tensor_scalar(c0, c0, float(E - 1), None, ALU.add))
            tt(t0, rb, over_tokens(c0), ALU.add)
            link(vec.scalar_tensor_tensor(out=t0, in0=rb, scalar=0.0, in1=t0, op0=ALU.is_gt, op1=ALU.mult))
            tt(t0, t0, over_tokens(ie), ALU.add)
            tt(t0, t0, rb, ALU.subtract)
            link(vec.scalar_tensor_tensor(out=row, in0=t0, scalar=float(P), in1=rank, op0=ALU.mult, op1=ALU.add))
            tt(hot2, hot, row.unsqueeze(2).to_broadcast((P, NT, TOPK, E)), ALU.mult)
            link(vec.tensor_reduce(t1[:, :, 0:TOPK], hot2, AX.X, ALU.add))
            link(vec.tensor_copy(yrow[:], t1[:, :, 0:TOPK]))
            link(vec.tensor_copy(ij, ie[:, 0:OVF]))
            bj = ij.unsqueeze(2).to_broadcast((P, OVF, E))

            def over_j(v):
                return v.unsqueeze(1).to_broadcast((P, OVF, E))
            tt(em, over_j(exc), bj, ALU.is_le)
            tt(em2, over_j(inc), bj, ALU.is_gt)
            tt(em, em, em2, ALU.mult)
            tt(em2, em, over_j(ie), ALU.mult)
            link(vec.tensor_reduce(ej, em2, AX.X, ALU.add))
            link(vec.tensor_copy(ovf[:, 1:1 + OVF], ej))
            link(vec.tensor_copy(ovf[:, 0:1], inc[:, E - 1:E]))
            link(vec.tensor_scalar(em3, over_j(exc), float(P), 1.0 - P, ALU.mult, ALU.add))
            link(vec.scalar_tensor_tensor(out=em3, in0=bj, scalar=-float(P), in1=em3, op0=ALU.mult, op1=ALU.add))
            tt(em3, em, em3, ALU.mult)
            link(vec.tensor_reduce(cj, em3, AX.X, ALU.add))
            for ti in range(NT):
                tt(big[:, ti], em, posblk[:, ti, 0:E].unsqueeze(1).to_broadcast((P, OVF, E)), ALU.mult)
            link(vec.tensor_reduce(posblk[:, :, E:NB], big, AX.X, ALU.add))
            link(vec.scalar_tensor_tensor(out=posblk[:, :, E:NB], in0=posblk[:, :, E:NB], scalar=-1.0,
                                          in1=cj.unsqueeze(1).to_broadcast((P, NT, OVF)), op0=ALU.add, op1=ALU.add))
            for k in range(3):
                link(vec.tensor_copy(sel96[E * k:E * (k + 1), 0:E], ident[E * k:E * (k + 1), E * k:E * (k + 1)]))
            dve.wait_ge(p_bnd2, 1)
            link(vec.tensor_copy(bnd[0:3 * E], PS[0:3 * E, 1, 0:P + 1:P]))
            sj = sel96[:, E:NB]
            link(vec.tensor_scalar(sj, ij[0:3 * E], bnd[0:3 * E, 0:1], None, ALU.is_ge))
            link(vec.scalar_tensor_tensor(out=sj, in0=ij[0:3 * E], scalar=bnd[0:3 * E, 1:2], in1=sj, op0=ALU.is_lt, op1=ALU.mult))


def stage_moe(nc, A, env):
    PS, ident, ring, ring_full = (env[k] for k in ("PS", "ident", "ring", "ring_full"))
    posblk, ovf, sel96, bias3 = (env[k] for k in ("posblk", "ovf", "sel96", "bias3"))
    h2_dram, y_dram, sem = env["h2_dram"], env["y_dram"], env["sem"]
    st = ExitStack()
    with st:
        def sb(name, shape, dt=F32):
            return st.enter_context(nc.sbuf_tensor(name, shape, dt))
        slots = sb("slots", [P, P])
        tok2 = sb("tok2", [P, NT, 2], BF16)
        it = sb("moe_iota", [P, P + NT * 2], I32)
        pick = sb("pick", [P, 2, NT, P], BF16)
        hotb = sb("hotb", [3 * E, 2, P], BF16)
        rowi = sb("rowi", [P, 2], U32)
        X = sb("X", [P, 2, D])
        XTh, XTl = (sb(n, [P, 2, KT, P], F32R) for n in ("XTh", "XTl"))
        hi, lo = (sb(n, [P, 4, 2048], F32R) for n in ("w_hi", "w_lo"))
        more = sb("more_ring", [P, RING - PRE_RING, 2048])
        g_, u_, s_ = (sb(n, [P, 512]) for n in ("g_", "u_", "s_"))
        h_ = sb("h_", [P, 2, 512])
        hTh, hTl = (sb(n, [P, KT, P], F32R) for n in ("hTh", "hTl"))
        y_ = sb("y_", [P, D])
        (iota_ok, cst_ok, hot_ok, pick_ok, num_ok, idx_ok, x_full0, x_full1, xt_done, xt_ok, g_ok, u_ok, s_ok, m_ok, hA, hB,
         hAt, hBt, hAc, hBc, y_ok, y_sent0, y_sent1, used_a, used_b, used_d) = (
            sem("e_" + n) for n in ("iota", "cst", "hot", "pick", "num", "idx", "x_full0", "x_full1", "xt", "xt_ok", "g", "u", "s", "m",
                                    "hA", "hB", "hAt", "hBt", "hAc", "hBc", "y", "y_sent0", "y_sent1", "used_a", "used_b", "used_d"))
        x_full, y_sent = (x_full0, x_full1), (y_sent0, y_sent1)
        cast = {g: sem("e_cast_" + g) for g in "abd"}
        low = {g: sem("e_low_" + g) for g in "abd"}
        low4 = {g: sem("e_low4_" + g) for g in "abd"}
        used = dict(a=used_a, b=used_b, d=used_d)
        xl_ok, hAl, hBl = sem("e_xl"), sem("e_hAl"), sem("e_hBl")

        def blocks(eng, first, last, head, body):
            head(first)
            if first == 0:
                body(0, 0, 2)
                body(1, 1, 2)
                first = 2
            with eng.Fori(0, (last - first) // 2) as n:
                for q in range(2):
                    body(n * 2 + (first + q), q, 2)
            body(last - 1, 0, 1)
            body(last, 1, 0)

        def all_blocks(eng, head, body):
            blocks(eng, 0, E - 1, head, body)
            n = eng.value_load(ovf[0:1, 0:1], min_val=0, max_val=OVF)
            with eng.If(n > 0):
                blocks(eng, E, NB - 1, head, body)

        def at_least(eng, sem, value):
            if not isinstance(value, int) or value > 0:
                eng.wait_ge(sem, value)

        RING_SLOT = dict(a=(0, 1, 2, 3), b=(2, 3, 4, 5), d=(4, 5, 0, 1))

        def raw(g, j):
            r = RING_SLOT[g][j]
            return ring[:, r, :] if r < PRE_RING else more[:, r - PRE_RING, :]

        def tiles(v):
            return v.rearrange("p (k c) -> p k c", k=4)

        def filled(g, i, j, end):
            r = RING_SLOT[g][j]
            if r in (0, 1):
                nth = (1 if end else 0) if g == "a" else (2 if end else 3)
            else:
                nth = 1 if (g, r) in (("a", 2), ("a", 3), ("b", 4), ("b", 5)) else 2
            return i * 32 + 16 * (nth + (PRE // PRE_RING if r < PRE_RING else 0))

        def take_low(eng, vec, g, i, j, done):
            eng.wait_ge(cast[g], i * 4 + (j + 1))
            vec.tensor_tensor(lo[:, j, :], raw(g, j), hi[:, j, :].bitcast(F32), ALU.subtract).then_inc(done, 1)

        with nc.Block() as block:
            @block.sync
            def _(sp):
                def load(e, g, j, *before):
                    if before:
                        gb, ib, jb = before
                        if jb < 3:
                            sp.wait_ge(low[gb], ib * 3 + (jb + 1))
                        else:
                            sp.wait_ge(low4[gb], ib + 1)
                    r = RING_SLOT[g][j]
                    sp.dma_start(tiles(raw(g, j)), moe_chunk(A, e, "abd".index(g) * 4 + j)).then_inc(ring_full[r], 16)

                def second_halves(e, i, start=False):
                    load(e, "b", 0, "a", i, 2)
                    load(e, "b", 1, "a", i, 3)
                    for j in (2, 3):
                        load(e, "b", j, *(() if start else ("d", i - 1, j - 2)))

                def next_first_halves(e, i, first=False):
                    for j in (0, 1):
                        load(e, "a", j, *(("a", i, j) if first else ("d", i - 1, j + 2)))
                    for j in (2, 3):
                        load(e, "a", j, "b", i, j - 2)

                def downs(e, i, last=False):
                    for j in (0, 1):
                        load(e, "d", j, "b", i, j + 2)
                    for j in (2, 3):
                        load(e, "d", j, *(("d", i - 1, j) if last else ("a", i + 1, j - 2)))

                second_halves(0, 0, start=True)
                next_first_halves(1, 0, first=True)
                downs(0, 0)
                with sp.Fori(1, E - 1) as i:
                    second_halves(i, i)
                    next_first_halves(i + 1, i)
                    downs(i, i)
                second_halves(E - 1, E - 1)
                downs(E - 1, E - 1, last=True)
                n = sp.value_load(ovf[0:1, 0:1], min_val=0, max_val=OVF)
                with sp.If(n > 0):
                    def expert(j):
                        return sp.value_load(ovf[0:1, bass.ds(j + 1, 1)], min_val=0, max_val=E - 1)

                    e, f = expert(0), expert(1)
                    for j in (0, 1):
                        load(e, "a", j, "d", E - 1, j + 2)
                    for j in (2, 3):
                        load(e, "a", j, "b", E - 1, j - 2)
                    second_halves(e, E)
                    next_first_halves(f, E, first=True)
                    downs(e, E)
                    with sp.Fori(1, OVF - 1) as j:
                        e, f = expert(j), expert(j + 1)
                        second_halves(e, j + E)
                        next_first_halves(f, j + E)
                        downs(e, j + E)
                    e = expert(OVF - 1)
                    second_halves(e, NB - 1)
                    downs(e, NB - 1, last=True)

            @block.gpsimd
            def _(pool):
                pool.iota(it[:, 0:P], pattern=[[1, P]], base=0, channel_multiplier=0).then_inc(iota_ok, 1)
                v = it[:, P:P + 2 * NT].rearrange("p (t a) -> p t a", a=2)
                pool.iota(v[:, :, 0:1], pattern=[[P, NT], [1, 1]], base=0, channel_multiplier=0).then_inc(iota_ok, 1)
                pool.iota(v[:, :, 1:2], pattern=[[0, NT], [1, 1]], base=0, channel_multiplier=1).then_inc(iota_ok, 1)

                def gather(i, q, reused):
                    pool.wait_ge(idx_ok, i + 1)
                    if reused:
                        pool.wait_ge(xt_done, i * 2 - 2)
                    pool.nop(nofuse=True)
                    pool.indirect_dma_start(out=X[:, q, :], out_offset=None, in_=h2_dram,
                                            in_offset=bass.IndirectOffsetOnAxis(ap=rowi[:, q:q + 1], axis=0)).then_inc(x_full[q], 16)

                def lows(g, i):
                    take_low(pool, nc.gpsimd, g, i, 3, low4[g])

                def head(first):
                    gather(first, 0, first > 0)
                    gather(first + 1, 1, first > 0)
                    lows("a", first)
                    lows("b", first)

                def body(i, q, later):
                    if later:
                        lows("a", i + 1)
                    if later == 2:
                        gather(i + 2, q, True)
                    lows("d", i)
                    if later:
                        lows("b", i + 1)
                all_blocks(pool, head, body)

            @block.tensor
            def _(pe):
                mm, tr = nc.tensor.matmul, nc.tensor.transpose

                def number(i, q):
                    pe.wait_ge(pick_ok, i + 1)
                    for ti in range(NT):
                        ins = mm(PS[:, 6, 0:2], pick[:, q, ti, :], tok2[:, ti, :], start=(ti == 0), stop=(ti == NT - 1))
                    ins.then_inc(num_ok, 1)

                def turn_x(i, q):
                    pe.wait_ge(x_full[q], (i - q) * 8 + 16)
                    pe.wait_ge(idx_ok, i + 1)
                    at_least(pe, hBl, i - 1)
                    for k in range(KT):
                        ins = tr(PS[:, 6 + k // 4, P * (k % 4):P * (k % 4 + 1)], X[:, q, P * k:P * (k + 1)], ident[:])
                        if k % 4 == 3:
                            ins.then_inc(xt_done, 1)

                def turn_h(i, half, ready, done):
                    pe.wait_ge(ready, i + 1)
                    for k in range(4):
                        ins = tr(PS[:, 6 + half, P * k:P * (k + 1)], h_[:, half, P * k:P * (k + 1)], ident[:])
                    ins.then_inc(done, 1)

                def products(o, h, l, g, i, p, start):
                    for k in range(KT):
                        j = 2 * p + k // 4
                        if k % 4 == 0:
                            if j < 3:
                                pe.wait_ge(low[g], i * 3 + (j + 1))
                            else:
                                pe.wait_ge(low4[g], i + 1)
                        wh, wl = tiles(hi[:, j, :])[:, k % 4, :], tiles(lo[:, j, :])[:, k % 4, :]
                        mm(o, h[:, k, :], wh, start=(start and k == 0), stop=False)
                        mm(o, l[:, k, :], wh, start=False, stop=False)
                        ins = mm(o, h[:, k, :], wl, start=False, stop=(k == KT - 1))
                        if k % 4 == 3:
                            ins.then_inc(used[g], 1)

                def up(i, q, half, p):
                    o = PS[:, 2 * half + p, :]
                    mm(o, hotb[:, q, :], bias3[:, FF * p + 512 * half:FF * p + 512 * half + 512], start=True, stop=False)
                    products(o, XTh[:, q], XTl[:, q], "ab"[half], i, p, False)

                def first_half(i, q, between):
                    pe.wait_ge(xl_ok, i * 2 + 2)
                    pe.wait_ge(hot_ok, i + 1)
                    at_least(pe, hA, i)
                    up(i, q, 0, 0)
                    between()
                    up(i, q, 0, 1)

                def down(i, between):
                    pe.wait_ge(hAl, i + 1)
                    pe.wait_ge(hBl, i + 1)
                    at_least(pe, y_ok, i * 2)
                    for half in range(2):
                        products(PS[:, 4 + half, :], hTh, hTl, "d", i, half, True)
                        if half == 0:
                            between()

                def head(first):
                    number(first, 0)
                    pe.wait_ge(idx_ok, first + 1)
                    number(first + 1, 1)
                    pe.wait_ge(idx_ok, first + 2)
                    turn_x(first, 0)
                    first_half(first, 0, lambda: None)
                    turn_x(first + 1, 1)

                def body(i, q, later):
                    if later:
                        pe.wait_ge(xl_ok, i * 2 + 3)
                    turn_h(i, 0, hA, hAt)
                    at_least(pe, hB, i)
                    up(i, q, 1, 0)
                    up(i, q, 1, 1)
                    if later == 2:
                        pe.wait_ge(hAl, i + 1)
                        number(i + 2, q)

                    def second_h():
                        if later:
                            pe.wait_ge(xl_ok, i * 2 + 4)
                        turn_h(i, 1, hB, hBt)
                    if later:
                        first_half(i + 1, 1 - q, second_h)
                    else:
                        second_h()
                    down(i, lambda: turn_x(i + 2, q) if later == 2 else None)

                pe.wait_ge(cst_ok, 2)
                all_blocks(pe, head, body)

            @block.scalar
            def _(act):
                def xt(i, q):
                    for k in range(2):
                        act.wait_ge(xt_done, i * 2 + (k + 1))
                        nc.scalar.copy(XTh[:, q, 4 * k:4 * k + 4, :], PS[:, 6 + k, :].rearrange("p (a b) -> p a b", a=4)).then_inc(xt_ok, 1)

                def ht(i, half, turned, done):
                    act.wait_ge(turned, i + 1)
                    at_least(act, used_d, i * 4)
                    nc.scalar.copy(hTh[:, 4 * half:4 * half + 4, :], PS[:, 6 + half, :].rearrange("p (a b) -> p a b", a=4)).then_inc(done, 1)

                def high(g, i, j, freed, value, end=False):
                    at_least(act, freed, value)
                    act.wait_ge(ring_full[RING_SLOT[g][j]], filled(g, i, j, end))
                    nc.scalar.copy(hi[:, j, :], raw(g, j)).then_inc(cast[g], 1)

                def sigmoid(n):
                    act.wait_ge(g_ok, n + 1)
                    nc.scalar.activation(s_[:], g_[:], ACT.Sigmoid, scale=SW_ALPHA).then_inc(s_ok, 1)

                def y(i, q, half):
                    if half == 0:
                        at_least(act, y_sent[1 - q], (i + q) * 8)
                    act.wait_ge(used_d, i * 4 + 2 * (half + 1))
                    nc.scalar.copy(y_[:, 512 * half:512 * (half + 1)], PS[:, 4 + half, :]).then_inc(y_ok, 1)
                    if half == 1:
                        act.wait_ge(y_ok, i * 2 + 2)
                        act.dma_start(y_dram[bass.ts(i, P), :], y_[:]).then_inc(y_sent[q], 16)

                def head(first):
                    for j in range(4):
                        high("a", first, j, used_d, 4 * first + j - 3 if first else 0, end=True)
                    xt(first, 0)
                    for j in range(4):
                        high("b", first, j, used_a, 4 * first + j + 1)
                        if j == 1:
                            sigmoid(2 * first)
                    xt(first + 1, 1)

                def body(i, q, later):
                    ht(i, 0, hAt, hAc)
                    for j in range(4):
                        if later:
                            high("a", i + 1, j, used_b, i * 4 + (j + 1))
                        else:
                            high("d", i, j, used_b, i * 4 + (j + 1), end=True)
                        if j == 2:
                            sigmoid(i * 2 + 1)
                    if later:
                        for j in range(2):
                            high("d", i, j, used_a, i * 4 + (j + 5))
                    ht(i, 1, hBt, hBc)
                    if later:
                        high("d", i, 2, used_a, i * 4 + 7)
                        sigmoid(i * 2 + 2)
                        high("d", i, 3, used_a, i * 4 + 8)
                    for half in range(2):
                        if later:
                            for j in (2 * half, 2 * half + 1):
                                high("b", i + 1, j, used_d, i * 4 + (j + 1))
                        y(i, q, half)
                        if half == 0 and later == 2:
                            xt(i + 2, q)
                    if later == 0:
                        for s in y_sent:
                            act.wait_ge(s, 8 * (i + 1))
                all_blocks(act, head, body)

            @block.vector
            def _(dve):
                vec = nc.vector

                def hot(i, q):
                    vec.tensor_copy(hotb[:, q, :], sel96[:, bass.ds(i, 1)].to_broadcast((3 * E, P))).then_inc(hot_ok, 1)

                def choose(i, q):
                    for ti in range(NT):
                        ins = vec.tensor_scalar(pick[:, q, ti, :], slots[:], posblk[:, ti, bass.ds(i, 1)], None, ALU.is_equal)
                    ins.then_inc(pick_ok, 1)

                def index(i, q):
                    dve.wait_ge(num_ok, i + 1)
                    with nc.allow_low_precision(reason="a sum of two whole numbers below 2^24, exact as an integer"):
                        vec.tensor_reduce(rowi[:, q:q + 1], PS[:, 6, 0:2], AX.X, ALU.add).then_inc(idx_ok, 1)

                def x_low(i, q):
                    for k in range(2):
                        dve.wait_ge(xt_ok, i * 2 + (k + 1))
                        vec.tensor_tensor(XTl[:, q, 4 * k:4 * k + 4, :], PS[:, 6 + k, :].rearrange("p (a b) -> p a b", a=4),
                                          XTh[:, q, 4 * k:4 * k + 4, :].bitcast(F32), ALU.subtract).then_inc(xl_ok, 1)

                def h_low(i, half, ready, done):
                    dve.wait_ge(ready, i + 1)
                    vec.tensor_tensor(hTl[:, 4 * half:4 * half + 4, :], PS[:, 6 + half, :].rearrange("p (a b) -> p a b", a=4),
                                      hTh[:, 4 * half:4 * half + 4, :].bitcast(F32), ALU.subtract).then_inc(done, 1)

                def lows(g, i, js):
                    for j in js:
                        take_low(dve, vec, g, i, j, low[g])

                def gate(half, i):
                    dve.wait_ge(used["ab"[half]], i * 4 + 2)
                    vec.tensor_scalar(g_[:], PS[:, 2 * half, :], LIMIT, None, ALU.min).then_inc(g_ok, 1)

                def act_out(half, i):
                    n = i * 2 + half
                    dve.wait_ge(used["ab"[half]], i * 4 + 4)
                    vec.tensor_scalar(u_[:], PS[:, 2 * half + 1, :], -LIMIT, LIMIT, ALU.max, ALU.min).then_inc(u_ok, 1)
                    dve.wait_ge(u_ok, n + 1)
                    vec.scalar_tensor_tensor(out=u_[:], in0=u_[:], scalar=1.0, in1=g_[:], op0=ALU.add, op1=ALU.mult).then_inc(m_ok, 1)
                    dve.wait_ge(m_ok, n + 1)
                    dve.wait_ge(s_ok, n + 1)
                    at_least(dve, (hAt, hBt)[half], i)
                    vec.tensor_tensor(h_[:, half, :], u_[:], s_[:], ALU.mult).then_inc((hA, hB)[half], 1)

                def head(first):
                    if first:
                        dve.wait_ge(used_b, 4 * first)
                        dve.wait_ge(x_full[1], 8 * first)
                        dve.wait_ge(x_full[0], 8 * first)
                    hot(first, 0)
                    choose(first, 0)
                    choose(first + 1, 1)
                    index(first, 0)
                    index(first + 1, 1)
                    lows("a", first, (0, 1, 2))
                    x_low(first, 0)
                    lows("b", first, (0,))
                    gate(0, first)
                    lows("b", first, (1, 2))
                    act_out(0, first)
                    x_low(first + 1, 1)

                def body(i, q, later):
                    h_low(i, 0, hAc, hAl)
                    g, ig = ("a", i + 1) if later else ("d", i)
                    if later:
                        at_least(dve, used_b, i * 4)
                        hot(i + 1, 1 - q)
                    if later == 2:
                        choose(i + 2, q)
                    lows(g, ig, (0, 1))
                    gate(1, i)
                    lows(g, ig, (2,))
                    act_out(1, i)
                    if later == 2:
                        dve.wait_ge(x_full[q], (i - q) * 8 + 16)
                        index(i + 2, q)
                    if later:
                        lows("d", i, (0, 1))
                    h_low(i, 1, hBc, hBl)
                    if later:
                        gate(0, i + 1)
                        lows("d", i, (2,))
                        act_out(0, i + 1)
                        lows("b", i + 1, (0, 1))
                        if later == 2:
                            x_low(i + 2, q)
                        lows("b", i + 1, (2,))

                dve.wait_ge(iota_ok, 3)
                vec.tensor_copy(slots[:], it[:, 0:P]).then_inc(cst_ok, 1)
                vec.tensor_copy(tok2[:].rearrange("p t a -> p (t a)"), it[:, P:P + 2 * NT]).then_inc(cst_ok, 1)
                dve.wait_ge(cst_ok, 2)
                all_blocks(dve, head, body)


def stage_output(nc, A, O, env):
    PS, ident, x_tok, one_p = (env[k] for k in ("PS", "ident", "x_tok", "one_p"))
    gates, gate_of, yrow, y_dram, mod_rows, sem = (env[k] for k in ("gates", "gate_of", "yrow", "y_dram", "mod_rows", "sem"))
    st = ExitStack()
    with st:
        def sb(name, shape, dt=F32):
            return st.enter_context(nc.sbuf_tensor(name, shape, dt))
        bd = sb("bd", [E, D])
        gT = sb("gT_", [E, NT, P])
        diag = sb("diag", [P, 2, TOPK, P])
        Y = sb("Y", [P, 2, TOPK, D])
        ln2 = sb("ln2", [P, 2, D])
        g2 = sb("g2", [P, 2, D])
        gated = sb("gated", [P, D])
        small = sb("out_small", [P, NT, 16])
        (o_rows, o_bd, o_y0, o_y1, o_gt, o_gtc, o_diag, o_sum, o_gated, o_var, o_std, o_x, o_sent, o_dve, o_normal, o_pool) = (
            sem("o_" + n) for n in ("rows", "bd", "y0", "y1", "gt", "gtc", "diag", "sum", "gated", "var", "std", "x", "sent", "dve", "normal", "pool"))
        o_y = (o_y0, o_y1)
        with nc.Block() as block:
            @block.gpsimd
            def _(pool):
                link = chained(pool, o_pool)

                def gather(ti):
                    r = ROWS[ti]
                    if ti >= 2:
                        pool.wait_ge(o_sum, ti - 1)
                    for k in range(TOPK):
                        pool.indirect_dma_start(out=Y[0:r, ti % 2, k, :], out_offset=None, in_=y_dram,
                                                in_offset=bass.IndirectOffsetOnAxis(ap=yrow[0:r, ti, k:k + 1], axis=0)).then_inc(o_y[ti % 2], 16)

                gather(0)
                gather(1)
                pool.wait_ge(o_rows, 64)
                for ti, r in enumerate(ROWS):
                    if ti + 2 < NT:
                        gather(ti + 2)
                    pool.wait_ge(o_normal, ti + 1)
                    x = x_tok[0:r, ti, :]
                    link(nc.gpsimd.tensor_tensor(x, x, ln2[0:r, 0, :], ALU.mult))
                    nc.gpsimd.tensor_tensor(x, x, ln2[0:r, 1, :], ALU.add).then_inc(o_x, 1)

            @block.sync
            def _(sp):
                sp.dma_start(bd[:], A["b_down"][0]).then_inc(o_bd, 16)
                sp.dma_start(ln2[:, 0, :], A["ln2_g"][0].partition_broadcast(P)).then_inc(o_rows, 16)
                sp.dma_start(ln2[:, 1, :], A["ln2_b"][0].partition_broadcast(P)).then_inc(o_rows, 16)
                for s in range(2):
                    sp.dma_start(g2[:, s, :], mod_rows[s, 5 * D:6 * D].partition_broadcast(P)).then_inc(o_rows, 16)
                for ti, r in enumerate(ROWS):
                    sp.wait_ge(o_x, ti + 1)
                    dst = O["y_p"][0][P * ti:P * (ti + 1)] if ti < NT - 1 else O["y_s"][0]
                    sp.dma_start(dst, x_tok[0:r, ti, :]).then_inc(o_sent, 16)
                sp.wait_ge(o_sent, 16 * NT)

            @block.tensor
            def _(pe):
                mm = nc.tensor.matmul
                for ti, r in enumerate(ROWS):
                    ins = nc.tensor.transpose(PS[0:E, 4 + ti // 4, P * (ti % 4):P * (ti % 4) + r], gate_of[0:r, ti, :], ident[0:r, 0:r])
                ins.then_inc(o_gt, 1)
                pe.wait_ge(o_gtc, 2)
                pe.wait_ge(o_bd, 16)
                for ti, r in enumerate(ROWS):
                    b = 2 * (ti % 2)
                    if ti >= 2:
                        pe.wait_ge(o_gated, ti - 1)
                    for h in range(2):
                        mm(PS[0:r, b + h, :], gT[:, ti, 0:r], bd[:, 512 * h:512 * (h + 1)], start=True, stop=False)
                    pe.wait_ge(o_diag, ti + 1)
                    pe.wait_ge(o_y[ti % 2], 64 * (ti // 2 + 1))
                    for k in range(TOPK):
                        for h in range(2):
                            ins = mm(PS[0:r, b + h, :], diag[0:r, ti % 2, k, 0:r], Y[0:r, ti % 2, k, 512 * h:512 * (h + 1)],
                                     start=False, stop=(k == TOPK - 1))
                    ins.then_inc(o_sum, 1)

            @block.scalar
            def _(act):
                for ti, r in enumerate(ROWS):
                    act.wait_ge(o_var, ti + 1)
                    nc.scalar.activation(small[0:r, ti, 14:15], small[0:r, ti, 13:14], ACT.Sqrt, bias=one_p[0:r, 1:2]).then_inc(o_std, 1)

            @block.vector
            def _(dve):
                link = chained(dve, o_dve)
                vec = nc.vector
                dve.wait_ge(o_gt, 1)
                vec.tensor_copy(gT[:, 0:NT - 1, :], PS[0:E, 4, :].rearrange("e (t p) -> e t p", t=NT - 1)).then_inc(o_gtc, 1)
                vec.tensor_copy(gT[:, NT - 1, 0:LS], PS[0:E, 5, 0:LS]).then_inc(o_gtc, 1)

                def diagonals(ti):
                    r = ROWS[ti]
                    if ti >= 2:
                        dve.wait_ge(o_sum, ti - 1)
                    for k in range(TOPK):
                        ins = vec.tensor_scalar(diag[0:r, ti % 2, k, 0:r], ident[0:r, 0:r], gates[0:r, ti, k:k + 1], None, ALU.mult)
                    ins.then_inc(o_diag, 1)
                diagonals(0)
                dve.wait_ge(o_rows, 64)
                for ti, r in enumerate(ROWS):
                    if ti + 1 < NT:
                        diagonals(ti + 1)
                    s, b = ti // (NT - 1), 2 * (ti % 2)
                    x, sq = x_tok[0:r, ti, :], small[0:r, ti]
                    dve.wait_ge(o_sum, ti + 1)
                    t = gated[0:r, :]
                    vec.tensor_tensor(t, PS[0:r, b:b + 2, :].rearrange("p a b -> p (a b)"), g2[0:r, s, :], ALU.mult).then_inc(o_gated, 1)
                    dve.wait_ge(o_gated, ti + 1)
                    link(vec.scalar_tensor_tensor(out=x, in0=x, scalar=DN_ALPHA, in1=t, op0=ALU.mult, op1=ALU.add))
                    normalise(vec, link, x, sq[:, 0:12].rearrange("p (a b) -> p a b", a=2), sq[:, 12:14], sq[:, 14:15],
                              (o_var, lambda: dve.wait_ge(o_std, ti + 1))).then_inc(o_normal, 1)


_INS = ['x_prompt', 'x_sample', 'cache_k', 'cache_v', 'state_s5_re', 'state_s5_im', 'c_prompt', 'c_sample',
        'ln_in_g', 'ln_in_b', 'w_ada', 'b_ada', 'w_in', 's5_a_re', 's5_a_im', 's5_log_dt', 's5_b_re', 's5_b_im',
        's5_c_re', 's5_c_im', 's5_d', 's5_w_glu', 's5_b_glu', 'w_out', 'ln1_g', 'ln1_b', 'w_router', 'b_router',
        'w_gate_up', 'b_gate_up', 'w_down', 'b_down', 'ln2_g', 'ln2_b']
_OUTS = [('y_p', (1, LP, D)), ('y_s', (1, LS, D)), ('k_p', (1, 1, H, LP, DH)), ('v_p', (1, 1, H, LP, DH)),
         ('s5_re_p', (1, 1, G, NS)), ('s5_im_p', (1, 1, G, NS)), ('k_s', (1, 1, H, LS, DH)), ('v_s', (1, 1, H, LS, DH)),
         ('s5_re_s', (1, 1, G, NS)), ('s5_im_s', (1, 1, G, NS))]


def kernel(**inputs):
    import numpy as _np
    import concourse.bacc as _bacc
    from concourse import mybir as _mybir
    from concourse.bass_utils import run_bass_kernel_spmd as _run

    nc = _bacc.Bacc("TRN2", target_bir_lowering=False, num_devices=1)
    arrays, ins, outs = {}, {}, {}
    for name in _INS:
        a = _np.ascontiguousarray(inputs[name])
        arrays[f"in_{name}_dram"] = a
        ins[name] = nc.dram_tensor(f"in_{name}_dram", a.shape, _mybir.dt.from_np(a.dtype), kind="ExternalInput").ap()
    for name, shape in _OUTS:
        outs[name] = nc.dram_tensor(f"out_{name}_dram", shape, F32, kind="ExternalOutput").ap()
    build(nc, ins, outs)
    r = _run(nc, [arrays], core_ids=[0])
    return tuple(r.results[0][f"out_{name}_dram"] for name, _ in _OUTS)
```
